# Optimizing a Trainium2 kernel written in Bass

```python
import jax
import jax.numpy as jnp
from jax import lax
import numpy as np
import jax, jax.numpy as jnp

D_MODEL = 1024
BATCH = 1
SEQ = 512
DEPTH = 2

GRID_W = 64
CTX_LEN = 256
N_MIXERS = 2
N_CONV_LAYERS = (DEPTH + 1) // 2
N_ATTN_LAYERS = DEPTH // 2
CONV_WIDTH = 31
HEAD_DIM = 64
N_HEADS = D_MODEL // HEAD_DIM
N_KV_HEADS = N_HEADS // 4
GQA_GROUP = N_HEADS // N_KV_HEADS
QKV_DIM = (N_HEADS + 2 * N_KV_HEADS) * HEAD_DIM
WINDOW = 128
BLOCK = 128
ROPE_BASE = 10000.0
D_FF = 2816
FFN_CONV_WIDTH = 3
EPS = 1e-6
NEG = -1e30


def rmsnorm(x, g):
    xf = x.astype(jnp.float32)
    y = xf * lax.rsqrt(jnp.mean(xf * xf, axis=-1, keepdims=True) + EPS)
    return (y * g.astype(jnp.float32)).astype(x.dtype)

def layernorm(x, g, b):
    xf = x.astype(jnp.float32)
    mu = jnp.mean(xf, axis=-1, keepdims=True)
    var = jnp.mean(jnp.square(xf - mu), axis=-1, keepdims=True)
    y = (xf - mu) * lax.rsqrt(var + EPS)
    return (y * g.astype(jnp.float32) + b.astype(jnp.float32)).astype(x.dtype)

def modulate(x, shift, scale):
    return x * (1.0 + scale) + shift

def dwconv(x, w, b):
    k = w.shape[0]
    pad = (k - 1) // 2
    y = lax.conv_general_dilated(x, w[:, None, :], window_strides=(1,), padding=[(pad, pad)],
                                 dimension_numbers=('NWC', 'WIO', 'NWC'),
                                 feature_group_count=x.shape[-1])
    return y + b

def axial_rope_tables(seq_len):
    rows = seq_len // GRID_W
    row = jnp.broadcast_to(jnp.arange(rows)[:, None], (rows, GRID_W)).reshape(-1).astype(jnp.float32)
    col = jnp.broadcast_to(jnp.arange(GRID_W)[None, :], (rows, GRID_W)).reshape(-1).astype(jnp.float32)
    n_freq = HEAD_DIM // 4
    inv = ROPE_BASE ** (-jnp.arange(n_freq, dtype=jnp.float32) / n_freq)
    ang = jnp.concatenate([row[:, None] * inv, col[:, None] * inv], axis=-1)
    return jnp.cos(ang), jnp.sin(ang)

def apply_rope(x, cos, sin):
    xf = x.astype(jnp.float32)
    half = HEAD_DIM // 2
    x1, x2 = xf[..., :half], xf[..., half:]
    c = cos[None, :, None, :]
    s = sin[None, :, None, :]
    return jnp.concatenate([x1 * c - x2 * s, x2 * c + x1 * s], axis=-1).astype(x.dtype)

def conformer_conv(h, w_pw1, b_pw1, w_dw, b_dw, ln_g, ln_b, w_pw2, b_pw2):
    u = h @ w_pw1 + b_pw1
    a, g = jnp.split(u, 2, axis=-1)
    v = a * jax.nn.sigmoid(g)
    v = dwconv(v, w_dw, b_dw)
    v = jax.nn.silu(layernorm(v, ln_g, ln_b))
    return v @ w_pw2 + b_pw2

def conv_ffn(h, w_up, w_dw, b_dw, w_down):
    u = dwconv(h @ w_up, w_dw, b_dw)
    a, b = jnp.split(u, 2, axis=-1)
    return (jax.nn.silu(a) * b) @ w_down

def split_qkv(h, w_qkv):
    bsz, length, _ = h.shape
    qkv = h @ w_qkv
    q = qkv[..., :N_HEADS * HEAD_DIM].reshape(bsz, length, N_HEADS, HEAD_DIM)
    k = qkv[..., N_HEADS * HEAD_DIM:(N_HEADS + N_KV_HEADS) * HEAD_DIM].reshape(bsz, length, N_KV_HEADS, HEAD_DIM)
    v = qkv[..., (N_HEADS + N_KV_HEADS) * HEAD_DIM:].reshape(bsz, length, N_KV_HEADS, HEAD_DIM)
    return q, k, v

def sink_logits(sink, bsz, nq):
    s = sink.astype(jnp.float32).reshape(N_KV_HEADS, GQA_GROUP)[None, :, :, None, None]
    return jnp.broadcast_to(s, (bsz, N_KV_HEADS, GQA_GROUP, nq, 1))

def window_attention(h_lat, h_ctx, w_qkv, w_o, sink, cos, sin, with_ctx_out):
    bsz, seq, _ = h_lat.shape
    scale = HEAD_DIM ** -0.5
    qc, kc, vc = split_qkv(h_ctx, w_qkv)
    q, k, v = split_qkv(h_lat, w_qkv)
    q = apply_rope(q, cos, sin) * scale
    k = apply_rope(k, cos, sin)
    q = q.reshape(bsz, seq, N_KV_HEADS, GQA_GROUP, HEAD_DIM)
    nb = seq // BLOCK
    k_pad = jnp.pad(k, ((0, 0), (BLOCK, BLOCK), (0, 0), (0, 0)))
    v_pad = jnp.pad(v, ((0, 0), (BLOCK, BLOCK), (0, 0), (0, 0)))
    q_blocks = jnp.moveaxis(q.reshape(bsz, nb, BLOCK, N_KV_HEADS, GQA_GROUP, HEAD_DIM), 1, 0)
    s_sink_lat = sink_logits(sink, bsz, BLOCK)

    def block_fn(args):
        i, qb = args
        kb = lax.dynamic_slice_in_dim(k_pad, i * BLOCK, 3 * BLOCK, axis=1)
        vb = lax.dynamic_slice_in_dim(v_pad, i * BLOCK, 3 * BLOCK, axis=1)
        qpos = i * BLOCK + jnp.arange(BLOCK)
        kpos = i * BLOCK - BLOCK + jnp.arange(3 * BLOCK)
        valid = (jnp.abs(qpos[:, None] - kpos[None, :]) <= WINDOW) & (kpos[None, :] >= 0) & (kpos[None, :] < seq)
        s_band = jnp.einsum('bqhgd,bkhd->bhgqk', qb, kb).astype(jnp.float32)
        s_band = jnp.where(valid[None, None, None], s_band, NEG)
        s_ctx = jnp.einsum('bqhgd,bkhd->bhgqk', qb, kc).astype(jnp.float32)
        p = jax.nn.softmax(jnp.concatenate([s_band, s_ctx, s_sink_lat], axis=-1), axis=-1)
        p_band = p[..., :3 * BLOCK].astype(vb.dtype)
        p_ctx = p[..., 3 * BLOCK:3 * BLOCK + CTX_LEN].astype(vc.dtype)
        o = jnp.einsum('bhgqk,bkhd->bqhgd', p_band, vb) + jnp.einsum('bhgqk,bkhd->bqhgd', p_ctx, vc)
        return o

    o_blocks = lax.map(block_fn, (jnp.arange(nb), q_blocks))
    o_lat = jnp.moveaxis(o_blocks, 0, 1).reshape(bsz, seq, N_HEADS * HEAD_DIM) @ w_o

    o_ctx = None
    if with_ctx_out:
        qcs = (qc * scale).reshape(bsz, CTX_LEN, N_KV_HEADS, GQA_GROUP, HEAD_DIM)
        s_c = jnp.einsum('bqhgd,bkhd->bhgqk', qcs, kc).astype(jnp.float32)
        p_c = jax.nn.softmax(jnp.concatenate([s_c, sink_logits(sink, bsz, CTX_LEN)], axis=-1), axis=-1)
        oc = jnp.einsum('bhgqk,bkhd->bqhgd', p_c[..., :CTX_LEN].astype(vc.dtype), vc)
        o_ctx = oc.reshape(bsz, CTX_LEN, N_HEADS * HEAD_DIM) @ w_o
    return o_lat, o_ctx

def first_inputs(seed: int = 0) -> dict:
    key = jax.random.key(seed)
    ks = jax.random.split(key, 32)
    D = D_MODEL

    def nrm(k, shape, scale):
        return jax.random.normal(k, shape, jnp.float32) * scale

    return {
        'x': nrm(ks[0], (BATCH, SEQ, D), 1.0),
        'c': nrm(ks[1], (BATCH, D), 1.0),
        'ctx': nrm(ks[2], (BATCH, CTX_LEN, D), 1.0),
        'c_ctx': nrm(ks[3], (D,), 1.0),
        'ada_w': nrm(ks[4], (DEPTH, D, 6 * D), 0.02),
        'ada_b': nrm(ks[5], (DEPTH, 6 * D), 0.02),
        'norm1_g': 1.0 + nrm(ks[6], (DEPTH, D), 0.05),
        'norm2_g': 1.0 + nrm(ks[7], (DEPTH, D), 0.05),
        'final_g': 1.0 + nrm(ks[8], (D,), 0.05),
        'conv_w_pw1': nrm(ks[9], (N_CONV_LAYERS, D, 2 * D), D ** -0.5),
        'conv_b_pw1': nrm(ks[10], (N_CONV_LAYERS, 2 * D), 0.02),
        'conv_w_dw': nrm(ks[11], (N_CONV_LAYERS, CONV_WIDTH, D), CONV_WIDTH ** -0.5),
        'conv_b_dw': nrm(ks[12], (N_CONV_LAYERS, D), 0.02),
        'conv_ln_g': 1.0 + nrm(ks[13], (N_CONV_LAYERS, D), 0.05),
        'conv_ln_b': nrm(ks[14], (N_CONV_LAYERS, D), 0.02),
        'conv_w_pw2': nrm(ks[15], (N_CONV_LAYERS, D, D), D ** -0.5),
        'conv_b_pw2': nrm(ks[16], (N_CONV_LAYERS, D), 0.02),
        'attn_w_qkv': nrm(ks[17], (N_ATTN_LAYERS, D, QKV_DIM), D ** -0.5),
        'attn_w_o': nrm(ks[18], (N_ATTN_LAYERS, N_HEADS * HEAD_DIM, D), (N_HEADS * HEAD_DIM) ** -0.5),
        'attn_sink': nrm(ks[19], (N_ATTN_LAYERS, N_HEADS), 1.0),
        'ffn_w_up': nrm(ks[20], (DEPTH, D, 2 * D_FF), D ** -0.5),
        'ffn_w_dw': nrm(ks[21], (DEPTH, FFN_CONV_WIDTH, 2 * D_FF), FFN_CONV_WIDTH ** -0.5),
        'ffn_b_dw': nrm(ks[22], (DEPTH, 2 * D_FF), 0.02),
        'ffn_w_down': nrm(ks[23], (DEPTH, D_FF, D), D_FF ** -0.5),
    }

def first_block(x, c, ctx, c_ctx, ada_w, ada_b, norm1_g, norm2_g, final_g,
              conv_w_pw1, conv_b_pw1, conv_w_dw, conv_b_dw, conv_ln_g, conv_ln_b, conv_w_pw2, conv_b_pw2,
              attn_w_qkv, attn_w_o, attn_sink,
              ffn_w_up, ffn_w_dw, ffn_b_dw, ffn_w_down):
    cos, sin = axial_rope_tables(x.shape[1])
    sc = jax.nn.silu(c)
    scc = jax.nn.silu(c_ctx)
    h_lat = x
    h_ctx = ctx
    for i in range(DEPTH):
        last = i == DEPTH - 1
        mod_lat = (sc @ ada_w[i] + ada_b[i])[:, None, :]
        mod_ctx = scc @ ada_w[i] + ada_b[i]
        sh1, sc1, g1, sh2, sc2, g2 = jnp.split(mod_lat, 6, axis=-1)
        csh1, csc1, cg1, csh2, csc2, cg2 = jnp.split(mod_ctx, 6, axis=-1)
        a_lat = modulate(rmsnorm(h_lat, norm1_g[i]), sh1, sc1)
        j = i // N_MIXERS
        if i % N_MIXERS == 0:
            y_lat = conformer_conv(a_lat, conv_w_pw1[j], conv_b_pw1[j], conv_w_dw[j], conv_b_dw[j],
                                   conv_ln_g[j], conv_ln_b[j], conv_w_pw2[j], conv_b_pw2[j])
            if not last:
                a_ctx = modulate(rmsnorm(h_ctx, norm1_g[i]), csh1, csc1)
                y_ctx = conformer_conv(a_ctx, conv_w_pw1[j], conv_b_pw1[j], conv_w_dw[j], conv_b_dw[j],
                                       conv_ln_g[j], conv_ln_b[j], conv_w_pw2[j], conv_b_pw2[j])
        else:
            a_ctx = modulate(rmsnorm(h_ctx, norm1_g[i]), csh1, csc1)
            y_lat, y_ctx = window_attention(a_lat, a_ctx, attn_w_qkv[j], attn_w_o[j], attn_sink[j],
                                            cos, sin, not last)
        h_lat = h_lat + g1 * y_lat
        b_lat = modulate(rmsnorm(h_lat, norm2_g[i]), sh2, sc2)
        h_lat = h_lat + g2 * conv_ffn(b_lat, ffn_w_up[i], ffn_w_dw[i], ffn_b_dw[i], ffn_w_down[i])
        if not last:
            h_ctx = h_ctx + cg1 * y_ctx
            b_ctx = modulate(rmsnorm(h_ctx, norm2_g[i]), csh2, csc2)
            h_ctx = h_ctx + cg2 * conv_ffn(b_ctx, ffn_w_up[i], ffn_w_dw[i], ffn_b_dw[i], ffn_w_down[i])
    return rmsnorm(h_lat, final_g)


DEPTH_2 = 1

MEM_LEN = 256
RMS_EPS = 1e-6
F_GROUPS = 8
F_GROUP_DIM = 64
F_WIDTH = F_GROUPS * F_GROUP_DIM
MLA_HEADS = 8
QK_NOPE_DIM = 64
QK_ROPE_DIM = 32
V_HEAD_DIM = 64
Q_LORA_RANK = 384
KV_LORA_RANK = 256
ROPE_THETA = 10000.0
Q_BLOCK = 128
MLA_OUT = MLA_HEADS * V_HEAD_DIM
MIX_WIDTH = F_WIDTH + MLA_OUT
IN_WIDTH = F_WIDTH + Q_LORA_RANK + KV_LORA_RANK + QK_ROPE_DIM
IN_SPLITS = (F_WIDTH, F_WIDTH + Q_LORA_RANK, F_WIDTH + Q_LORA_RANK + KV_LORA_RANK)
MEM_HEADS = 4
MEM_HEAD_DIM = D_MODEL // MEM_HEADS
N_EXPERTS = 16
CAPACITY_FACTOR = 2
D_EXPERT = D_MODEL


def rms_norm(x, g):
    xf = x.astype(jnp.float32)
    y = xf * lax.rsqrt(jnp.mean(xf * xf, axis=-1, keepdims=True) + RMS_EPS)
    return (y * g.astype(jnp.float32)).astype(x.dtype)

def rope_tables(positions):
    freqs = 1.0 / (ROPE_THETA ** (jnp.arange(0, QK_ROPE_DIM, 2, dtype=jnp.float32) / QK_ROPE_DIM))
    ang = positions.astype(jnp.float32)[..., None] * freqs
    return jnp.cos(ang), jnp.sin(ang)

def apply_rope_2(x, cos, sin):
    xf = x.astype(jnp.float32)
    x1, x2 = jnp.split(xf, 2, axis=-1)
    out = jnp.concatenate([x1 * cos - x2 * sin, x1 * sin + x2 * cos], axis=-1)
    return out.astype(x.dtype)

def fourier_mix(u_f, w_fourier):
    B, S, _ = u_f.shape
    ug = u_f.reshape(B, S, F_GROUPS, F_GROUP_DIM).astype(jnp.float32)
    z = jnp.fft.fft2(ug, axes=(1, 3), norm="ortho").real.astype(u_f.dtype)
    y = jnp.einsum("bsgc,gce->bsge", z, w_fourier)
    return y.reshape(B, S, F_WIDTH)

def mla_attention(u_q, u_kv, u_kr, cos, sin, g_q_lat, w_q_up, g_kv_lat, w_kv_up):
    B, S, _ = u_q.shape
    q = (rms_norm(u_q, g_q_lat) @ w_q_up).reshape(B, S, MLA_HEADS, QK_NOPE_DIM + QK_ROPE_DIM)
    q_nope, q_rope = q[..., :QK_NOPE_DIM], q[..., QK_NOPE_DIM:]
    q_rope = apply_rope_2(q_rope, cos[:, :, None, :], sin[:, :, None, :])
    kv = (rms_norm(u_kv, g_kv_lat) @ w_kv_up).reshape(B, S, MLA_HEADS, QK_NOPE_DIM + V_HEAD_DIM)
    k_nope, v = kv[..., :QK_NOPE_DIM], kv[..., QK_NOPE_DIM:]
    k_rope = apply_rope_2(u_kr, cos, sin)
    scale = (QK_NOPE_DIM + QK_ROPE_DIM) ** -0.5
    nb = S // Q_BLOCK
    qn = q_nope.reshape(B, nb, Q_BLOCK, MLA_HEADS, QK_NOPE_DIM).swapaxes(0, 1)
    qr = q_rope.reshape(B, nb, Q_BLOCK, MLA_HEADS, QK_ROPE_DIM).swapaxes(0, 1)

    def block(args):
        qn_b, qr_b = args
        s = (jnp.einsum("bqhd,bkhd->bhqk", qn_b, k_nope)
             + jnp.einsum("bqhd,bkd->bhqk", qr_b, k_rope))
        p = jax.nn.softmax(s.astype(jnp.float32) * scale, axis=-1).astype(v.dtype)
        return jnp.einsum("bhqk,bkhd->bqhd", p, v)

    o = lax.map(block, (qn, qr))
    return o.swapaxes(0, 1).reshape(B, S, MLA_OUT)

def memory_cross_attention(hq, mn, w_mem_q, w_mem_kv, w_mem_o):
    B, S, D = hq.shape
    M = mn.shape[1]
    q = (hq @ w_mem_q).reshape(B, S, MEM_HEADS, MEM_HEAD_DIM)
    k, v = jnp.split(mn @ w_mem_kv, 2, axis=-1)
    k = k.reshape(B, M, MEM_HEADS, MEM_HEAD_DIM)
    v = v.reshape(B, M, MEM_HEADS, MEM_HEAD_DIM)
    s = jnp.einsum("bshd,bmhd->bhsm", q, k).astype(jnp.float32) * (MEM_HEAD_DIM ** -0.5)
    p = jax.nn.softmax(s, axis=-1).astype(v.dtype)
    o = jnp.einsum("bhsm,bmhd->bshd", p, v).reshape(B, S, D)
    return o @ w_mem_o

def expert_choice_moe(h, w_router, w_gate, w_up, w_down):
    B, S, D = h.shape
    cap = CAPACITY_FACTOR * S // N_EXPERTS
    aff = jax.nn.softmax((h @ w_router).astype(jnp.float32), axis=-1)
    gates, idx = lax.top_k(aff.swapaxes(1, 2), cap)
    xin = jax.vmap(lambda hb, ib: hb[ib])(h, idx)
    a = jnp.einsum("becd,edf->becf", xin, w_gate)
    b = jnp.einsum("becd,edf->becf", xin, w_up)
    y = jnp.einsum("becf,efd->becd", jax.nn.silu(a) * b, w_down)
    y = y * gates.astype(y.dtype)[..., None]
    out = jax.vmap(lambda ib, yb: jnp.zeros((S, D), yb.dtype).at[ib].add(yb))(
        idx.reshape(B, -1), y.reshape(B, -1, D))
    return out

def second_inputs(seed: int = 0) -> dict:
    key = jax.random.key(seed)
    ks = jax.random.split(key, 24)
    f32 = jnp.float32

    def nrm(k, shape, fan_in):
        return jax.random.normal(k, shape, f32) * (fan_in ** -0.5)

    def gain(k, shape):
        return 1.0 + 0.02 * jax.random.normal(k, shape, f32)

    L = DEPTH_2
    x = jax.random.normal(ks[0], (BATCH, SEQ, D_MODEL), f32)
    mem = jax.random.normal(ks[1], (BATCH, MEM_LEN, D_MODEL), f32)
    offs = jax.random.randint(ks[2], (BATCH, 1), 0, 1024, dtype=jnp.int32)
    positions = offs + jnp.arange(SEQ, dtype=jnp.int32)[None, :]
    return {
        "x": x,
        "mem": mem,
        "positions": positions,
        "g_mix": gain(ks[3], (L, D_MODEL)),
        "w_in": nrm(ks[4], (L, D_MODEL, IN_WIDTH), D_MODEL),
        "g_q_lat": gain(ks[5], (L, Q_LORA_RANK)),
        "w_q_up": nrm(ks[6], (L, Q_LORA_RANK, MLA_HEADS * (QK_NOPE_DIM + QK_ROPE_DIM)), Q_LORA_RANK),
        "g_kv_lat": gain(ks[7], (L, KV_LORA_RANK)),
        "w_kv_up": nrm(ks[8], (L, KV_LORA_RANK, MLA_HEADS * (QK_NOPE_DIM + V_HEAD_DIM)), KV_LORA_RANK),
        "w_fourier": nrm(ks[9], (L, F_GROUPS, F_GROUP_DIM, F_GROUP_DIM), F_GROUP_DIM),
        "w_out": nrm(ks[10], (L, MIX_WIDTH, D_MODEL), MIX_WIDTH),
        "g_mem_q": gain(ks[11], (L, D_MODEL)),
        "g_mem_kv": gain(ks[12], (L, D_MODEL)),
        "w_mem_q": nrm(ks[13], (L, D_MODEL, D_MODEL), D_MODEL),
        "w_mem_kv": nrm(ks[14], (L, D_MODEL, 2 * D_MODEL), D_MODEL),
        "w_mem_o": nrm(ks[15], (L, D_MODEL, D_MODEL), D_MODEL),
        "g_ffn": gain(ks[16], (L, D_MODEL)),
        "w_router": nrm(ks[17], (L, D_MODEL, N_EXPERTS), D_MODEL),
        "w_exp_gate": nrm(ks[18], (L, N_EXPERTS, D_MODEL, D_EXPERT), D_MODEL),
        "w_exp_up": nrm(ks[19], (L, N_EXPERTS, D_MODEL, D_EXPERT), D_MODEL),
        "w_exp_down": nrm(ks[20], (L, N_EXPERTS, D_EXPERT, D_MODEL), D_EXPERT),
        "g_final": gain(ks[21], (D_MODEL,)),
    }

def second_block(x, mem, positions, g_mix, w_in, g_q_lat, w_q_up, g_kv_lat, w_kv_up, w_fourier,
              w_out, g_mem_q, g_mem_kv, w_mem_q, w_mem_kv, w_mem_o, g_ffn, w_router,
              w_exp_gate, w_exp_up, w_exp_down, g_final):
    cos, sin = rope_tables(positions)
    for l in range(DEPTH_2):
        h = rms_norm(x, g_mix[l])
        u = h @ w_in[l]
        u_f, u_q, u_kv, u_kr = jnp.split(u, IN_SPLITS, axis=-1)
        y_f = fourier_mix(u_f, w_fourier[l])
        y_a = mla_attention(u_q, u_kv, u_kr, cos, sin, g_q_lat[l], w_q_up[l], g_kv_lat[l], w_kv_up[l])
        x = x + jnp.concatenate([y_f, y_a], axis=-1) @ w_out[l]
        x = x + memory_cross_attention(rms_norm(x, g_mem_q[l]), rms_norm(mem, g_mem_kv[l]),
                                       w_mem_q[l], w_mem_kv[l], w_mem_o[l])
        x = x + expert_choice_moe(rms_norm(x, g_ffn[l]), w_router[l],
                                  w_exp_gate[l], w_exp_up[l], w_exp_down[l])
    return rms_norm(x, g_final)


def setup_inputs(seed=0):
    out = dict(first_inputs(seed))
    for name, value in second_inputs(seed + 1).items():
        if name != "x":
            out[name + "_2"] = value
    return out


def reference(
    x, c, ctx, c_ctx, ada_w, ada_b, norm1_g, norm2_g, final_g, conv_w_pw1, conv_b_pw1,
    conv_w_dw, conv_b_dw, conv_ln_g, conv_ln_b, conv_w_pw2, conv_b_pw2, attn_w_qkv, attn_w_o,
    attn_sink, ffn_w_up, ffn_w_dw, ffn_b_dw, ffn_w_down, mem_2, positions_2, g_mix_2, w_in_2,
    g_q_lat_2, w_q_up_2, g_kv_lat_2, w_kv_up_2, w_fourier_2, w_out_2, g_mem_q_2, g_mem_kv_2,
    w_mem_q_2, w_mem_kv_2, w_mem_o_2, g_ffn_2, w_router_2, w_exp_gate_2, w_exp_up_2,
    w_exp_down_2, g_final_2,
):
    x = first_block(
        x, c, ctx, c_ctx, ada_w, ada_b, norm1_g, norm2_g, final_g, conv_w_pw1, conv_b_pw1,
        conv_w_dw, conv_b_dw, conv_ln_g, conv_ln_b, conv_w_pw2, conv_b_pw2, attn_w_qkv,
        attn_w_o, attn_sink, ffn_w_up, ffn_w_dw, ffn_b_dw, ffn_w_down,
    )
    return second_block(
        x, mem_2, positions_2, g_mix_2, w_in_2, g_q_lat_2, w_q_up_2, g_kv_lat_2, w_kv_up_2,
        w_fourier_2, w_out_2, g_mem_q_2, g_mem_kv_2, w_mem_q_2, w_mem_kv_2, w_mem_o_2, g_ffn_2,
        w_router_2, w_exp_gate_2, w_exp_up_2, w_exp_down_2, g_final_2,
    )


_drawn_inputs = setup_inputs


def setup_inputs(seed=0):
    import zlib

    import numpy as np

    out = dict(_drawn_inputs(seed))
    spreads = {}
    factors = {'norm1_g': 3.033,
     'conv_b_pw1': 7.6,
     'conv_b_dw': 4.733,
     'conv_ln_g': 2.764,
     'conv_ln_b': 7.015,
     'conv_b_pw2': 5.133,
     'attn_sink': 64.0,
     'ffn_b_dw': 3.63,
     'g_mix_2': 4.56,
     'g_q_lat_2': 8.0,
     'g_kv_lat_2': 8.0,
     'g_mem_q_2': 8.0,
     'g_mem_kv_2': 8.0,
     'g_ffn_2': 4.058,
     'g_final_2': 8.017}
    for name, (base, spread) in spreads.items():
        noise = np.random.default_rng([zlib.crc32(name.encode()), seed]).standard_normal(out[name].shape)
        drawn = base * np.exp(spread * noise) if base else spread * noise
        out[name] = jnp.asarray(drawn.astype(out[name].dtype))
    for name, factor in factors.items():
        out[name] = (out[name] * factor).astype(out[name].dtype)
    return out
```

```python
import math
from contextlib import contextmanager

import numpy as np

import concourse.bass as bass
from concourse import mybir

F32 = mybir.dt.float32
F32R = mybir.dt.float32r
I32 = mybir.dt.int32
ACT = mybir.ActivationFunctionType
ALU = mybir.AluOpType
AX = mybir.AxisListType

P = 128
D = 1024
KD = D // P
LAT, CTX = 512, 256
TOK = LAT + CTX
EPS = 1e-6
CONV_TAPS = 31
PAD = (CONV_TAPS - 1) // 2
LAT_AT, CTX_AT = PAD, PAD + LAT + 2 * PAD
VLEN = CTX_AT + CTX + PAD
CLEN = VLEN - 2 * PAD
CLAT, CCTX = 0, LAT + 2 * PAD
D_FF = 2816
HID = D_FF // P // 2
HEADS, KV_HEADS, HEAD_DIM = 16, 4, 64
BLOCK = 128
NEG = -1e30
SLOT = HID * P
RAWS, SPLITS = 4, 2
STAGE_SEMS = 40
LATENT, BOTH, CONTEXT = [(0, LAT)], [(0, LAT), (LAT, TOK)], [(LAT, TOK)]

PARAMS = {}
_at = 0
for _name, _n in (("norm1_0", 16), ("norm2_0", 16), ("norm1_1", 16), ("norm2_1", 16), ("ada_b0", 96), ("ada_b1", 96),
                  ("b_pw1", 16), ("w_dw", 8 * CONV_TAPS), ("b_dw", 8), ("ln_g", 8), ("ln_b", 8), ("b_pw2", 8),
                  ("ffn0", 44 * 4), ("ffn1", 44 * 4), ("sink", HEADS), ("g_mix", 16), ("g_mem", 16), ("g_ffn", 16),
                  ("g_q", 3), ("g_kv", 2), ("cond", 16), ("final_1", 8), ("freq", 1), ("slot", 1), ("final_2", 8)):
    PARAMS[_name] = (_at, _n)
    _at += _n
N_PARAMS = _at


class Gemm:
    def __init__(self, name, src, k):
        self.name, self.src, self.k = name, src, k
        self.n, self.length = src.shape[0], k * P
        self.base, self.next = 0, None


class Steps:
    def __init__(self, eng, sem, per_round=0):
        self.eng, self.sem, self.per_round = eng, sem, per_round
        self.base, self.n = 0, 0

    def round(self, i):
        self.base, self.n = self.per_round * i, 0

    def did(self, instruction):
        instruction.then_inc(self.sem, 1)
        self.n += 1

    def wait(self):
        self.eng.wait_ge(self.sem, self.base + self.n)


class Program:
    def __init__(self, nc, dram):
        self.nc, self.dram = nc, dram
        self.stage_no = 0
        self.stage_sems = []
        nc_sem = nc.alloc_semaphore
        self.raw_landed = [nc_sem(f"raw_landed{i}") for i in range(RAWS)]
        self.weights_hi = nc_sem("weights_hi")
        self.weights_lo = nc_sem("weights_lo")
        self.unit_done = nc_sem("unit_done")
        self.raw_landed_x = nc_sem("x_landed")
        first = self.raw_landed_x.num + 1
        self.banks = [first, first + STAGE_SEMS]
        base = (nc.sbuf_base + 63) // 64 * 64
        self.top = nc.sbuf_usable_end // 64 * 64
        self.small = base
        self.small_end = base + 8192
        at = self.small_end
        self.X = self.at("X", [P, KD, TOK], F32, at)
        self.XNH = self.at("XNH", [P, KD, TOK], F32R, at + 24576)
        self.XNL = self.at("XNL", [P, KD, TOK], F32R, at + 2 * 24576)
        at += 3 * 24576
        self.RAW = self.at("RAW", [P, RAWS, SLOT], F32, at)
        at += RAWS * SLOT * 4
        self.WHI = self.at("WHI", [P, SPLITS, SLOT], F32R, at)
        at += SPLITS * SLOT * 4
        self.WLO = self.at("WLO", [P, SPLITS, SLOT], F32R, at)
        at += SPLITS * SLOT * 4
        self.arena = at
        self.tmp = at + 2 * HID * TOK * 4
        self.PRM = self.keep("PRM", [P, N_PARAMS], F32)
        self.ONES = self.keep("ONES", [P, P], F32)
        self.EPSC = self.keep("EPSC", [P, 1], F32)
        self.IDENT = self.keep("IDENT", [P, P], F32)
        self.MOD = [self.keep(f"MOD{l}", [P, 48, 2], F32) for l in range(2)]
        self.GAIN = [[self.keep(f"GAIN{l}{n}", [P, KD, 2], F32) for n in range(2)] for l in range(2)]
        self.G1B = self.keep("G1B", [P, KD, 2], F32)
        self.SC = self.keep("SC", [P, KD, 2], F32)
        self.PS = nc.alloc_psum_tensor("PS", [P, 4, 1024], F32)

    def at(self, name, shape, dtype, offset):
        size = 4 * math.prod(shape[1:])
        assert offset % 32 == 0 and offset + size <= self.top, (name, offset, size, self.top)
        return self.nc.alloc_sbuf_tensor_at(name, shape, dtype, offset=offset)

    def keep(self, name, shape, dtype):
        t = self.at(name, shape, dtype, self.small)
        self.small += (4 * math.prod(shape[1:]) + 31) // 32 * 32
        assert self.small <= self.small_end, (name, self.small - self.small_end)
        return t

    def region(self, start, end):
        return Region(self, start, end)

    def sem(self, name):
        s = self.nc.alloc_semaphore(f"{name}_{self.stage_no}", num=self.banks[self.stage_no % 2] + len(self.stage_sems))
        self.stage_sems.append(s)
        assert len(self.stage_sems) <= STAGE_SEMS
        return s

    @contextmanager
    def block(self, name):
        with self.nc.Block(f"{name}{self.stage_no}") as block:
            yield block
        self.nc.clear_and_free_semaphores(self.stage_sems)
        self.stage_sems = []
        self.stage_no += 1

    def prm(self, name, index=0, n=1):
        a = PARAMS[name][0]
        return self.PRM[:, bass.ds(a + index, n)]

    def prm3(self, name, width):
        a, n = PARAMS[name]
        return self.PRM[:, a:a + n].rearrange("p (k w) -> p k w", w=width)


class Region:
    def __init__(self, prog, start, end):
        self.prog, self.at_, self.end = prog, (start + 31) // 32 * 32, end

    def take(self, name, shape, dtype=F32):
        t = self.prog.at(f"{name}_{self.prog.stage_no}", shape, dtype, self.at_)
        self.at_ += (4 * math.prod(shape[1:]) + 31) // 32 * 32
        assert self.at_ <= self.end, (name, self.at_ - self.end)
        return t


def f32(ap):
    return ap.bitcast(F32)



def run_units(eng, n, step):
    rounds = max((n - 4) // 4, 0)
    if rounds > 1:
        with eng.Fori(0, rounds) as i:
            for s in range(4):
                step(i, s)
    elif rounds == 1:
        for s in range(4):
            step(0, s)
    for u in range(4 * rounds, n):
        step(u // 4, u % 4)


def ahead(g, i, s, by):
    if isinstance(i, int) and 4 * i + s + by >= g.n:
        if g.next is None:
            return None, None
        return g.next, 4 * i + s + by - g.n
    return g, 4 * i + s + by


def load_ahead(prog, sp, g, i, s):
    to, u = ahead(g, i, s, RAWS)
    if to is None:
        return
    slot = (g.base + s) % RAWS
    sp.wait_ge(prog.weights_lo, g.base + 4 * i + s + 1)
    sp.dma_start(prog.RAW[:, slot, 0:to.length], to.src[u]).then_inc(prog.raw_landed[slot], 16)


def split_hi_ahead(prog, act, g, i, s):
    to, _ = ahead(g, i, s, SPLITS)
    if to is None:
        return
    at = g.base + s + SPLITS
    act.wait_ge(prog.raw_landed[at % RAWS], 16 * (i + at // RAWS + 1))
    act.wait_ge(prog.unit_done, g.base + 4 * i + s + 1)
    act.activation(prog.WHI[:, at % SPLITS, 0:to.length], prog.RAW[:, at % RAWS, 0:to.length],
                   ACT.Copy).then_inc(prog.weights_hi, 1)


def split_lo_ahead(prog, dve, g, i, s):
    to, _ = ahead(g, i, s, SPLITS)
    if to is None:
        return
    at = g.base + s + SPLITS
    dve.wait_ge(prog.weights_hi, g.base + 4 * i + s + SPLITS + 1)
    dve.wait_ge(prog.unit_done, g.base + 4 * i + s + 1)
    dve.tensor_tensor(prog.WLO[:, at % SPLITS, 0:to.length], prog.RAW[:, at % RAWS, 0:to.length],
                      f32(prog.WHI[:, at % SPLITS, 0:to.length]), ALU.subtract).then_inc(prog.weights_lo, 1)


def multiply(prog, pe, g, i, s, xh, xl, segments, psum_free):
    slot = (g.base + s) % SPLITS
    pe.wait_ge(prog.weights_lo, g.base + 4 * i + s + 1)
    pe.wait_ge(psum_free, 4 * i + s + 1)
    last = None
    for k in range(g.k):
        wh = prog.WHI[:, slot, k * P:(k + 1) * P]
        wl = prog.WLO[:, slot, k * P:(k + 1) * P]
        for n, (w, x) in enumerate(((wh, xh), (wh, xl), (wl, xh))):
            for a, b in segments:
                last = pe.matmul(prog.PS[:, s, a:b], w, x[:, k, a:b], start=(k == 0 and n == 0),
                                 stop=(k == g.k - 1 and n == 2))
    last.then_inc(prog.unit_done, 1)


def multiply_tokens(prog, pe, g, i, s, xh, xl, chunks, psum_free):
    slot = (g.base + s) % SPLITS
    pe.wait_ge(prog.weights_lo, g.base + 4 * i + s + 1)
    pe.wait_ge(psum_free, 4 * i + s + 1)
    last = None
    for n, t in enumerate(chunks):
        for k in range(g.k):
            wh, wl = (w[:, slot, k * P:(k + 1) * P] for w in (prog.WHI, prog.WLO))
            for m, (x, w) in enumerate(((xh, wh), (xh, wl), (xl, wh))):
                last = pe.matmul(prog.PS[:, s, n * P:(n + 1) * P], x[:, k, t:t + P], w,
                                 start=(k == 0 and m == 0), stop=(k == g.k - 1 and m == 2))
    last.then_inc(prog.unit_done, 1)



def start(prog, gemms):
    nc = prog.nc
    first = gemms[0]
    loaded, consts, silu = prog.sem("loaded"), prog.sem("consts"), prog.sem("silu")
    with prog.block("start") as block:
        @block.sync
        def _(sp):
            sp.dma_start(prog.PRM[:], prog.dram["params"]).then_inc(loaded, 16)
            sp.dma_start(prog.IDENT[:], prog.dram["ident"]).then_inc(loaded, 16)
            sp.dma_start(prog.X[:], prog.dram["xT"]).then_inc(prog.raw_landed_x, 16)
            for u in range(RAWS):
                sp.dma_start(prog.RAW[:, u, 0:first.length], first.src[u]).then_inc(prog.raw_landed[u], 16)

        @block.scalar
        def _(act):
            act.wait_ge(loaded, 32)
            act.activation(prog.SC[:], prog.prm3("cond", 2), ACT.Silu).then_inc(silu, 1)
            for u in range(SPLITS):
                act.wait_ge(prog.raw_landed[u], 16)
                act.activation(prog.WHI[:, u, 0:first.length], prog.RAW[:, u, 0:first.length],
                               ACT.Copy).then_inc(prog.weights_hi, 1)

        @block.vector
        def _(dve):
            dve.memset(prog.ONES[:], 1.0 / D).then_inc(consts, 1)
            dve.memset(prog.EPSC[:], EPS).then_inc(consts, 1)
            for u in range(SPLITS):
                dve.wait_ge(prog.weights_hi, u + 1)
                dve.tensor_tensor(prog.WLO[:, u, 0:first.length], prog.RAW[:, u, 0:first.length],
                                  f32(prog.WHI[:, u, 0:first.length]), ALU.subtract).then_inc(prog.weights_lo, 1)


ADA_RING = 4


class Ada:
    def __init__(self, prog, layer, ring, psum):
        self.prog, self.layer, self.ring, self.psum = prog, layer, ring, psum
        self.src = prog.dram["ada"]
        self.landed = [prog.sem(f"ada_landed{s}") for s in range(ADA_RING)]
        self.used, self.step = prog.sem("ada_used"), prog.sem("ada_step")

    def load(self, sp):
        rounds = 48 // ADA_RING
        for s in range(ADA_RING):
            sp.dma_start(self.ring[:, s, :], self.src[48 * self.layer + s]).then_inc(self.landed[s], 16)
        with sp.Fori(1, rounds) as i:
            for s in range(ADA_RING):
                sp.wait_ge(self.used, ADA_RING * i - ADA_RING + s + 1)
                sp.dma_start(self.ring[:, s, :], self.src[48 * self.layer + ADA_RING * i + s]).then_inc(self.landed[s], 16)

    def multiply(self, pe):
        with pe.Fori(0, 48 // ADA_RING) as i:
            for s in range(ADA_RING):
                pe.wait_ge(self.landed[s], 16 * i + 16)
                for k in range(KD):
                    last = pe.matmul(self.psum[:, bass.ds(2 * (ADA_RING * i + s), 2)], self.ring[:, s, k * P:(k + 1) * P],
                                     self.prog.SC[:, k, :], start=(k == 0), stop=(k == KD - 1))
                last.then_inc(self.used, 1)

    def finish(self, dve):
        prog, l = self.prog, self.layer
        mod = prog.MOD[l]
        step = Steps(dve, self.step)
        dve.wait_ge(self.used, 48)
        step.did(dve.tensor_tensor(mod[:].rearrange("p a b -> p (a b)"), self.psum[:, 0:96],
                                   prog.PRM[:, PARAMS[f"ada_b{l}"][0]:PARAMS[f"ada_b{l}"][0] + 96], ALU.add))
        step.wait()
        for n in range(2):
            scale = mod[:, 24 * n + 8:24 * n + 16, :]
            step.did(dve.scalar_tensor_tensor(prog.GAIN[l][n][:], scale, 1.0, prog.prm3(f"norm{n + 1}_{l}", 2),
                                              ALU.add, ALU.mult))
        if l == 0:
            for t in range(2):
                step.did(dve.tensor_tensor(prog.G1B[:, :, t], mod[:, 16:24, t], prog.prm("b_pw2", 0, 8), ALU.mult))
        return step


def condition(prog):
    reg = prog.region(prog.arena, prog.tmp)
    with prog.block("ada") as block:
        ada = Ada(prog, 0, reg.take("ADAW", [P, ADA_RING, D]), prog.PS[:, 0, 0:512])

        @block.sync
        def _(sp):
            ada.load(sp)
            sp.wait_ge(prog.raw_landed_x, 16)

        @block.tensor
        def _(pe):
            ada.multiply(pe)

        @block.vector
        def _(dve):
            ada.finish(dve).wait()


def norm(prog, gain, shift, segments, out_hi=None, out_lo=None):
    tok = segments[-1][1]
    out_hi, out_lo = out_hi or prog.XNH, out_lo or prog.XNL
    with prog.block("norm") as block:
        reg = prog.region(prog.tmp, prog.top)
        sq = reg.take("SQ", [P, 2, tok])
        scaled = reg.take("SCALED", [P, 2, tok])
        rstd = reg.take("RSTD", [P, tok])
        mean = prog.PS[:, 0, 0:tok]
        squared, summed, root, rstd_done = prog.sem("squared"), prog.sem("summed"), prog.sem("root"), prog.sem("rstd")
        normed, full, hi, lo = prog.sem("normed"), prog.sem("full"), prog.sem("hi"), prog.sem("lo")

        @block.scalar
        def _(act):
            for k in range(KD):
                if k >= 2:
                    act.wait_ge(summed, k - 1)
                act.activation(sq[:, k % 2, :], prog.X[:, k, 0:tok], ACT.Square).then_inc(squared, 1)
            act.wait_ge(summed, KD)
            act.activation(rstd[:], mean, ACT.Sqrt, bias=prog.EPSC[:, 0:1]).then_inc(root, 1)
            for k in range(KD):
                act.wait_ge(normed, k + 1)
                if k >= 2:
                    act.wait_ge(lo, k - 1)
                for t, (a, b) in enumerate(segments):
                    ins = act.activation(scaled[:, k % 2, a:b], sq[:, k % 2, a:b], ACT.Identity,
                                         bias=0.0 if shift is None else shift[:, k, t:t + 1], scale=gain[:, k, t:t + 1])
                ins.then_inc(full, 1)
                act.wait_ge(full, k + 1)
                act.activation(out_hi[:, k, 0:tok], scaled[:, k % 2, :], ACT.Copy).then_inc(hi, 1)

        @block.tensor
        def _(pe):
            for k in range(KD):
                pe.wait_ge(squared, k + 1)
                for a, b in segments:
                    last = pe.matmul(mean[:, a:b], prog.ONES[:], sq[:, k % 2, a:b], start=(k == 0), stop=(k == KD - 1))
                last.then_inc(summed, 1)

        @block.vector
        def _(dve):
            dve.wait_ge(root, 1)
            dve.reciprocal(rstd[:], rstd[:]).then_inc(rstd_done, 1)
            dve.wait_ge(rstd_done, 1)
            for k in range(KD + 1):
                if k < KD:
                    if k >= 2:
                        dve.wait_ge(full, k - 1)
                    dve.tensor_tensor(sq[:, k % 2, :], prog.X[:, k, 0:tok], rstd[:], ALU.mult).then_inc(normed, 1)
                if k >= 1:
                    dve.wait_ge(hi, k)
                    dve.tensor_tensor(out_lo[:, k - 1, 0:tok], scaled[:, (k - 1) % 2, :],
                                      f32(out_hi[:, k - 1, 0:tok]), ALU.subtract).then_inc(lo, 1)


def gated_projection(prog, g):
    with prog.block("pw1") as block:
        reg = prog.region(prog.arena, prog.tmp)
        V = prog.V = reg.take("V", [P, KD, VLEN])
        prog.v_end = reg.at_
        tmp = prog.region(prog.tmp, prog.top)
        sig = tmp.take("SIG", [P, 2, TOK])
        psum_free, sigmoid, gated, padded = prog.sem("psum_free"), prog.sem("sigmoid"), prog.sem("gated"), prog.sem("pad")

        @block.sync
        def _(sp):
            run_units(sp, g.n, lambda i, s: load_ahead(prog, sp, g, i, s))

        @block.scalar
        def _(act):
            def step(i, s):
                split_hi_ahead(prog, act, g, i, s)
                if s % 2 == 0:
                    return
                act.wait_ge(prog.unit_done, g.base + 4 * i + s + 1)
                act.wait_ge(gated, 2 * i + s // 2 + 1)
                act.activation(sig[:, s // 2, :], prog.PS[:, s, 0:TOK], ACT.Sigmoid,
                               bias=prog.prm("b_pw1", 4 * i + s)).then_inc(sigmoid, 1)
            run_units(act, g.n, step)

        @block.vector
        def _(dve):
            dve.nop().then_inc(gated, 2)
            for a, b in ((0, LAT_AT), (LAT_AT + LAT, CTX_AT), (CTX_AT + CTX, VLEN)):
                dve.memset(V[:, :, a:b], 0.0).then_inc(padded, 1)

            def step(i, s):
                split_lo_ahead(prog, dve, g, i, s)
                if s % 2 == 0:
                    return
                dve.wait_ge(sigmoid, 2 * i + s // 2 + 1)
                for (a, b), at in zip(BOTH, (LAT_AT, CTX_AT)):
                    ins = dve.scalar_tensor_tensor(V[:, 2 * i + s // 2, at:at + b - a], prog.PS[:, s - 1, a:b],
                                                   prog.prm("b_pw1", 4 * i + s - 1), sig[:, s // 2, a:b], ALU.add, ALU.mult)
                ins.then_inc(gated, 1)
            run_units(dve, g.n, step)

        @block.tensor
        def _(pe):
            def step(i, s):
                if s % 2 == 0:
                    pe.wait_ge(gated, 2 * i + s // 2 + 1)
                multiply(prog, pe, g, i, s, prog.XNH, prog.XNL, BOTH, psum_free)
            pe.nop().then_inc(psum_free, g.n)
            run_units(pe, g.n, step)


def depthwise(prog):
    with prog.block("conv") as block:
        reg = prog.region(prog.v_end, prog.tmp)
        C = prog.C = reg.take("C", [P, KD, CLEN])
        ada = Ada(prog, 1, prog.region(prog.tmp, prog.top).take("ADAW", [P, ADA_RING, D]), prog.PS[:, 0, 0:512])
        tap_done = prog.sem("tap_done")

        @block.sync
        def _(sp):
            ada.load(sp)

        @block.tensor
        def _(pe):
            ada.multiply(pe)

        @block.vector
        def _(dve):
            steps = Steps(dve, tap_done, 2 * CONV_TAPS)
            with dve.Fori(0, KD // 2) as i:
                steps.round(i)
                for tap in range(CONV_TAPS):
                    for c in range(2):
                        v = prog.V[:, 2 * i + c, tap:tap + CLEN]
                        w = prog.prm("w_dw", (2 * i + c) * CONV_TAPS + tap)
                        out = C[:, 2 * i + c, :]
                        if tap == 0:
                            steps.did(dve.tensor_scalar(out, v, w, prog.prm("b_dw", 2 * i + c), ALU.mult, ALU.add))
                        else:
                            dve.wait_ge(tap_done, steps.base + steps.n - 1)
                            steps.did(dve.scalar_tensor_tensor(out, v, w, out, ALU.mult, ALU.add))
            ada.finish(dve).wait()


def layer_norm_silu(prog):
    with prog.block("ln") as block:
        reg = prog.region(prog.tmp, prog.top)
        tmp = reg.take("TMP", [P, 2, TOK])
        full = reg.take("FULL", [P, 2, TOK])
        rstd = reg.take("RSTD", [P, TOK])
        C = prog.C
        spans = [(0, LAT, CLAT), (LAT, TOK, CCTX)]
        mean, var = prog.PS[:, 0, 0:TOK], prog.PS[:, 1, 0:TOK]
        summed, centred, squared, sq_summed = prog.sem("summed"), prog.sem("centred"), prog.sem("squared"), prog.sem("sqs")
        root, rstd_done, normed, act_full = prog.sem("root"), prog.sem("rstd"), prog.sem("normed"), prog.sem("full")
        hi, lo = prog.sem("hi"), prog.sem("lo")

        @block.tensor
        def _(pe):
            for k in range(KD):
                for a, b, at in spans:
                    last = pe.matmul(mean[:, a:b], prog.ONES[:], C[:, k, at:at + b - a], start=(k == 0), stop=(k == KD - 1))
            last.then_inc(summed, 1)
            for k in range(KD):
                pe.wait_ge(squared, k + 1)
                for a, b in BOTH:
                    last = pe.matmul(var[:, a:b], prog.ONES[:], tmp[:, k % 2, a:b], start=(k == 0), stop=(k == KD - 1))
                last.then_inc(sq_summed, 1)

        @block.scalar
        def _(act):
            for k in range(KD):
                act.wait_ge(centred, k + 1)
                if k >= 2:
                    act.wait_ge(sq_summed, k - 1)
                for a, b, at in spans:
                    ins = act.activation(tmp[:, k % 2, a:b], C[:, k, at:at + b - a], ACT.Square)
                ins.then_inc(squared, 1)
            act.wait_ge(sq_summed, KD)
            act.activation(rstd[:], var, ACT.Sqrt, bias=prog.EPSC[:, 0:1]).then_inc(root, 1)
            for k in range(KD):
                act.wait_ge(normed, k + 1)
                if k >= 2:
                    act.wait_ge(lo, k - 1)
                act.activation(full[:, k % 2, :], tmp[:, k % 2, :], ACT.Silu, bias=prog.prm("ln_b", k),
                               scale=prog.prm("ln_g", k)).then_inc(act_full, 1)
                act.wait_ge(act_full, k + 1)
                act.activation(prog.XNH[:, k, :], full[:, k % 2, :], ACT.Copy).then_inc(hi, 1)

        @block.vector
        def _(dve):
            dve.wait_ge(summed, 1)
            for k in range(KD):
                for a, b, at in spans:
                    ins = dve.tensor_tensor(C[:, k, at:at + b - a], C[:, k, at:at + b - a], mean[:, a:b], ALU.subtract)
                ins.then_inc(centred, 1)
            dve.wait_ge(root, 1)
            dve.reciprocal(rstd[:], rstd[:]).then_inc(rstd_done, 1)
            dve.wait_ge(rstd_done, 1)
            for k in range(KD + 1):
                if k < KD:
                    if k >= 2:
                        dve.wait_ge(act_full, k - 1)
                    for a, b, at in spans:
                        ins = dve.tensor_tensor(tmp[:, k % 2, a:b], C[:, k, at:at + b - a], rstd[:, a:b], ALU.mult)
                    ins.then_inc(normed, 1)
                if k >= 1:
                    dve.wait_ge(hi, k)
                    dve.tensor_tensor(prog.XNL[:, k - 1, :], full[:, (k - 1) % 2, :], f32(prog.XNH[:, k - 1, :]),
                                      ALU.subtract).then_inc(lo, 1)


def project(prog, g, xh, xl, segments, gate=None, bias=None):
    with prog.block(g.name) as block:
        psum_free = prog.sem("psum_free")
        if bias is not None:
            tmp = prog.region(prog.tmp, prog.top).take("SCALED", [P, 2, TOK])
            scaled = prog.sem("scaled")

        @block.sync
        def _(sp):
            run_units(sp, g.n, lambda i, s: load_ahead(prog, sp, g, i, s))

        @block.scalar
        def _(act):
            def step(i, s):
                split_hi_ahead(prog, act, g, i, s)
                if bias is not None:
                    act.wait_ge(prog.unit_done, g.base + 4 * i + s + 1)
                    act.wait_ge(psum_free, 4 * i + s + 3)
                    for t, (a, b) in enumerate(segments):
                        ins = act.activation(tmp[:, s % 2, a:b], prog.PS[:, s, a:b], ACT.Identity,
                                             bias=bias(4 * i + s, t), scale=gate(4 * i + s, t))
                    ins.then_inc(scaled, 1)
            run_units(act, g.n, step)

        @block.vector
        def _(dve):
            def step(i, s):
                split_lo_ahead(prog, dve, g, i, s)
                u = 4 * i + s
                if bias is not None:
                    dve.wait_ge(scaled, u + 1)
                    a, b = segments[0][0], segments[-1][1]
                    dve.tensor_tensor(prog.X[:, u, a:b], tmp[:, s % 2, a:b], prog.X[:, u, a:b], ALU.add).then_inc(psum_free, 1)
                    return
                dve.wait_ge(prog.unit_done, g.base + u + 1)
                for t, (a, b) in enumerate(segments):
                    if gate is None:
                        ins = dve.tensor_tensor(prog.X[:, u, a:b], prog.PS[:, s, a:b], prog.X[:, u, a:b], ALU.add)
                    else:
                        ins = dve.scalar_tensor_tensor(prog.X[:, u, a:b], prog.PS[:, s, a:b], gate(u, t),
                                                       prog.X[:, u, a:b], ALU.mult, ALU.add)
                ins.then_inc(psum_free, 1)
            run_units(dve, g.n, step)

        @block.tensor
        def _(pe):
            pe.nop().then_inc(psum_free, 4)
            run_units(pe, g.n, lambda i, s: multiply(prog, pe, g, i, s, xh, xl, segments, psum_free))


def ffn_up(prog, g, layer, group, segments):
    tok = segments[-1][1]
    with prog.block("up") as block:
        reg = prog.region(prog.arena, prog.tmp)
        HH = prog.HH = reg.take("HH", [P, HID, TOK], F32R)
        HL = prog.HL = reg.take("HL", [P, HID, TOK], F32R)
        Y = prog.region(prog.tmp, prog.top).take("Y", [P, 4, tok])
        psum_free, centre, silu, hidden = prog.sem("psum_free"), prog.sem("centre"), prog.sem("silu"), prog.sem("hidden")
        hid_hi, y_free, tap = prog.sem("hid_hi"), prog.sem("y_free"), prog.sem("tap")

        def coef(i, s, n):
            return prog.prm(f"ffn{layer}", (2 * HID * group + 4 * i + s) * 4 + n)

        @block.sync
        def _(sp):
            run_units(sp, g.n, lambda i, s: load_ahead(prog, sp, g, i, s))

        @block.scalar
        def _(act):
            def step(i, s):
                split_hi_ahead(prog, act, g, i, s)
                u, j = 4 * i + s, 2 * i + s // 2
                act.wait_ge(prog.unit_done, g.base + u + 1)
                act.wait_ge(y_free, j + 1)
                act.activation(Y[:, s, :], prog.PS[:, s, 0:tok], ACT.Identity, bias=coef(i, s, 3),
                               scale=coef(i, s, 1)).then_inc(centre, 1)
                if s % 2 == 1:
                    act.wait_ge(psum_free, 4 + u)
                    act.activation(Y[:, s - 1, :], Y[:, s - 1, :], ACT.Silu).then_inc(silu, 1)
                    act.wait_ge(hidden, j + 1)
                    act.activation(HH[:, j, 0:tok], Y[:, s, :], ACT.Copy).then_inc(hid_hi, 1)
            run_units(act, g.n, step)

        @block.vector
        def _(dve):
            dve.nop().then_inc(y_free, 2)
            dve.nop().then_inc(psum_free, 4)

            def step(i, s):
                split_lo_ahead(prog, dve, g, i, s)
                u, j = 4 * i + s, 2 * i + s // 2
                dve.wait_ge(centre, u + 1)
                for a, b in segments:
                    ins = dve.scalar_tensor_tensor(Y[:, s, a + 1:b], prog.PS[:, s, a:b - 1], coef(i, s, 0),
                                                   Y[:, s, a + 1:b], ALU.mult, ALU.add)
                ins.then_inc(tap, 1)
                dve.wait_ge(tap, u + 1)
                for a, b in segments:
                    ins = dve.scalar_tensor_tensor(Y[:, s, a:b - 1], prog.PS[:, s, a + 1:b], coef(i, s, 2),
                                                   Y[:, s, a:b - 1], ALU.mult, ALU.add)
                ins.then_inc(psum_free, 1)
                if s % 2 == 1:
                    dve.wait_ge(silu, j + 1)
                    dve.wait_ge(psum_free, 4 + u + 1)
                    dve.tensor_tensor(Y[:, s, :], Y[:, s - 1, :], Y[:, s, :], ALU.mult).then_inc(hidden, 1)
                    dve.wait_ge(hid_hi, j + 1)
                    dve.tensor_tensor(HL[:, j, 0:tok], Y[:, s, :], f32(HH[:, j, 0:tok]), ALU.subtract).then_inc(y_free, 1)
            run_units(dve, g.n, step)

        @block.tensor
        def _(pe):
            run_units(pe, g.n, lambda i, s: multiply(prog, pe, g, i, s, prog.XNH, prog.XNL, segments, psum_free))


def collect(prog, g, segments_of, dest_of, chunks_of=lambda u: None, loads=()):
    with prog.block(g.name) as block:
        psum_free, loaded = prog.sem("psum_free"), prog.sem("loaded")

        def shape(ps, u):
            chunks = chunks_of(u)
            if chunks is None:
                a, b = segments_of(u)[0][0], segments_of(u)[-1][1]
                return ps[:, a:b]
            return ps[:, 0:len(chunks) * P].rearrange("p (c m) -> p c m", m=P)

        @block.sync
        def _(sp):
            for to, src in loads:
                sp.dma_start(to, src).then_inc(loaded, 16)
            run_units(sp, g.n, lambda i, s: load_ahead(prog, sp, g, i, s))
            if loads:
                sp.wait_ge(loaded, 16 * len(loads))

        @block.scalar
        def _(act):
            def step(i, s):
                split_hi_ahead(prog, act, g, i, s)
                u = 4 * i + s
                act.wait_ge(prog.unit_done, g.base + u + 1)
                act.activation(dest_of(u), shape(prog.PS[:, s, :], u), ACT.Copy).then_inc(psum_free, 1)
            run_units(act, g.n, step)

        @block.vector
        def _(dve):
            run_units(dve, g.n, lambda i, s: split_lo_ahead(prog, dve, g, i, s))

        @block.tensor
        def _(pe):
            pe.nop().then_inc(psum_free, 4)

            def step(i, s):
                chunks = chunks_of(4 * i + s)
                if chunks is None:
                    multiply(prog, pe, g, i, s, prog.XNH, prog.XNL, segments_of(4 * i + s), psum_free)
                else:
                    multiply_tokens(prog, pe, g, i, s, prog.XNH, prog.XNL, chunks, psum_free)
            run_units(pe, g.n, step)


def window_qkv(prog, g):
    reg = prog.attn = prog.region(prog.arena, prog.top)
    QT = prog.QT = reg.take("QT", [P, KD, LAT])
    KT = prog.KT = reg.take("KT", [P, 2, TOK])
    V = prog.VT = reg.take("VT", [P, TOK // P, KV_HEADS * HEAD_DIM])
    prog.AXIAL = reg.take("AXIAL", [P, 2, LAT])
    prog.MASKS = reg.take("MASKS", [P, 2, BLOCK])
    prog.ROT = reg.take("ROT", [P, P])

    def kind(u):
        return u if isinstance(u, int) and u >= KD else 0

    def dest(u):
        if kind(u) == 0:
            return QT[:, u, :]
        return KT[:, u - KD, :] if u < KD + 2 else V[:, :, (u - KD - 2) * P:(u - KD - 1) * P]

    collect(prog, g, lambda u: BOTH if kind(u) else LATENT, dest,
            lambda u: range(0, TOK, P) if kind(u) >= KD + 2 else None,
            [(prog.AXIAL[:], prog.dram["axial"]), (prog.MASKS[:], prog.dram["masks"]), (prog.ROT[:], prog.dram["rot_head"])])


def window_rope(prog):
    with prog.block("rope") as block:
        reg = prog.region(prog.attn.at_, prog.top)
        part = reg.take("PART", [P, 2, LAT])
        turned = reg.take("TURNED", [P, 2, LAT])
        rotated, cosined, sined, summed = prog.sem("rotated"), prog.sem("cosined"), prog.sem("sined"), prog.sem("summed")
        tiles = [prog.QT[:, k, :] for k in range(KD)] + [prog.KT[:, k, 0:LAT] for k in range(2)]

        @block.tensor
        def _(pe):
            for n, t in enumerate(tiles):
                if n >= 4:
                    pe.wait_ge(sined, n - 3)
                pe.matmul(prog.PS[:, n % 4, 0:LAT], prog.ROT[:], t, start=True, stop=True).then_inc(rotated, 1)

        @block.gpsimd
        def _(pool):
            for n, t in enumerate(tiles):
                if n >= 2:
                    pool.wait_ge(summed, n - 1)
                pool.tensor_tensor(part[:, n % 2, :], t, prog.AXIAL[:, 0, :], ALU.mult).then_inc(cosined, 1)

        @block.vector
        def _(dve):
            for n, t in enumerate(tiles):
                dve.wait_ge(rotated, n + 1)
                if n >= 2:
                    dve.wait_ge(summed, n - 1)
                dve.tensor_tensor(turned[:, n % 2, :], prog.PS[:, n % 4, 0:LAT], prog.AXIAL[:, 1, :],
                                  ALU.mult).then_inc(sined, 1)
                dve.wait_ge(cosined, n + 1)
                dve.wait_ge(sined, n + 1)
                dve.tensor_tensor(t, part[:, n % 2, :], turned[:, n % 2, :], ALU.add).then_inc(summed, 1)


def window_attention(prog):
    with prog.block("attn") as block:
        reg = prog.region(prog.attn.at_, prog.top)
        QS = reg.take("QS", [P, LAT])
        probs = reg.take("PROBS", [P, 2, 640])
        probsT = reg.take("PROBST", [P, 2, 640])
        stats = reg.take("STATS", [P, 2, 8])
        nsink = reg.take("NSINK", [P, HEADS])
        scale = HEAD_DIM ** -0.5
        NB = LAT // BLOCK
        UNITS = 2 * NB
        PS = prog.PS
        staged, scored, bias_ready, exped = prog.sem("staged"), prog.sem("scored"), prog.sem("bias"), prog.sem("exped")
        sunk, normed, turned, copied = prog.sem("sunk"), prog.sem("normed"), prog.sem("turned"), prog.sem("copied")
        attended, out_hi, out_free, step = prog.sem("attended"), prog.sem("out_hi"), prog.sem("out_free"), prog.sem("step")

        def keys(b):
            return [kb for kb in (b - 1, b, b + 1) if 0 <= kb < NB]

        def width(n):
            return CTX + BLOCK * len(keys(n % NB))

        def each_tile(eng, body):
            for p in range(2):
                with eng.Fori(0, NB) as j:
                    body(p, j, NB * p + j)

        @block.gpsimd
        def _(pool):
            def body(p, j, t):
                pool.wait_ge(attended, t + 1)
                pool.tensor_copy(QS[:], prog.QT[:, t, :]).then_inc(staged, 1)
            each_tile(pool, body)

        @block.tensor
        def _(pe):
            pe.nop().then_inc(attended, 1)
            pe.nop().then_inc(exped, 2)
            pe.nop().then_inc(copied, 1)
            pe.nop().then_inc(out_free, 1)
            pe.nop().then_inc(turned, 2)

            def scores(p, t, n):
                half, b = n // NB, n % NB
                q = QS[64 * half:64 * half + 64, b * BLOCK:(b + 1) * BLOCK]
                k = prog.KT[64 * half:64 * half + 64, p, :]
                S = PS[:, n % 2, :]
                kb = keys(b)
                pe.wait_ge(exped, UNITS * t + n + 1)
                pe.matmul(S[:, 0:CTX], q, k[:, LAT:TOK], start=True, stop=True)
                near = kb[:2]
                pe.matmul(S[:, CTX:CTX + 2 * BLOCK], q, k[:, near[0] * BLOCK:(near[0] + 2) * BLOCK], start=True, stop=False)
                m = 0 if near[0] < b else 1
                last = pe.matmul(S[:, CTX + m * BLOCK:CTX + (m + 1) * BLOCK], prog.IDENT[:], prog.MASKS[:, m, :],
                                 start=False, stop=True)
                if len(kb) == 3:
                    pe.matmul(S[:, 512:640], q, k[:, kb[2] * BLOCK:(kb[2] + 1) * BLOCK], start=True, stop=False)
                    last = pe.matmul(S[:, 512:640], prog.IDENT[:], prog.MASKS[:, 1, :], start=False, stop=True)
                last.then_inc(scored, 1)
                return last

            def transposes(t, n):
                pe.wait_ge(normed, UNITS * t + n + 1)
                pe.wait_ge(copied, UNITS * t + n + 1)
                for c in range(width(n) // P):
                    last = pe.transpose(PS[:, 2, c * P:(c + 1) * P], probs[:, n % 2, c * P:(c + 1) * P], prog.IDENT[:])
                last.then_inc(turned, 1)

            def values(p, t, n):
                half, b = n // NB, n % NB
                chunks = [NB, NB + 1] + keys(b)
                g = 2 * p + half
                if n == 0:
                    pe.wait_ge(out_free, t + 1)
                pe.wait_ge(copied, 1 + UNITS * t + n + 1)
                for c, v in enumerate(chunks):
                    last = pe.matmul(PS[64 * half:64 * half + 64, 3, b * BLOCK:(b + 1) * BLOCK],
                                     prog.VT[:, v, g * HEAD_DIM:(g + 1) * HEAD_DIM], probsT[:, n % 2, c * P:(c + 1) * P],
                                     start=(c == 0), stop=(c == len(chunks) - 1))
                return last

            def body(p, j, t):
                pe.wait_ge(staged, t + 1)
                scores(p, t, 0)
                for n in range(UNITS):
                    if n + 1 < UNITS:
                        last = scores(p, t, n + 1)
                    transposes(t, n)
                    last = values(p, t, n)
                last.then_inc(attended, 1)
            each_tile(pe, body)

        @block.vector
        def _(dve):
            steps = Steps(dve, step, 3 * UNITS)
            dve.tensor_scalar(nsink[:], prog.prm("sink", 0, HEADS), -1.0, None, ALU.mult).then_inc(sunk, 1)
            dve.wait_ge(sunk, 1)

            def maxima(t, n):
                dve.wait_ge(scored, UNITS * t + n + 1)
                st = stats[:, n % 2, :]
                steps.did(dve.reduce_max(st[:, 0:1], PS[:, n % 2, 0:width(n)], AX.X))
                steps.wait()
                dve.tensor_scalar(st[:, 1:2], st[:, 0:1], -scale, nsink[:, bass.ds(2 * t + n // NB, 1)], ALU.mult,
                                  ALU.min).then_inc(bias_ready, 1)

            def normalise(t, n):
                st = stats[:, n % 2, :]
                dve.wait_ge(exped, 2 + UNITS * t + n + 1)
                dve.wait_ge(sunk, 1 + UNITS * t + n + 1)
                steps.did(dve.tensor_tensor(st[:, 4:5], st[:, 2:3], st[:, 3:4], ALU.add))
                steps.wait()
                steps.did(dve.reciprocal(st[:, 5:6], st[:, 4:5]))
                steps.wait()
                dve.tensor_scalar(probs[:, n % 2, 0:width(n)], probs[:, n % 2, 0:width(n)], st[:, 5:6], None,
                                  ALU.mult).then_inc(normed, 1)

            def body(p, j, t):
                steps.round(t)
                maxima(t, 0)
                for n in range(UNITS):
                    if n + 1 < UNITS:
                        maxima(t, n + 1)
                    normalise(t, n)
                assert steps.n == steps.per_round
                dve.wait_ge(out_hi, t + 1)
                dve.tensor_tensor(prog.XNL[:, t, 0:LAT], PS[:, 3, 0:LAT], f32(prog.XNH[:, t, 0:LAT]),
                                  ALU.subtract).then_inc(out_free, 1)
            each_tile(dve, body)

        @block.scalar
        def _(act):
            def exponentials(t, n):
                st = stats[:, n % 2, :]
                act.wait_ge(bias_ready, UNITS * t + n + 1)
                act.wait_ge(turned, UNITS * t + n + 1)
                act.activation(probs[:, n % 2, 0:width(n)], PS[:, n % 2, 0:width(n)], ACT.Exp, bias=st[:, 1:2], scale=scale,
                               accum_out=st[:, 2:3]).then_inc(exped, 1)
                act.activation(st[:, 3:4], st[:, 1:2], ACT.Exp,
                               bias=prog.prm("sink", 2 * t + n // NB)).then_inc(sunk, 1)

            def copy(t, n):
                act.wait_ge(turned, 2 + UNITS * t + n + 1)
                act.activation(probsT[:, n % 2, 0:width(n)], PS[:, 2, 0:width(n)], ACT.Copy).then_inc(copied, 1)

            def body(p, j, t):
                exponentials(t, 0)
                for n in range(UNITS):
                    if n + 1 < UNITS:
                        exponentials(t, n + 1)
                    copy(t, n)
                act.wait_ge(attended, 1 + t + 1)
                act.activation(prog.XNH[:, t, 0:LAT], PS[:, 3, 0:LAT], ACT.Copy).then_inc(out_hi, 1)
            each_tile(act, body)


def rescale(prog, gain, out=None):
    with prog.block("final") as block:
        reg = prog.region(prog.tmp, prog.top)
        sq = reg.take("SQ", [P, 2, LAT])
        rstd = reg.take("RSTD", [P, LAT])
        mean = prog.PS[:, 0, 0:LAT]
        squared, summed, root, scaled = prog.sem("squared"), prog.sem("summed"), prog.sem("root"), prog.sem("scaled")
        loaded, rescaled = prog.sem("loaded"), prog.sem("rescaled")

        @block.sync
        def _(sp):
            if out is None:
                sp.dma_start(prog.X[:, :, LAT:TOK], prog.dram["memT"]).then_inc(loaded, 16)
                sp.wait_ge(loaded, 16)
                return
            for k in range(0, KD, 2):
                sp.wait_ge(rescaled, k + 2)
                sp.dma_start(out[:, k:k + 2, :], prog.X[:, k:k + 2, 0:LAT]).then_inc(loaded, 16)
            sp.wait_ge(loaded, 16 * KD // 2)

        @block.scalar
        def _(act):
            for k in range(KD):
                if k >= 2:
                    act.wait_ge(summed, k - 1)
                act.activation(sq[:, k % 2, :], prog.X[:, k, 0:LAT], ACT.Square).then_inc(squared, 1)
            act.wait_ge(summed, KD)
            act.activation(rstd[:], mean, ACT.Sqrt, bias=prog.EPSC[:, 0:1]).then_inc(root, 1)

        @block.tensor
        def _(pe):
            for k in range(KD):
                pe.wait_ge(squared, k + 1)
                pe.matmul(mean, prog.ONES[:], sq[:, k % 2, :], start=(k == 0), stop=(k == KD - 1)).then_inc(summed, 1)

        @block.vector
        def _(dve):
            dve.wait_ge(root, 1)
            dve.reciprocal(rstd[:], rstd[:]).then_inc(scaled, 1)
            dve.wait_ge(scaled, 1)
            for k in range(KD):
                dve.scalar_tensor_tensor(prog.X[:, k, 0:LAT], prog.X[:, k, 0:LAT], gain[:, k:k + 1], rstd[:], ALU.mult,
                                         ALU.mult).then_inc(rescaled, 1)



MLA_HEADS, NOPE, ROPE, V_DIM = 8, 64, 32, 64
QK = NOPE + ROPE
Q_RANK, KV_RANK = 384, 256
MLA_PAIR = 2 * (Q_RANK // P * QK + KV_RANK // P * (QK + V_DIM))
MEM_HEADS, MEM_DIM = 4, 256
EXPERTS, CAPACITY = 16, 64
TWO_PI = (6.28125, 0.0019350051879882812, float(2 * np.pi - 6.28125 - 0.0019350051879882812))
SIN_LIMIT = 3.1415925


def mixing_input(prog, g):
    reg = prog.mix = prog.region(prog.arena, prog.top)
    UT = prog.UT = reg.take("UT", [P, g.n, LAT])
    prog.KRR = reg.take("KRR", [P, LAT])
    prog.COS = reg.take("COS", [P, LAT])
    prog.SIN = reg.take("SIN", [P, LAT])
    prog.ROT_ROPE = reg.take("ROTROPE", [P, QK])
    prog.mix_end = reg.at_
    prog.POS = reg.take("POS", [P, LAT], I32)
    prog.GROUP_DFT = reg.take("GROUPDFT", [P, 2, P])
    prog.WF = reg.take("WF", [P, 4, P])
    prog.DFT = reg.take("DFT", [P, LAT // P, 2, LAT])
    prog.fourier_at = reg.at_
    collect(prog, g, lambda u: LATENT, lambda u: UT[:, u, :], loads=[
        (prog.ROT_ROPE[0:QK, :], prog.dram["rot_rope"]), (prog.POS[0:QK, :], prog.dram["positions"]),
        (prog.GROUP_DFT[:], prog.dram["group_dft"]), (prog.WF[:], prog.dram["w_fourier"]),
        (prog.DFT[:], prog.dram["dft"])])


def fourier(prog):
    with prog.block("fourier") as block:
        reg = prog.region(prog.fourier_at, prog.top)
        M = reg.take("M", [P, 4, 2, P])
        PT = reg.take("PT", [P, LAT // P, 4, 2, P])
        PS = prog.PS
        mixed, m_kept = prog.sem("mixed"), prog.sem("m_kept")
        projected, p_kept = prog.sem("projected"), prog.sem("p_kept")
        summed, hi, lo = prog.sem("summed"), prog.sem("hi"), prog.sem("lo")
        slots = [1, 2, 3, 0]

        @block.tensor
        def _(pe):
            for c in range(4):
                for n in range(2):
                    last = pe.matmul(PS[:, 0, (2 * c + n) * P:(2 * c + n + 1) * P], prog.GROUP_DFT[:, n, :],
                                     prog.WF[:, c, :], start=True, stop=True)
            last.then_inc(mixed, 1)
            pe.wait_ge(m_kept, 1)
            for t in range(LAT // P):
                for c in range(4):
                    last = pe.matmul(PS[:, slots[t], c * 2 * P:(c + 1) * 2 * P], prog.UT[:, c, t * P:(t + 1) * P],
                                     M[:, c, :, :].rearrange("p a b -> p (a b)"), start=True, stop=True)
                last.then_inc(projected, 1)
            for c in range(4):
                pe.wait_ge(p_kept, LAT // P)
                for t in range(LAT // P):
                    for n in range(2):
                        last = pe.matmul(PS[:, c, 0:LAT], PT[:, t, c, n, :], prog.DFT[:, t, n, :],
                                         start=(t == 0 and n == 0), stop=(t == LAT // P - 1 and n == 1))
                last.then_inc(summed, 1)

        @block.scalar
        def _(act):
            act.wait_ge(mixed, 1)
            act.activation(M[:].rearrange("p a b c -> p (a b c)"), PS[:, 0, :], ACT.Copy).then_inc(m_kept, 1)
            for t in range(LAT // P):
                act.wait_ge(projected, t + 1)
                act.activation(PT[:, t, :, :, :].rearrange("p a b c -> p (a b c)"), PS[:, slots[t], :],
                               ACT.Copy).then_inc(p_kept, 1)
            for c in range(4):
                act.wait_ge(summed, c + 1)
                act.activation(prog.XNH[:, c, 0:LAT], PS[:, c, 0:LAT], ACT.Copy).then_inc(hi, 1)

        @block.vector
        def _(dve):
            for c in range(4):
                dve.wait_ge(hi, c + 1)
                dve.tensor_tensor(prog.XNL[:, c, 0:LAT], PS[:, c, 0:LAT], f32(prog.XNH[:, c, 0:LAT]),
                                  ALU.subtract).then_inc(lo, 1)


def latents(prog):
    with prog.block("latents") as block:
        reg = prog.region(prog.fourier_at, prog.top)
        sq = reg.take("SQ", [P, 5, LAT])
        rstd = reg.take("RSTD", [P, 2, LAT])
        ang = reg.take("ANG", [P, LAT])
        turns = reg.take("TURNS", [P, LAT])
        whole = reg.take("WHOLE", [P, LAT], I32)
        wrap = reg.take("WRAP", [P, 2, LAT])
        arg = reg.take("ARG", [P, 2, LAT])
        U, PS = prog.UT, prog.PS
        squared, summed, root, done = prog.sem("squared"), prog.sem("summed"), prog.sem("root"), prog.sem("done")
        args_ready, tables, turned = prog.sem("args"), prog.sem("tables"), prog.sem("turned")
        parts = [(0, 3, Q_RANK, "g_q"), (3, 5, KV_RANK, "g_kv")]
        r = slice(0, QK)

        @block.scalar
        def _(act):
            act.activation(sq[:], U[:, 4:9, :], ACT.Square).then_inc(squared, 1)
            act.wait_ge(summed, 1)
            for n, (a, b, rank, _) in enumerate(parts):
                ins = act.activation(rstd[:, n, :], PS[:, n, 0:LAT], ACT.Sqrt, bias=prog.EPSC[:, 0:1], scale=D / rank)
            ins.then_inc(root, 1)
            act.wait_ge(args_ready, 1)
            act.activation(prog.SIN[r, :], arg[r, 0, :], ACT.Sin)
            act.activation(prog.COS[r, :], arg[r, 1, :], ACT.Sin).then_inc(tables, 1)

        @block.tensor
        def _(pe):
            pe.wait_ge(squared, 1)
            for n, (a, b, _, _) in enumerate(parts):
                for k in range(a, b):
                    last = pe.matmul(PS[:, n, 0:LAT], prog.ONES[:], sq[:, k, :], start=(k == a), stop=(k == b - 1))
            last.then_inc(summed, 1)
            pe.matmul(PS[r, 2, 0:LAT], prog.ROT_ROPE[r, :], U[r, 9, :], start=True, stop=True).then_inc(turned, 1)

        @block.vector
        def _(dve):
            step = Steps(dve, done)

            def then(instruction):
                step.did(instruction)
                step.wait()
            then(dve.tensor_copy(turns[r, :], prog.POS[r, :]))
            then(dve.tensor_scalar(ang[r, :], turns[r, :], prog.prm("freq")[r, :], None, ALU.mult))
            then(dve.tensor_scalar(whole[r, :], ang[r, :], 1 / (2 * math.pi), None, ALU.mult))
            then(dve.tensor_copy(turns[r, :], whole[r, :]))
            for part in TWO_PI:
                then(dve.scalar_tensor_tensor(ang[r, :], turns[r, :], -part, ang[r, :], ALU.mult, ALU.add))
            dve.tensor_copy(arg[r, 0, :], ang[r, :])
            then(dve.tensor_scalar(arg[r, 1, :], ang[r, :], math.pi / 2, None, ALU.add))
            for compare, by in ((ALU.is_gt, -2 * math.pi), (ALU.is_lt, 2 * math.pi)):
                then(dve.tensor_scalar(wrap[r, :, :], arg[r, :, :], math.pi if by < 0 else -math.pi, by, compare, ALU.mult))
                then(dve.tensor_tensor(arg[r, :, :], arg[r, :, :], wrap[r, :, :], ALU.add))
            dve.tensor_scalar(arg[r, :, :], arg[r, :, :], SIN_LIMIT, -SIN_LIMIT, ALU.min, ALU.max).then_inc(args_ready, 1)
            dve.wait_ge(root, 1)
            then(dve.reciprocal(rstd[:], rstd[:]))
            for n, (a, b, _, gain) in enumerate(parts):
                for k in range(a, b):
                    dve.scalar_tensor_tensor(U[:, 4 + k, :], U[:, 4 + k, :], prog.prm(gain, k - a), rstd[:, n, :],
                                             ALU.mult, ALU.mult)
            dve.wait_ge(tables, 1)
            dve.wait_ge(turned, 1)
            step.did(dve.tensor_tensor(turns[r, :], PS[r, 2, 0:LAT], prog.SIN[r, :], ALU.mult))
            then(dve.tensor_tensor(ang[r, :], U[r, 9, :], prog.COS[r, :], ALU.mult))
            then(dve.tensor_tensor(prog.KRR[r, :], turns[r, :], ang[r, :], ALU.add))


def latent_attention(prog):
    with prog.block("mla") as block:
        reg = prog.region(prog.mix_end, prog.top)
        W = reg.take("W", [P, MLA_PAIR])
        nq, nkv = Q_RANK // P, KV_RANK // P
        WQ = W[:, 0:nq * 2 * QK].rearrange("p (k m) -> p k m", m=2 * QK)
        WK = W[:, nq * 2 * QK:(nq + nkv) * 2 * QK].rearrange("p (k m) -> p k m", m=2 * QK)
        WV = W[:, (nq + nkv) * 2 * QK:].rearrange("p (k m) -> p k m", m=2 * V_DIM)
        QS, QC, QR, KS, TS = (reg.take(n, [P, 2, LAT]) for n in ("QS", "QC", "QR", "KS", "TS"))
        VS = reg.take("VS", [P, LAT // P, 2 * V_DIM])
        probs, probsT = reg.take("PROBS", [P, 2, LAT]), reg.take("PROBST", [P, 2, LAT])
        stats = reg.take("STATS", [P, 2, 8])
        scale = QK ** -0.5
        NB = LAT // BLOCK
        UNITS, PAIRS = 2 * NB, MLA_HEADS // 2
        U, PS = prog.UT, prog.PS
        r = slice(0, QK)
        w_landed, q_made, k_made, v_made = (prog.sem(n) for n in ("w_landed", "q_made", "k_made", "v_made"))
        q_kept, k_kept, v_kept, rotated = (prog.sem(n) for n in ("q_kept", "k_kept", "v_kept", "rotated"))
        cosined, sined, roped = prog.sem("cosined"), prog.sem("sined"), prog.sem("roped")
        scored, bias_ready, exped, normed = (prog.sem(n) for n in ("scored", "bias", "exped", "normed"))
        turned, copied, attended = prog.sem("turned"), prog.sem("copied"), prog.sem("attended")
        out_hi, out_free, step = prog.sem("out_hi"), prog.sem("out_free"), prog.sem("step")

        def two(slot):
            return PS[r, slot, :].rearrange("p (h t) -> p h t", h=2)

        @block.sync
        def _(sp):
            sp.dma_start(W[:], prog.dram["mla"][0]).then_inc(w_landed, 16)
            with sp.Fori(1, PAIRS) as p:
                sp.wait_ge(v_made, p)
                sp.dma_start(W[:], prog.dram["mla"][p]).then_inc(w_landed, 16)

        @block.gpsimd
        def _(pool):
            with pool.Fori(0, PAIRS) as p:
                pool.wait_ge(q_kept, p + 1)
                pool.wait_ge(roped, p + 1)
                pool.tensor_tensor(QC[r, :, :], QS[r, :, :], prog.COS[r, :].unsqueeze(1).to_broadcast([QK, 2, LAT]),
                                   ALU.mult).then_inc(cosined, 1)

        @block.tensor
        def _(pe):
            pe.nop().then_inc(exped, 2)
            pe.nop().then_inc(copied, 1)
            pe.nop().then_inc(out_free, 1)
            pe.nop().then_inc(turned, 2)

            def scores(p, n):
                h, b = n // NB, n % NB
                pe.wait_ge(exped, UNITS * p + n + 1)
                pe.matmul(PS[:, n % 2, 0:LAT], QR[r, h, b * BLOCK:(b + 1) * BLOCK], KS[r, h, :], start=True,
                          stop=True).then_inc(scored, 1)

            def transposes(p, n):
                pe.wait_ge(normed, UNITS * p + n + 1)
                pe.wait_ge(copied, UNITS * p + n + 1)
                for c in range(LAT // P):
                    last = pe.transpose(PS[:, 2, c * P:(c + 1) * P], probs[:, n % 2, c * P:(c + 1) * P], prog.IDENT[:])
                last.then_inc(turned, 1)

            def values(p, n):
                h, b = n // NB, n % NB
                pe.wait_ge(copied, 1 + UNITS * p + n + 1)
                for c in range(LAT // P):
                    last = pe.matmul(PS[64 * h:64 * h + 64, 3, b * BLOCK:(b + 1) * BLOCK], VS[:, c, h * V_DIM:(h + 1) * V_DIM],
                                     probsT[:, n % 2, c * P:(c + 1) * P], start=(c == 0), stop=(c == LAT // P - 1))
                return last

            with pe.Fori(0, PAIRS) as p:
                pe.wait_ge(w_landed, 16 * p + 16)
                pe.wait_ge(exped, 2 + UNITS * p)
                pe.wait_ge(copied, 1 + UNITS * p)
                for h in range(2):
                    for k in range(nq):
                        last = pe.matmul(two(0)[:, h, :], WQ[:, k, h * QK:(h + 1) * QK], U[:, 4 + k, :], start=(k == 0),
                                         stop=(k == nq - 1))
                last.then_inc(q_made, 1)
                for h in range(2):
                    for k in range(nkv):
                        last = pe.matmul(two(1)[:, h, :], WK[:, k, h * QK:(h + 1) * QK], U[:, 7 + k, :], start=(k == 0),
                                         stop=(k == nkv - 1))
                last.then_inc(k_made, 1)
                for t in range(LAT // P):
                    for k in range(nkv):
                        last = pe.matmul(PS[:, 2, t * P:(t + 1) * P], U[:, 7 + k, t * P:(t + 1) * P], WV[:, k, :],
                                         start=(k == 0), stop=(k == nkv - 1))
                last.then_inc(v_made, 1)
                pe.wait_ge(q_kept, p + 1)
                pe.wait_ge(out_free, p + 1)
                for h in range(2):
                    last = pe.matmul(two(3)[:, h, :], prog.ROT_ROPE[r, :], QS[r, h, :], start=True, stop=True)
                last.then_inc(rotated, 1)
                pe.wait_ge(roped, 1 + p + 1)
                pe.wait_ge(k_kept, p + 1)
                pe.wait_ge(v_kept, p + 1)
                scores(p, 0)
                for n in range(UNITS):
                    if n + 1 < UNITS:
                        scores(p, n + 1)
                    transposes(p, n)
                    last = values(p, n)
                last.then_inc(attended, 1)

        @block.vector
        def _(dve):
            steps = Steps(dve, step, 2 * UNITS)
            dve.nop().then_inc(roped, 1)

            def maxima(p, n):
                dve.wait_ge(scored, UNITS * p + n + 1)
                st = stats[:, n % 2, :]
                steps.did(dve.reduce_max(st[:, 0:1], PS[:, n % 2, 0:LAT], AX.X))
                steps.wait()
                dve.wait_ge(exped, UNITS * p + n + 1)
                dve.tensor_scalar(st[:, 1:2], st[:, 0:1], -scale, None, ALU.mult).then_inc(bias_ready, 1)

            def normalise(p, n):
                st = stats[:, n % 2, :]
                dve.wait_ge(exped, 2 + UNITS * p + n + 1)
                steps.did(dve.reciprocal(st[:, 3:4], st[:, 2:3]))
                steps.wait()
                dve.tensor_scalar(probs[:, n % 2, :], probs[:, n % 2, :], st[:, 3:4], None, ALU.mult).then_inc(normed, 1)

            with dve.Fori(0, PAIRS) as p:
                steps.round(p)
                dve.wait_ge(k_made, p + 1)
                dve.tensor_tensor(KS[r, :, :], two(1), prog.KRR[r, :].unsqueeze(1).to_broadcast([QK, 2, LAT]),
                                  ALU.add).then_inc(k_kept, 1)
                dve.wait_ge(rotated, p + 1)
                dve.tensor_tensor(TS[r, :, :], two(3), prog.SIN[r, :].unsqueeze(1).to_broadcast([QK, 2, LAT]),
                                  ALU.mult).then_inc(sined, 1)
                dve.wait_ge(sined, p + 1)
                dve.wait_ge(cosined, p + 1)
                dve.tensor_tensor(QR[r, :, :], TS[r, :, :], QC[r, :, :], ALU.add).then_inc(roped, 1)
                maxima(p, 0)
                for n in range(UNITS):
                    if n + 1 < UNITS:
                        maxima(p, n + 1)
                    normalise(p, n)
                assert steps.n == steps.per_round
                dve.wait_ge(out_hi, p + 1)
                dve.tensor_tensor(prog.XNL[:, 4 + p, 0:LAT], PS[:, 3, 0:LAT], f32(prog.XNH[:, 4 + p, 0:LAT]),
                                  ALU.subtract).then_inc(out_free, 1)

        @block.scalar
        def _(act):
            def exponentials(p, n):
                st = stats[:, n % 2, :]
                act.wait_ge(bias_ready, UNITS * p + n + 1)
                act.wait_ge(turned, UNITS * p + n + 1)
                act.activation(probs[:, n % 2, :], PS[:, n % 2, 0:LAT], ACT.Exp, bias=st[:, 1:2], scale=scale,
                               accum_out=st[:, 2:3]).then_inc(exped, 1)

            def copy(p, n):
                act.wait_ge(turned, 2 + UNITS * p + n + 1)
                act.activation(probsT[:, n % 2, :], PS[:, 2, 0:LAT], ACT.Copy).then_inc(copied, 1)

            with act.Fori(0, PAIRS) as p:
                act.wait_ge(q_made, p + 1)
                act.wait_ge(roped, p + 1)
                act.activation(QS[r, :, :], two(0), ACT.Copy).then_inc(q_kept, 1)
                act.wait_ge(v_made, p + 1)
                act.activation(VS[:].rearrange("p a b -> p (a b)"), PS[:, 2, 0:LAT], ACT.Copy).then_inc(v_kept, 1)
                exponentials(p, 0)
                for n in range(UNITS):
                    if n + 1 < UNITS:
                        exponentials(p, n + 1)
                    copy(p, n)
                act.wait_ge(attended, p + 1)
                act.activation(prog.XNH[:, 4 + p, 0:LAT], PS[:, 3, 0:LAT], ACT.Copy).then_inc(out_hi, 1)


def memory_attention(prog):
    with prog.block("mem") as block:
        reg = prog.region(prog.memory_at, prog.top)
        QS = reg.take("QS", [P, 2, LAT])
        VS = reg.take("VS", [P, 2, MEM_DIM])
        probs, probsT = reg.take("PROBS", [P, 2, CTX]), reg.take("PROBST", [P, 2, CTX])
        stats = reg.take("STATS", [P, 2, 8])
        scale = MEM_DIM ** -0.5
        NB = LAT // BLOCK
        PS = prog.PS
        staged, scored, bias_ready, exped, normed = (prog.sem(n) for n in ("staged", "scored", "bias", "exped", "normed"))
        turned, copied, attended = prog.sem("turned"), prog.sem("copied"), prog.sem("attended")
        out_hi, out_free, step = prog.sem("out_hi"), prog.sem("out_free"), prog.sem("step")
        out = PS[:, 3, :].rearrange("p (d t) -> p d t", d=2)

        @block.gpsimd
        def _(pool):
            with pool.Fori(0, MEM_HEADS) as h:
                pool.wait_ge(attended, h + 1)
                pool.tensor_copy(QS[:], prog.QM[:, bass.ds(2 * h, 2), :])
                pool.tensor_copy(VS[:], prog.VM[:, :, bass.ds(MEM_DIM * h, MEM_DIM)]).then_inc(staged, 1)

        @block.tensor
        def _(pe):
            pe.nop().then_inc(attended, 1)
            pe.nop().then_inc(exped, 2)
            pe.nop().then_inc(copied, 1)
            pe.nop().then_inc(out_free, 1)
            pe.nop().then_inc(turned, 2)

            def scores(h, b):
                pe.wait_ge(exped, NB * h + b + 1)
                for d in range(2):
                    last = pe.matmul(PS[:, b % 2, 0:CTX], QS[:, d, b * BLOCK:(b + 1) * BLOCK], prog.KM[:, 2 * h + d, :],
                                     start=(d == 0), stop=(d == 1))
                last.then_inc(scored, 1)

            def transposes(h, b):
                pe.wait_ge(normed, NB * h + b + 1)
                pe.wait_ge(copied, NB * h + b + 1)
                for c in range(CTX // P):
                    last = pe.transpose(PS[:, 2, c * P:(c + 1) * P], probs[:, b % 2, c * P:(c + 1) * P], prog.IDENT[:])
                last.then_inc(turned, 1)

            def values(h, b):
                if b == 0:
                    pe.wait_ge(out_free, h + 1)
                pe.wait_ge(copied, 1 + NB * h + b + 1)
                for d in range(2):
                    for c in range(CTX // P):
                        last = pe.matmul(out[:, d, b * BLOCK:(b + 1) * BLOCK], VS[:, c, d * P:(d + 1) * P],
                                         probsT[:, b % 2, c * P:(c + 1) * P], start=(c == 0), stop=(c == CTX // P - 1))
                return last

            with pe.Fori(0, MEM_HEADS) as h:
                pe.wait_ge(staged, h + 1)
                scores(h, 0)
                for b in range(NB):
                    if b + 1 < NB:
                        scores(h, b + 1)
                    transposes(h, b)
                    last = values(h, b)
                last.then_inc(attended, 1)

        @block.vector
        def _(dve):
            steps = Steps(dve, step, 2 * NB)

            def maxima(h, b):
                dve.wait_ge(scored, NB * h + b + 1)
                st = stats[:, b % 2, :]
                steps.did(dve.reduce_max(st[:, 0:1], PS[:, b % 2, 0:CTX], AX.X))
                steps.wait()
                dve.wait_ge(exped, NB * h + b + 1)
                dve.tensor_scalar(st[:, 1:2], st[:, 0:1], -scale, None, ALU.mult).then_inc(bias_ready, 1)

            def normalise(h, b):
                st = stats[:, b % 2, :]
                dve.wait_ge(exped, 2 + NB * h + b + 1)
                steps.did(dve.reciprocal(st[:, 3:4], st[:, 2:3]))
                steps.wait()
                dve.tensor_scalar(probs[:, b % 2, :], probs[:, b % 2, :], st[:, 3:4], None, ALU.mult).then_inc(normed, 1)

            with dve.Fori(0, MEM_HEADS) as h:
                steps.round(h)
                maxima(h, 0)
                for b in range(NB):
                    if b + 1 < NB:
                        maxima(h, b + 1)
                    normalise(h, b)
                assert steps.n == steps.per_round
                dve.wait_ge(out_hi, h + 1)
                dve.tensor_tensor(prog.XNL[:, bass.ds(2 * h, 2), 0:LAT], out, f32(prog.XNH[:, bass.ds(2 * h, 2), 0:LAT]),
                                  ALU.subtract).then_inc(out_free, 1)

        @block.scalar
        def _(act):
            def exponentials(h, b):
                st = stats[:, b % 2, :]
                act.wait_ge(bias_ready, NB * h + b + 1)
                act.wait_ge(turned, NB * h + b + 1)
                act.activation(probs[:, b % 2, :], PS[:, b % 2, 0:CTX], ACT.Exp, bias=st[:, 1:2], scale=scale,
                               accum_out=st[:, 2:3]).then_inc(exped, 1)

            def copy(h, b):
                act.wait_ge(turned, 2 + NB * h + b + 1)
                act.activation(probsT[:, b % 2, :], PS[:, 2, 0:CTX], ACT.Copy).then_inc(copied, 1)

            with act.Fori(0, MEM_HEADS) as h:
                exponentials(h, 0)
                for b in range(NB):
                    if b + 1 < NB:
                        exponentials(h, b + 1)
                    copy(h, b)
                act.wait_ge(attended, 1 + h + 1)
                act.activation(prog.XNH[:, bass.ds(2 * h, 2), 0:LAT], out, ACT.Copy).then_inc(out_hi, 1)


def memory_inputs(prog, gemms):
    reg = prog.region(prog.arena, prog.top)
    QM = prog.QM = reg.take("QM", [P, KD, LAT])
    KM = prog.KM = reg.take("KM", [P, KD, CTX])
    VM = prog.VM = reg.take("VM", [P, CTX // P, D])
    prog.memory_at = reg.at_
    collect(prog, gemms["memq"], lambda u: LATENT, lambda u: QM[:, u, :])
    collect(prog, gemms["memk"], lambda u: CONTEXT, lambda u: KM[:, u, :])
    collect(prog, gemms["memv"], lambda u: CONTEXT, lambda u: VM[:, :, bass.ds(u * P, P)], lambda u: range(LAT, TOK, P))


MOE_UNITS = 12
HALF_K = KD // 2


class Moe:
    def __init__(self, prog):
        at = prog.small_end + 24576
        self.XS = prog.at("XS", [P, EXPERTS, KD, P], F32R, at)
        at += EXPERTS * KD * P * 4
        self.RAW = prog.at("RAWM", [P, RAWS, HALF_K * 512], F32, at)
        at += RAWS * HALF_K * 512 * 4
        self.WHI = prog.at("WHIM", [P, SPLITS, HALF_K * 512], F32R, at)
        self.S = prog.at("SLOTS", [P, LAT // P, EXPERTS * CAPACITY], F32R, at)
        at += SPLITS * HALF_K * 512 * 4
        self.WLO = prog.at("WLOM", [P, SPLITS, HALF_K * 512], F32R, at)
        at += SPLITS * HALF_K * 512 * 4
        self.scratch = at


def router(prog):
    moe = prog.moe = Moe(prog)
    with prog.block("router") as block:
        reg = prog.region(moe.scratch, prog.top)
        NT = LAT // P
        HTH = prog.HTH = reg.take("HTH", [P, NT, D], F32R)
        HTL = prog.HTL = reg.take("HTL", [P, NT, D], F32R)
        prog.SLOT_T = reg.take("SLOTT", [P, NT, EXPERTS])
        prog.IOTA = reg.take("IOTA", [P, CAPACITY])
        R = reg.take("R", [P, KD, EXPERTS])
        RH, RL = reg.take("RH", [P, KD, EXPERTS], F32R), reg.take("RL", [P, KD, EXPERTS], F32R)
        L, stats = reg.take("L", [P, NT, EXPERTS]), reg.take("STATS", [P, 2, NT])
        ROW, WORK = reg.take("ROW", [P, 2, LAT]), reg.take("WORK", [P, LAT])
        SEL, RANK, ZERO = reg.take("SEL", [P, LAT]), reg.take("RANK", [P, LAT]), reg.take("ZERO", [P, LAT])
        TOP = reg.take("TOP", [P, 8])
        loaded, r_hi, r_lo, logits, step = (prog.sem(n) for n in ("loaded", "r_hi", "r_lo", "logits", "step"))
        exped, probs, rows, rows_kept = (prog.sem(n) for n in ("exped", "probs", "rows", "rows_kept"))
        turned, hT_kept, slots, slot_turned, stored = (prog.sem(n) for n in ("turned", "ht", "slots", "sturned", "stored"))
        PS, E = prog.PS, slice(0, EXPERTS)
        halves = [(x, t, h) for t in range(NT) for x in range(2) for h in range(2)]

        @block.sync
        def _(sp):
            sp.dma_start(R[:], prog.dram["router"]).then_inc(loaded, 16)
            sp.dma_start(prog.IOTA[:], prog.dram["iota"]).then_inc(loaded, 16)
            sp.wait_ge(slots, 1)
            sp.dma_start(prog.dram["rows"], ROW[E, :, :]).then_inc(stored, 16)
            sp.wait_ge(stored, 16)

        @block.tensor
        def _(pe):
            pe.wait_ge(r_lo, 1)
            for t in range(NT):
                for k in range(KD):
                    for n, (x, w) in enumerate(((prog.XNH, RH), (prog.XNH, RL), (prog.XNL, RH), (prog.XNL, RL))):
                        last = pe.matmul(PS[:, 0, t * EXPERTS:(t + 1) * EXPERTS], x[:, k, t * P:(t + 1) * P], w[:, k, :],
                                         start=(k == 0 and n == 0), stop=(k == KD - 1 and n == 3))
            last.then_inc(logits, 1)
            pe.wait_ge(probs, 1)
            for t in range(NT):
                last = pe.transpose(PS[E, 1, t * P:(t + 1) * P], L[:, t, :], prog.IDENT[:])
            last.then_inc(rows, 1)
            for n, (x, t, h) in enumerate(halves):
                if n >= 4:
                    pe.wait_ge(hT_kept, n - 3)
                src = (prog.XNH, prog.XNL)[x]
                for k in range(4):
                    at = n % 2 * 512 + k * P
                    last = pe.transpose(PS[:, 2 + n // 2 % 2, at:at + P], f32(src[:, 4 * h + k, t * P:(t + 1) * P]),
                                        prog.IDENT[:])
                last.then_inc(turned, 1)
            pe.wait_ge(slots, 1)
            for t in range(NT):
                last = pe.transpose(PS[:, 0, t * EXPERTS:(t + 1) * EXPERTS], ROW[E, 0, t * P:(t + 1) * P],
                                    prog.IDENT[E, E])
            last.then_inc(slot_turned, 1)

        @block.scalar
        def _(act):
            act.wait_ge(loaded, 32)
            act.activation(RH[:], R[:], ACT.Copy).then_inc(r_hi, 1)
            act.wait_ge(step, 2)
            act.activation(L[:], L[:], ACT.Exp).then_inc(exped, 1)
            act.wait_ge(rows, 1)
            act.activation(ROW[E, 1, :], PS[E, 1, 0:LAT], ACT.Copy).then_inc(rows_kept, 1)
            for n, (x, t, h) in enumerate(halves):
                act.wait_ge(turned, n + 1)
                act.activation((HTH, HTL)[x][:, t, h * 512:(h + 1) * 512], PS[:, 2 + n // 2 % 2, n % 2 * 512:n % 2 * 512 + 512],
                               ACT.Copy).then_inc(hT_kept, 1)
            act.wait_ge(slot_turned, 1)
            act.activation(prog.SLOT_T[:].rearrange("p a b -> p (a b)"), PS[:, 0, 0:NT * EXPERTS], ACT.Copy)

        @block.vector
        def _(dve):
            steps = Steps(dve, step)

            def then(instruction):
                steps.did(instruction)
                steps.wait()
            dve.memset(ZERO[E, :], 0.0)
            dve.wait_ge(r_hi, 1)
            dve.tensor_tensor(RL[:], R[:], f32(RH[:]), ALU.subtract).then_inc(r_lo, 1)
            dve.wait_ge(logits, 1)
            pl = PS[:, 0, 0:NT * EXPERTS].rearrange("p (t e) -> p t e", e=EXPERTS)
            wide = lambda s: s.unsqueeze(2).to_broadcast([P, NT, EXPERTS])
            then(dve.reduce_max(stats[:, 0, :], pl, AX.X))
            then(dve.tensor_tensor(L[:], pl, wide(stats[:, 0, :]), ALU.subtract))
            dve.wait_ge(exped, 1)
            then(dve.reduce_sum(stats[:, 0, :], L[:], AX.X))
            then(dve.reciprocal(stats[:, 1, :], stats[:, 0, :]))
            dve.tensor_tensor(L[:], L[:], wide(stats[:, 1, :]), ALU.mult).then_inc(probs, 1)
            dve.wait_ge(rows_kept, 1)
            then(dve.tensor_copy(WORK[E, :], ROW[E, 1, :]))
            for _ in range(CAPACITY // 8):
                then(dve.max(TOP[E, :], WORK[E, :]))
                then(dve.match_replace(WORK[E, :], TOP[E, :], WORK[E, :], -1.0))
            then(dve.tensor_scalar(SEL[E, :], WORK[E, :], 0.0, None, ALU.is_lt))
            then(dve.tensor_tensor_scan(RANK[E, :], SEL[E, :], ZERO[E, :], 0.0, ALU.add, ALU.add))
            dve.tensor_tensor(ROW[E, 0, :], RANK[E, :], SEL[E, :], ALU.mult).then_inc(slots, 1)


def gather(prog):
    moe = prog.moe
    with prog.block("gather") as block:
        NT = LAT // P
        hot, gathered = prog.sem("hot"), prog.sem("gathered")
        kept = [prog.sem("kept_by_act"), prog.sem("kept_by_dve")]
        work = [(k, x) for k in range(KD) for x in range(2)]

        @block.vector
        def _(dve):
            for t in range(NT):
                dve.tensor_tensor(moe.S[:, t, :].rearrange("p (e s) -> p e s", s=CAPACITY),
                                  prog.IOTA[:].unsqueeze(1).to_broadcast([P, EXPERTS, CAPACITY]),
                                  prog.SLOT_T[:, t, :].unsqueeze(2).to_broadcast([P, EXPERTS, CAPACITY]),
                                  ALU.is_equal).then_inc(hot, 1)
            for n, (k, x) in enumerate(work):
                if n % 2 == 1:
                    dve.wait_ge(gathered, n + 1)
                    dve.tensor_copy(moe.XS[:, :, k, x * 64:(x + 1) * 64],
                                    prog.PS[:, n % 4, :].rearrange("p (e s) -> p e s", s=CAPACITY)).then_inc(kept[1], 1)

        @block.scalar
        def _(act):
            for n, (k, x) in enumerate(work):
                if n % 2 == 0:
                    act.wait_ge(gathered, n + 1)
                    act.activation(moe.XS[:, :, k, x * 64:(x + 1) * 64],
                                   prog.PS[:, n % 4, :].rearrange("p (e s) -> p e s", s=CAPACITY), ACT.Copy).then_inc(kept[0], 1)

        @block.tensor
        def _(pe):
            for n, (k, x) in enumerate(work):
                if n >= 4:
                    pe.wait_ge(kept[n % 2], n // 2 - 1)
                src = (prog.HTH, prog.HTL)[x]
                for t in range(NT):
                    if n == 0:
                        pe.wait_ge(hot, t + 1)
                    for half in range(2):
                        last = pe.matmul(prog.PS[:, n % 4, half * 512:(half + 1) * 512], src[:, t, k * P:(k + 1) * P],
                                         moe.S[:, t, half * 512:(half + 1) * 512], start=(t == 0), stop=(t == NT - 1))
                last.then_inc(gathered, 1)


def experts(prog):
    moe = prog.moe
    with prog.block("moe") as block:
        reg = prog.region(moe.scratch, prog.top)
        ROWS = reg.take("ROWS", [P, 2, LAT])
        XSB = reg.take("XSB", [P, KD, P], F32R)
        HT = reg.take("HT", [P, KD, P], F32R)
        HS = reg.take("HS", [P, KD, CAPACITY])
        SIL = reg.take("SIL", [P, 512])
        AB = reg.take("AB", [P, 2, D])
        YH, YL = reg.take("YH", [P, D], F32R), reg.take("YL", [P, D], F32R)
        ST = reg.take("ST", [P, LAT], F32R)
        prod = reg.take("PROD", [P, LAT])
        gate = reg.take("GATE", [P, 2])
        SUM2 = reg.take("SUM2", [P, CAPACITY])
        RAW, WHI, WLO, XS, PS, X = moe.RAW, moe.WHI, moe.WLO, moe.XS, prog.PS, prog.X
        landed = [prog.sem(f"landed{s}") for s in range(RAWS)]
        w_hi, w_lo, done, staged = (prog.sem(n) for n in ("w_hi", "w_lo", "done", "staged"))
        rows_landed, hot, gated, ab_turned = (prog.sem(n) for n in ("rows_landed", "hot", "gated", "ab_turned"))
        a_kept, b_kept = prog.sem("a_kept"), prog.sem("b_kept")
        silu, hidden, h_hi, h_lo, y_hi, y_lo = (prog.sem(n) for n in ("silu", "hidden", "h_hi", "h_lo", "y_hi", "y_lo"))
        scattered, added, consts = prog.sem("scattered"), prog.sem("added"), prog.sem("consts")
        N, last_e = MOE_UNITS, EXPERTS - 1

        def rounds(eng, body):
            with eng.Fori(0, last_e) as e:
                body(e, False)
            body(last_e, True)

        @block.sync
        def _(sp):
            sp.dma_start(SUM2[:], prog.dram["sum2"]).then_inc(consts, 16)
            for j in range(RAWS):
                sp.dma_start(RAW[:, j, :], prog.dram["experts"][0, j]).then_inc(landed[j], 16)

            def load_rows(e):
                sp.dma_start(ROWS[:], prog.dram["rows"][e].partition_broadcast(P)).then_inc(rows_landed, 16)
            load_rows(0)

            def body(e, last):
                for j in range(N):
                    if last and j + RAWS >= N:
                        continue
                    sp.wait_ge(w_lo, N * e + j + 1)
                    to = (e, j + RAWS) if j + RAWS < N else (e + 1, j + RAWS - N)
                    sp.dma_start(RAW[:, j % RAWS, :], prog.dram["experts"][to[0], to[1]]).then_inc(landed[j % RAWS], 16)
                    if j == 9 and not last:
                        sp.wait_ge(gated, e + 1)
                        load_rows(e + 1)
            rounds(sp, body)

        @block.gpsimd
        def _(pool):
            pool.tensor_copy(XSB[:], XS[:, 0, :, :]).then_inc(staged, 1)
            with pool.Fori(1, EXPERTS) as e:
                pool.wait_ge(done, N * e - N + 8)
                pool.tensor_copy(XSB[:], XS[:, e, :, :]).then_inc(staged, 1)

        @block.tensor
        def _(pe):
            def unit(e, j, x, slot):
                half, kk = j % 4 // 2, j % 2
                pe.wait_ge(w_lo, N * e + j + 1)
                for k in range(HALF_K):
                    for n, w in enumerate((WHI, WLO)):
                        last = pe.matmul(PS[:, slot, half * 512:(half + 1) * 512], x[:, HALF_K * kk + k, :],
                                         w[:, j % SPLITS, k * 512:(k + 1) * 512], start=(kk == 0 and k == 0 and n == 0),
                                         stop=(kk == 1 and k == HALF_K - 1 and n == 1))
                last.then_inc(done, 1)

            def turn(n):
                for k in range(KD):
                    last = pe.matmul(PS[:, 2, n * 512 + k * CAPACITY:n * 512 + (k + 1) * CAPACITY],
                                     AB[:, n, k * P:(k + 1) * P], SUM2[:], start=True, stop=True)
                last.then_inc(ab_turned, 1)

            def body(e, last):
                pe.wait_ge(staged, e + 1)
                for j in range(8):
                    if j == 0:
                        pe.wait_ge(added, 4 * e + 1)
                    if j == 4:
                        pe.wait_ge(added, 4 * e + 2)
                    unit(e, j, XSB, j // 4)
                    if j == 5:
                        pe.wait_ge(added, 4 * e + 3)
                        pe.wait_ge(a_kept, e + 1)
                        turn(0)
                pe.wait_ge(b_kept, e + 1)
                turn(1)
                pe.wait_ge(h_lo, e + 1)
                for j in range(8, N):
                    unit(e, j, HT, 0)
                pe.wait_ge(hot, e + 1)
                pe.wait_ge(y_lo, e + 1)
                pe.wait_ge(added, 4 * e + 4)
                for slot in range(4):
                    for k in range(2):
                        for n, y in enumerate((YH, YL)):
                            ins = pe.matmul(PS[:, slot, k * 512:(k + 1) * 512], y[:, (2 * slot + k) * P:(2 * slot + k + 1) * P],
                                            ST[:], start=(n == 0), stop=(n == 1))
                    ins.then_inc(scattered, 1)
            pe.wait_ge(consts, 16)
            pe.nop().then_inc(added, 4)
            rounds(pe, body)

        @block.scalar
        def _(act):
            def split(e, j):
                at, turn = (e, j) if j < N else (e + 1, j - N)
                act.wait_ge(landed[turn % RAWS], 16 * (N // RAWS) * at + 16 * (turn // RAWS) + 16)
                if not (isinstance(e, int) and e == 0 and j < SPLITS):
                    act.wait_ge(done, N * e + j - SPLITS + 1)
                act.activation(WHI[:, turn % SPLITS, :], RAW[:, turn % RAWS, :], ACT.Copy).then_inc(w_hi, 1)

            def body(e, last):
                for j in range(N):
                    if not (last and j + SPLITS >= N):
                        split(e, j + SPLITS)
                    if j == 3:
                        act.wait_ge(done, N * e + 4)
                        act.activation(AB[:, 0, :], PS[:, 0, :], ACT.Copy).then_inc(a_kept, 1)
                    if j == 6:
                        act.wait_ge(ab_turned, 2 * e + 1)
                        act.activation(SIL[:], PS[:, 2, 0:512], ACT.Silu).then_inc(silu, 1)
                    if j == 7:
                        act.wait_ge(hidden, e + 1)
                        act.activation(HT[:, :, 0:CAPACITY], HS[:], ACT.Copy).then_inc(h_hi, 1)
                act.wait_ge(done, N * e + N)
                act.wait_ge(gated, e + 1)
                act.activation(YH[:], PS[:, 0, :], ACT.Copy, scale=gate[:, 0:1]).then_inc(y_hi, 1)
            for j in range(SPLITS):
                split(0, j)
            rounds(act, body)

        @block.vector
        def _(dve):
            def split(e, j):
                at, turn = (e, j) if j < N else (e + 1, j - N)
                dve.wait_ge(w_hi, N * e + j + 1)
                if not (isinstance(e, int) and e == 0 and j < SPLITS):
                    dve.wait_ge(done, N * e + j - SPLITS + 1)
                dve.tensor_tensor(WLO[:, turn % SPLITS, :], RAW[:, turn % RAWS, :], f32(WHI[:, turn % SPLITS, :]),
                                  ALU.subtract).then_inc(w_lo, 1)

            def add(e, slot):
                dve.wait_ge(scattered, 4 * e + slot + 1)
                dve.tensor_tensor(X[:, 2 * slot:2 * slot + 2, 0:LAT], PS[:, slot, :].rearrange("p (k t) -> p k t", k=2),
                                  X[:, 2 * slot:2 * slot + 2, 0:LAT], ALU.add).then_inc(added, 1)

            def body(e, last):
                for j in range(N):
                    if not (last and j + SPLITS >= N):
                        split(e, j + SPLITS)
                    if j == 7:
                        dve.wait_ge(done, N * e + 8)
                        dve.tensor_copy(AB[:, 1, :], PS[:, 1, :]).then_inc(b_kept, 1)
                        dve.wait_ge(ab_turned, 2 * e + 2)
                        dve.wait_ge(silu, e + 1)
                        dve.tensor_tensor(HS[:].rearrange("p a b -> p (a b)"), PS[:, 2, 512:1024], SIL[:],
                                          ALU.mult).then_inc(hidden, 1)
                        dve.wait_ge(h_hi, e + 1)
                        dve.tensor_tensor(HT[:, :, CAPACITY:P], HS[:], f32(HT[:, :, 0:CAPACITY]), ALU.subtract).then_inc(h_lo, 1)
                    if j == 8:
                        dve.wait_ge(rows_landed, 16 * e + 16)
                        dve.tensor_scalar(ST[:], ROWS[:, 0, :], prog.prm("slot"), None, ALU.is_equal).then_inc(hot, 1)
                        dve.wait_ge(hot, e + 1)
                        dve.tensor_tensor_reduce(prod[:], f32(ST[:]), ROWS[:, 1, :], 1.0, 0.0, ALU.mult, ALU.add,
                                                 gate[:, 0:1]).then_inc(gated, 1)
                dve.wait_ge(y_hi, e + 1)
                dve.scalar_tensor_tensor(YL[:], PS[:, 0, :], gate[:, 0:1], f32(YH[:]), ALU.mult, ALU.subtract).then_inc(y_lo, 1)
                for slot in range(4):
                    add(e, slot)
            for j in range(SPLITS):
                split(0, j)
            rounds(dve, body)



def build(nc, dram, out):
    prog = Program(nc, dram)
    gemms = {n: Gemm(n, dram[n], k) for n, k in GEMMS}
    order = list(gemms.values())
    for a, b in zip(order, order[1:]):
        b.base, a.next = a.base + a.n, b

    def mod(layer, section):
        m = prog.MOD[layer]
        return lambda u, t: m[:, bass.ds(8 * section + u, 1), t]

    def shift(layer, section):
        return prog.MOD[layer][:, 8 * section:8 * section + 8, :]

    stages = []
    add = lambda name, f: stages.append((name, f))
    add("start", lambda: start(prog, order))
    add("ada", lambda: condition(prog))
    add("norm1", lambda: norm(prog, prog.GAIN[0][0], shift(0, 0), BOTH))
    add("pw1", lambda: gated_projection(prog, gemms["pw1"]))
    add("conv", lambda: depthwise(prog))
    add("ln", lambda: layer_norm_silu(prog))
    add("pw2", lambda: project(prog, gemms["pw2"], prog.XNH, prog.XNL, BOTH, mod(0, 2),
                               lambda u, t: prog.G1B[:, bass.ds(u, 1), t]))
    add("norm2", lambda: norm(prog, prog.GAIN[0][1], shift(0, 3), BOTH))
    for grp in range(2):
        add(f"up0{grp}", lambda grp=grp: ffn_up(prog, gemms[f"up0{grp}"], 0, grp, BOTH))
        add(f"down0{grp}", lambda grp=grp: project(prog, gemms[f"down0{grp}"], prog.HH, prog.HL, BOTH, mod(0, 5)))
    add("norm1_1", lambda: norm(prog, prog.GAIN[1][0], shift(1, 0), BOTH))
    add("qkv", lambda: window_qkv(prog, gemms["qkv"]))
    add("rope", lambda: window_rope(prog))
    add("attn", lambda: window_attention(prog))
    add("wo", lambda: project(prog, gemms["wo"], prog.XNH, prog.XNL, LATENT, mod(1, 2)))
    add("norm2_1", lambda: norm(prog, prog.GAIN[1][1], shift(1, 3), LATENT))
    for grp in range(2):
        add(f"up1{grp}", lambda grp=grp: ffn_up(prog, gemms[f"up1{grp}"], 1, grp, LATENT))
        add(f"down1{grp}", lambda grp=grp: project(prog, gemms[f"down1{grp}"], prog.HH, prog.HL, LATENT, mod(1, 5)))
    add("final_1", lambda: rescale(prog, prog.prm("final_1", 0, 8)))
    add("norm_mix", lambda: norm(prog, prog.prm3("g_mix", 2), None, LATENT))
    add("w_in", lambda: mixing_input(prog, gemms["w_in"]))
    add("fourier", lambda: fourier(prog))
    add("latents", lambda: latents(prog))
    add("mla", lambda: latent_attention(prog))
    add("w_out", lambda: project(prog, gemms["w_out"], prog.XNH, prog.XNL, LATENT))
    add("norm_mem", lambda: norm(prog, prog.prm3("g_mem", 2), None, BOTH))
    add("mem_in", lambda: memory_inputs(prog, gemms))
    add("mem_attn", lambda: memory_attention(prog))
    add("mem_o", lambda: project(prog, gemms["mem_o"], prog.XNH, prog.XNL, LATENT))
    add("norm_moe", lambda: norm(prog, prog.prm3("g_ffn", 2), None, LATENT))
    add("router", lambda: router(prog))
    add("gather", lambda: gather(prog))
    add("moe", lambda: experts(prog))
    add("end", lambda: rescale(prog, prog.prm("final_2", 0, 8), out))
    for _, stage in stages:
        stage()


SCRATCH = {"rows": (EXPERTS, 2, LAT)}

GEMMS = [("pw1", 8), ("pw2", 8), ("up00", 8), ("down00", HID), ("up01", 8), ("down01", HID), ("qkv", 8), ("wo", 8),
         ("up10", 8), ("down10", HID), ("up11", 8), ("down11", HID), ("w_in", 8), ("w_out", 8), ("memq", 8), ("memk", 8), ("memv", 8),
         ("mem_o", 8)]



def units(w):
    k, m = w.shape
    return np.ascontiguousarray(w.reshape(k // P, P, m // P, P).transpose(2, 1, 0, 3).reshape(m // P, P, k))


def columns(v):
    return v.reshape(-1, P).T


def both(a, b):
    return np.stack([a, b], axis=-1).reshape(P, -1)


def pairs(w):
    k, m = w.shape
    return w.reshape(k, 2, m // 2 // P, P).transpose(0, 2, 1, 3).reshape(k, m)


def features(x):
    return x.T.reshape(-1, P, x.shape[0]).transpose(1, 0, 2)


def axial_tables():
    t = np.arange(LAT)
    n = HEAD_DIM // 4
    inv = np.float32(10000.0) ** (-np.arange(n, dtype=np.float32) / np.float32(n))
    row, col = (t // 64).astype(np.float32), (t % 64).astype(np.float32)
    ang = np.concatenate([row[:, None] * inv, col[:, None] * inv], axis=-1).T
    return np.stack([np.tile(np.cos(ang), (4, 1)), np.tile(np.sin(ang), (4, 1))], axis=1).astype(np.float32)


def rotation(size, at, half):
    r = np.zeros((size, size), np.float32)
    for m in range(at, size):
        if (m - at) % (2 * half) < half:
            r[m + half, m] = -1.0
        else:
            r[m - half, m] = 1.0
    return r


def window_order():
    group = HEADS // KV_HEADS
    return [group * (2 * p + half) + j for p in range(2) for j in range(group) for half in range(2)]


def layouts(x, c, ctx, c_ctx, ada_w, ada_b, norm1_g, norm2_g, final_g, conv_w_pw1, conv_b_pw1, conv_w_dw, conv_b_dw,
            conv_ln_g, conv_ln_b, conv_w_pw2, conv_b_pw2, attn_w_qkv, attn_w_o, attn_sink, ffn_w_up, ffn_w_dw, ffn_b_dw,
            ffn_w_down, mem_2, positions_2, g_mix_2, w_in_2, g_q_lat_2, w_q_up_2, g_kv_lat_2, w_kv_up_2, w_fourier_2,
            w_out_2, g_mem_q_2, g_mem_kv_2, w_mem_q_2, w_mem_kv_2, w_mem_o_2, g_ffn_2, w_router_2, w_exp_gate_2,
            w_exp_up_2, w_exp_down_2, g_final_2):
    a = {}
    a["xT"] = np.concatenate([features(x[0]), features(ctx[0])], axis=2)
    a["ada"] = np.concatenate([units(ada_w[0]), units(ada_w[1])])
    a["pw1"] = units(pairs(conv_w_pw1[0]))
    a["pw2"] = units(conv_w_pw2[0])
    for l in range(2):
        up = pairs(ffn_w_up[l])
        for grp in range(2):
            a[f"up{l}{grp}"] = units(up[:, grp * 2 * HID * P:(grp + 1) * 2 * HID * P])
            a[f"down{l}{grp}"] = units(ffn_w_down[l][grp * HID * P:(grp + 1) * HID * P])
    heads = window_order()
    q = attn_w_qkv[0][:, :D].reshape(D, HEADS, HEAD_DIM)[:, heads].reshape(D, D)
    a["qkv"] = np.concatenate([units(q), units(attn_w_qkv[0][:, D:])])
    a["wo"] = units(attn_w_o[0].reshape(HEADS, HEAD_DIM, D)[heads].reshape(D, D))
    a["memT"] = features(mem_2[0])
    a["ident"] = np.eye(P, dtype=np.float32)
    a["axial"] = axial_tables()
    a["rot_head"] = rotation(P, 0, HEAD_DIM // 2)
    r, j = np.mgrid[0:BLOCK, 0:BLOCK]
    a["masks"] = np.stack([np.where(j >= r, 0, NEG), np.where(j <= r, 0, NEG)], axis=1).astype(np.float32)
    prm = {}
    prm["sink"] = np.tile(attn_sink[0][heads], (P, 1))
    prm["final_1"] = columns(final_g)
    for l in range(2):
        prm[f"norm1_{l}"] = both(columns(norm1_g[l]), columns(norm1_g[l]))
        prm[f"norm2_{l}"] = both(columns(norm2_g[l]), columns(norm2_g[l]))
        prm[f"ada_b{l}"] = both(columns(ada_b[l]), columns(ada_b[l]))
        taps = np.stack([columns(pairs(v[None])[0]) for v in (*ffn_w_dw[l], ffn_b_dw[l])], axis=-1)
        prm[f"ffn{l}"] = taps.reshape(P, -1)
    prm["b_pw1"] = columns(pairs(conv_b_pw1)[0])
    prm["w_dw"] = np.stack([columns(v) for v in conv_w_dw[0]], axis=-1).reshape(P, -1)
    prm["b_dw"], prm["ln_g"], prm["ln_b"], prm["b_pw2"] = map(columns, (conv_b_dw[0], conv_ln_g[0], conv_ln_b[0], conv_b_pw2[0]))
    w_in = np.zeros((D, 10 * P), np.float32)
    w_in[:, 0:9 * P] = w_in_2[0][:, 0:9 * P]
    w_in[:, 9 * P + NOPE:9 * P + QK] = w_in_2[0][:, 9 * P:]
    a["w_in"] = units(w_in)
    a["w_out"], a["memq"], a["mem_o"] = units(w_out_2[0]), units(w_mem_q_2[0]), units(w_mem_o_2[0])
    a["memk"], a["memv"] = units(w_mem_kv_2[0][:, :D]), units(w_mem_kv_2[0][:, D:])
    n = np.arange(LAT)
    turn = np.outer(n, n) % LAT * (2 * np.pi / LAT)
    dft = np.stack([np.cos(turn), -np.sin(turn)], axis=1) / np.sqrt(LAT)
    a["dft"] = dft.reshape(LAT // P, P, 2, LAT).transpose(1, 0, 2, 3).astype(np.float32)
    turn = np.outer(n[:64], n[:64]) % 64 * (2 * np.pi / 64)
    a["group_dft"] = np.stack([np.kron(np.eye(2), np.cos(turn)), np.kron(np.eye(2), np.sin(turn))], axis=1).astype(np.float32) / 8
    a["w_fourier"] = np.zeros((P, 4, P), np.float32)
    for grp in range(8):
        h = grp % 2 * 64
        a["w_fourier"][h:h + 64, grp // 2, h:h + 64] = w_fourier_2[0][grp]
    a["rot_rope"] = rotation(QK, NOPE, ROPE // 2)
    a["positions"] = np.tile(positions_2, (QK, 1))
    wq = w_q_up_2[0].reshape(Q_RANK // P, P, MLA_HEADS // 2, 2 * QK)
    wkv = w_kv_up_2[0].reshape(KV_RANK // P, P, MLA_HEADS // 2, 2, NOPE + V_DIM)
    wk = np.zeros(wkv.shape[:4] + (QK,), np.float32)
    wk[..., :NOPE] = wkv[..., :NOPE]
    a["mla"] = np.concatenate([w.transpose(2, 1, 0, *range(3, w.ndim)).reshape(MLA_HEADS // 2, P, -1)
                               for w in (wq, wk, wkv[..., NOPE:])], axis=2)
    a["router"] = w_router_2[0].reshape(KD, P, EXPERTS).transpose(1, 0, 2)
    a["iota"] = np.tile(np.arange(1, CAPACITY + 1, dtype=np.float32), (P, 1))
    a["sum2"] = np.tile(np.eye(CAPACITY, dtype=np.float32), (2, 1))
    w = np.stack([w_exp_gate_2[0], w_exp_up_2[0], w_exp_down_2[0]], axis=1)
    a["experts"] = w.reshape(EXPERTS, 3, 2, HALF_K, P, 2, 512).transpose(0, 1, 5, 2, 4, 3, 6).reshape(EXPERTS, MOE_UNITS, P, HALF_K * 512)
    for name, v, w in (("g_mix", g_mix_2, g_mix_2), ("g_mem", g_mem_q_2, g_mem_kv_2), ("g_ffn", g_ffn_2, g_ffn_2)):
        prm[name] = both(columns(v[0]), columns(w[0]))
    prm["g_q"], prm["g_kv"], prm["final_2"] = columns(g_q_lat_2[0]), columns(g_kv_lat_2[0]), columns(g_final_2)
    freq = np.float32(1) / np.float32(10000.0) ** (np.arange(0, ROPE, 2, dtype=np.float32) / np.float32(ROPE))
    prm["freq"] = np.concatenate([np.zeros(NOPE), freq, freq, np.zeros(P - QK)])[:, None]
    prm["slot"] = (np.arange(P) % CAPACITY + 1.0)[:, None]
    prm["cond"] = both(columns(c[0]), columns(c_ctx))
    table = np.zeros((P, N_PARAMS), np.float32)
    for name, v in prm.items():
        at, n = PARAMS[name]
        table[:, at:at + n] = v
    a["params"] = table
    return {k: np.ascontiguousarray(v) for k, v in a.items()}


def kernel(**inputs):
    import concourse.bacc as _bacc
    from concourse.bass_utils import run_bass_kernel_spmd as _run

    nc = _bacc.Bacc("TRN2", target_bir_lowering=False, num_devices=1)
    arrays = layouts(**{name: np.asarray(v) for name, v in inputs.items()})
    dram = {n: nc.dram_tensor(n, a.shape, mybir.dt.from_np(a.dtype), kind="ExternalInput").ap() for n, a in arrays.items()}
    for n, shape in SCRATCH.items():
        dram[n] = nc.dram_tensor(n, shape, F32, kind="Internal").ap()
    out = nc.dram_tensor("out", (P, KD, LAT), F32, kind="ExternalOutput").ap()
    build(nc, dram, out)
    r = _run(nc, [arrays], core_ids=[0]).results[0]["out"]
    return np.ascontiguousarray(r.transpose(2, 1, 0).reshape(1, LAT, D))
```

```python
import math
from contextlib import contextmanager

import numpy as np

import concourse.bass as bass
from concourse import mybir

F32 = mybir.dt.float32
F32R = mybir.dt.float32r
I32 = mybir.dt.int32
ACT = mybir.ActivationFunctionType
ALU = mybir.AluOpType
AX = mybir.AxisListType

P = 128
D = 1024
KD = D // P
LAT, CTX = 512, 256
TOK = LAT + CTX
EPS = 1e-6
CONV_TAPS = 31
PAD = (CONV_TAPS - 1) // 2
LAT_AT, CTX_AT = PAD, PAD + LAT + 2 * PAD
VLEN = CTX_AT + CTX + PAD
CLEN = VLEN - 2 * PAD
CLAT, CCTX = 0, LAT + 2 * PAD
D_FF = 2816
HID = D_FF // P // 2
HEADS, KV_HEADS, HEAD_DIM = 16, 4, 64
BLOCK = 128
NEG = -1e30
SLOT = HID * P
RAWS, SPLITS = 4, 2
STAGE_SEMS = 40
LATENT, BOTH, CONTEXT = [(0, LAT)], [(0, LAT), (LAT, TOK)], [(LAT, TOK)]

PARAMS = {}
_at = 0
for _name, _n in (("norm1_0", 16), ("norm2_0", 16), ("norm1_1", 16), ("norm2_1", 16), ("ada_b0", 96), ("ada_b1", 96),
                  ("b_pw1", 16), ("w_dw", 8 * CONV_TAPS), ("b_dw", 8), ("ln_g", 8), ("ln_b", 8), ("b_pw2", 8),
                  ("ffn0", 44 * 4), ("ffn1", 44 * 4), ("sink", HEADS), ("g_mix", 16), ("g_mem", 16), ("g_ffn", 16),
                  ("g_q", 3), ("g_kv", 2), ("cond", 16), ("final_1", 8), ("freq", 1), ("slot", 1), ("final_2", 8)):
    PARAMS[_name] = (_at, _n)
    _at += _n
N_PARAMS = _at


class Gemm:
    def __init__(self, name, src, k):
        self.name, self.src, self.k = name, src, k
        self.n, self.length = src.shape[0], k * P
        self.base, self.next = 0, None


class Steps:
    def __init__(self, eng, sem, per_round=0):
        self.eng, self.sem, self.per_round = eng, sem, per_round
        self.base, self.n = 0, 0

    def round(self, i):
        self.base, self.n = self.per_round * i, 0

    def did(self, instruction):
        instruction.then_inc(self.sem, 1)
        self.n += 1

    def wait(self):
        self.eng.wait_ge(self.sem, self.base + self.n)


class Program:
    def __init__(self, nc, dram):
        self.nc, self.dram = nc, dram
        self.stage_no = 0
        self.stage_sems = []
        nc_sem = nc.alloc_semaphore
        self.raw_landed = [nc_sem(f"raw_landed{i}") for i in range(RAWS)]
        self.weights_hi = nc_sem("weights_hi")
        self.weights_lo = nc_sem("weights_lo")
        self.unit_done = nc_sem("unit_done")
        self.raw_landed_x = nc_sem("x_landed")
        self.expert_landed = [nc_sem(f"expert_landed{i}") for i in range(RAWS)]
        first = self.expert_landed[-1].num + 1
        self.banks = [first, first + STAGE_SEMS]
        base = (nc.sbuf_base + 63) // 64 * 64
        self.top = nc.sbuf_usable_end // 64 * 64
        self.small = base
        self.small_end = base + 8192
        at = self.small_end
        self.X = self.at("X", [P, KD, TOK], F32, at)
        self.XNH = self.at("XNH", [P, KD, TOK], F32R, at + 24576)
        self.XNL = self.at("XNL", [P, KD, TOK], F32R, at + 2 * 24576)
        at += 3 * 24576
        self.RAW = self.at("RAW", [P, RAWS, SLOT], F32, at)
        at += RAWS * SLOT * 4
        self.WHI = self.at("WHI", [P, SPLITS, SLOT], F32R, at)
        at += SPLITS * SLOT * 4
        self.WLO = self.at("WLO", [P, SPLITS, SLOT], F32R, at)
        at += SPLITS * SLOT * 4
        self.arena = at
        self.tmp = at + 2 * HID * TOK * 4
        self.PRM = self.keep("PRM", [P, N_PARAMS], F32)
        self.ONES = self.keep("ONES", [P, P], F32)
        self.EPSC = self.keep("EPSC", [P, 1], F32)
        self.IDENT = self.keep("IDENT", [P, P], F32)
        self.MOD = [self.keep(f"MOD{l}", [P, 48, 2], F32) for l in range(2)]
        self.GAIN = [[self.keep(f"GAIN{l}{n}", [P, KD, 2], F32) for n in range(2)] for l in range(2)]
        self.G1B = self.keep("G1B", [P, KD, 2], F32)
        self.SC = self.keep("SC", [P, KD, 2], F32)
        self.PS = nc.alloc_psum_tensor("PS", [P, 4, 1024], F32)

    def at(self, name, shape, dtype, offset):
        size = 4 * math.prod(shape[1:])
        assert offset % 32 == 0 and offset + size <= self.top, (name, offset, size, self.top)
        return self.nc.alloc_sbuf_tensor_at(name, shape, dtype, offset=offset)

    def keep(self, name, shape, dtype):
        t = self.at(name, shape, dtype, self.small)
        self.small += (4 * math.prod(shape[1:]) + 31) // 32 * 32
        assert self.small <= self.small_end, (name, self.small - self.small_end)
        return t

    def region(self, start, end):
        return Region(self, start, end)

    def sem(self, name):
        s = self.nc.alloc_semaphore(f"{name}_{self.stage_no}", num=self.banks[self.stage_no % 2] + len(self.stage_sems))
        self.stage_sems.append(s)
        assert len(self.stage_sems) <= STAGE_SEMS
        return s

    @contextmanager
    def block(self, name):
        with self.nc.Block(f"{name}{self.stage_no}") as block:
            yield block
        self.nc.clear_and_free_semaphores(self.stage_sems)
        self.stage_sems = []
        self.stage_no += 1

    def prm(self, name, index=0, n=1):
        a = PARAMS[name][0]
        return self.PRM[:, bass.ds(a + index, n)]

    def prm3(self, name, width):
        a, n = PARAMS[name]
        return self.PRM[:, a:a + n].rearrange("p (k w) -> p k w", w=width)


class Region:
    def __init__(self, prog, start, end):
        self.prog, self.at_, self.end = prog, (start + 31) // 32 * 32, end

    def take(self, name, shape, dtype=F32):
        t = self.prog.at(f"{name}_{self.prog.stage_no}", shape, dtype, self.at_)
        self.at_ += (4 * math.prod(shape[1:]) + 31) // 32 * 32
        assert self.at_ <= self.end, (name, self.at_ - self.end)
        return t


def f32(ap):
    return ap.bitcast(F32)



def run_units(eng, n, step):
    rounds = max((n - 4) // 4, 0)
    if rounds > 1:
        with eng.Fori(0, rounds) as i:
            for s in range(4):
                step(i, s)
    elif rounds == 1:
        for s in range(4):
            step(0, s)
    for u in range(4 * rounds, n):
        step(u // 4, u % 4)


def ahead(g, i, s, by):
    if isinstance(i, int) and 4 * i + s + by >= g.n:
        if g.next is None:
            return None, None
        return g.next, 4 * i + s + by - g.n
    return g, 4 * i + s + by


def load_ahead(prog, sp, g, i, s):
    to, u = ahead(g, i, s, RAWS)
    if to is None:
        return
    slot = (g.base + s) % RAWS
    sp.wait_ge(prog.weights_lo, g.base + 4 * i + s + 1)
    sp.dma_start(prog.RAW[:, slot, 0:to.length], to.src[u]).then_inc(prog.raw_landed[slot], 16)


def split_hi_ahead(prog, act, g, i, s):
    to, _ = ahead(g, i, s, SPLITS)
    if to is None:
        return
    at = g.base + s + SPLITS
    act.wait_ge(prog.raw_landed[at % RAWS], 16 * (i + at // RAWS + 1))
    act.wait_ge(prog.unit_done, g.base + 4 * i + s + 1)
    act.activation(prog.WHI[:, at % SPLITS, 0:to.length], prog.RAW[:, at % RAWS, 0:to.length],
                   ACT.Copy).then_inc(prog.weights_hi, 1)


def split_lo_ahead(prog, dve, g, i, s):
    to, _ = ahead(g, i, s, SPLITS)
    if to is None:
        return
    at = g.base + s + SPLITS
    dve.wait_ge(prog.weights_hi, g.base + 4 * i + s + SPLITS + 1)
    dve.wait_ge(prog.unit_done, g.base + 4 * i + s + 1)
    dve.tensor_tensor(prog.WLO[:, at % SPLITS, 0:to.length], prog.RAW[:, at % RAWS, 0:to.length],
                      f32(prog.WHI[:, at % SPLITS, 0:to.length]), ALU.subtract).then_inc(prog.weights_lo, 1)


def multiply(prog, pe, g, i, s, xh, xl, segments, psum_free):
    slot = (g.base + s) % SPLITS
    pe.wait_ge(prog.weights_lo, g.base + 4 * i + s + 1)
    pe.wait_ge(psum_free, 4 * i + s + 1)
    last = None
    for k in range(g.k):
        wh = prog.WHI[:, slot, k * P:(k + 1) * P]
        wl = prog.WLO[:, slot, k * P:(k + 1) * P]
        for n, (w, x) in enumerate(((wh, xh), (wh, xl), (wl, xh))):
            for a, b in segments:
                last = pe.matmul(prog.PS[:, s, a:b], w, x[:, k, a:b], start=(k == 0 and n == 0),
                                 stop=(k == g.k - 1 and n == 2))
    last.then_inc(prog.unit_done, 1)



def start(prog, gemms):
    nc = prog.nc
    first = gemms[0]
    loaded, consts, silu = prog.sem("loaded"), prog.sem("consts"), prog.sem("silu")
    with prog.block("start") as block:
        @block.sync
        def _(sp):
            sp.dma_start(prog.PRM[:], prog.dram["params"]).then_inc(loaded, 16)
            sp.dma_start(prog.IDENT[:], prog.dram["ident"]).then_inc(loaded, 16)
            sp.dma_start(prog.X[:], prog.dram["xT"]).then_inc(prog.raw_landed_x, 16)
            for u in range(RAWS):
                sp.dma_start(prog.RAW[:, u, 0:first.length], first.src[u]).then_inc(prog.raw_landed[u], 16)

        @block.scalar
        def _(act):
            act.wait_ge(loaded, 32)
            act.activation(prog.SC[:], prog.prm3("cond", 2), ACT.Silu).then_inc(silu, 1)
            for u in range(SPLITS):
                act.wait_ge(prog.raw_landed[u], 16)
                act.activation(prog.WHI[:, u, 0:first.length], prog.RAW[:, u, 0:first.length],
                               ACT.Copy).then_inc(prog.weights_hi, 1)

        @block.vector
        def _(dve):
            dve.memset(prog.ONES[:], 1.0 / D).then_inc(consts, 1)
            dve.memset(prog.EPSC[:], EPS).then_inc(consts, 1)
            for u in range(SPLITS):
                dve.wait_ge(prog.weights_hi, u + 1)
                dve.tensor_tensor(prog.WLO[:, u, 0:first.length], prog.RAW[:, u, 0:first.length],
                                  f32(prog.WHI[:, u, 0:first.length]), ALU.subtract).then_inc(prog.weights_lo, 1)


ADA_RING = 4


class Ada:
    def __init__(self, prog, layer, ring, psum):
        self.prog, self.layer, self.ring, self.psum = prog, layer, ring, psum
        self.src = prog.dram["ada"]
        self.landed = [prog.sem(f"ada_landed{s}") for s in range(ADA_RING)]
        self.used, self.step = prog.sem("ada_used"), prog.sem("ada_step")

    def load(self, sp):
        rounds = 48 // ADA_RING
        for s in range(ADA_RING):
            sp.dma_start(self.ring[:, s, :], self.src[48 * self.layer + s]).then_inc(self.landed[s], 16)
        with sp.Fori(1, rounds) as i:
            for s in range(ADA_RING):
                sp.wait_ge(self.used, ADA_RING * i - ADA_RING + s + 1)
                sp.dma_start(self.ring[:, s, :], self.src[48 * self.layer + ADA_RING * i + s]).then_inc(self.landed[s], 16)

    def multiply(self, pe):
        with pe.Fori(0, 48 // ADA_RING) as i:
            for s in range(ADA_RING):
                pe.wait_ge(self.landed[s], 16 * i + 16)
                for k in range(KD):
                    last = pe.matmul(self.psum[:, bass.ds(2 * (ADA_RING * i + s), 2)], self.ring[:, s, k * P:(k + 1) * P],
                                     self.prog.SC[:, k, :], start=(k == 0), stop=(k == KD - 1))
                last.then_inc(self.used, 1)

    def finish(self, dve):
        prog, l = self.prog, self.layer
        mod = prog.MOD[l]
        step = Steps(dve, self.step)
        dve.wait_ge(self.used, 48)
        step.did(dve.tensor_tensor(mod[:].rearrange("p a b -> p (a b)"), self.psum[:, 0:96],
                                   prog.PRM[:, PARAMS[f"ada_b{l}"][0]:PARAMS[f"ada_b{l}"][0] + 96], ALU.add))
        step.wait()
        for n in range(2):
            scale = mod[:, 24 * n + 8:24 * n + 16, :]
            step.did(dve.scalar_tensor_tensor(prog.GAIN[l][n][:], scale, 1.0, prog.prm3(f"norm{n + 1}_{l}", 2),
                                              ALU.add, ALU.mult))
        if l == 0:
            for t in range(2):
                step.did(dve.tensor_tensor(prog.G1B[:, :, t], mod[:, 16:24, t], prog.prm("b_pw2", 0, 8), ALU.mult))
        return step


def condition(prog):
    reg = prog.region(prog.arena, prog.tmp)
    with prog.block("ada") as block:
        ada = Ada(prog, 0, reg.take("ADAW", [P, ADA_RING, D]), prog.PS[:, 0, 0:512])

        @block.sync
        def _(sp):
            ada.load(sp)
            sp.wait_ge(prog.raw_landed_x, 16)

        @block.tensor
        def _(pe):
            ada.multiply(pe)

        @block.vector
        def _(dve):
            ada.finish(dve).wait()


def norm(prog, gain, shift, segments, out_hi=None, out_lo=None):
    tok = segments[-1][1]
    out_hi, out_lo = out_hi or prog.XNH, out_lo or prog.XNL
    with prog.block("norm") as block:
        reg = prog.region(prog.tmp, prog.top)
        sq = reg.take("SQ", [P, 2, tok])
        scaled = reg.take("SCALED", [P, 2, tok])
        rstd = reg.take("RSTD", [P, tok])
        mean = prog.PS[:, 0, 0:tok]
        squared, summed, root, rstd_done = prog.sem("squared"), prog.sem("summed"), prog.sem("root"), prog.sem("rstd")
        normed, full, hi, lo = prog.sem("normed"), prog.sem("full"), prog.sem("hi"), prog.sem("lo")

        @block.scalar
        def _(act):
            for k in range(KD):
                if k >= 2:
                    act.wait_ge(summed, k - 1)
                act.activation(sq[:, k % 2, :], prog.X[:, k, 0:tok], ACT.Square).then_inc(squared, 1)
            act.wait_ge(summed, KD)
            act.activation(rstd[:], mean, ACT.Sqrt, bias=prog.EPSC[:, 0:1]).then_inc(root, 1)
            for k in range(KD):
                act.wait_ge(normed, k + 1)
                if k >= 2:
                    act.wait_ge(lo, k - 1)
                for t, (a, b) in enumerate(segments):
                    ins = act.activation(scaled[:, k % 2, a:b], sq[:, k % 2, a:b], ACT.Identity,
                                         bias=0.0 if shift is None else shift[:, k, t:t + 1], scale=gain[:, k, t:t + 1])
                ins.then_inc(full, 1)
                act.wait_ge(full, k + 1)
                act.activation(out_hi[:, k, 0:tok], scaled[:, k % 2, :], ACT.Copy).then_inc(hi, 1)

        @block.tensor
        def _(pe):
            for k in range(KD):
                pe.wait_ge(squared, k + 1)
                for a, b in segments:
                    last = pe.matmul(mean[:, a:b], prog.ONES[:], sq[:, k % 2, a:b], start=(k == 0), stop=(k == KD - 1))
                last.then_inc(summed, 1)

        @block.vector
        def _(dve):
            dve.wait_ge(root, 1)
            dve.reciprocal(rstd[:], rstd[:]).then_inc(rstd_done, 1)
            dve.wait_ge(rstd_done, 1)
            for k in range(KD + 1):
                if k < KD:
                    if k >= 2:
                        dve.wait_ge(full, k - 1)
                    dve.tensor_tensor(sq[:, k % 2, :], prog.X[:, k, 0:tok], rstd[:], ALU.mult).then_inc(normed, 1)
                if k >= 1:
                    dve.wait_ge(hi, k)
                    dve.tensor_tensor(out_lo[:, k - 1, 0:tok], scaled[:, (k - 1) % 2, :],
                                      f32(out_hi[:, k - 1, 0:tok]), ALU.subtract).then_inc(lo, 1)


def gated_projection(prog, g):
    with prog.block("pw1") as block:
        reg = prog.region(prog.arena, prog.tmp)
        V = prog.V = reg.take("V", [P, KD, VLEN])
        prog.v_end = reg.at_
        tmp = prog.region(prog.tmp, prog.top)
        sig = tmp.take("SIG", [P, 2, TOK])
        psum_free, sigmoid, gated, padded = prog.sem("psum_free"), prog.sem("sigmoid"), prog.sem("gated"), prog.sem("pad")

        @block.sync
        def _(sp):
            run_units(sp, g.n, lambda i, s: load_ahead(prog, sp, g, i, s))

        @block.scalar
        def _(act):
            def step(i, s):
                split_hi_ahead(prog, act, g, i, s)
                if s % 2 == 0:
                    return
                act.wait_ge(prog.unit_done, g.base + 4 * i + s + 1)
                act.wait_ge(gated, 2 * i + s // 2 + 1)
                act.activation(sig[:, s // 2, :], prog.PS[:, s, 0:TOK], ACT.Sigmoid,
                               bias=prog.prm("b_pw1", 4 * i + s)).then_inc(sigmoid, 1)
            run_units(act, g.n, step)

        @block.vector
        def _(dve):
            dve.nop().then_inc(gated, 2)
            for a, b in ((0, LAT_AT), (LAT_AT + LAT, CTX_AT), (CTX_AT + CTX, VLEN)):
                dve.memset(V[:, :, a:b], 0.0).then_inc(padded, 1)

            def step(i, s):
                split_lo_ahead(prog, dve, g, i, s)
                if s % 2 == 0:
                    return
                dve.wait_ge(sigmoid, 2 * i + s // 2 + 1)
                for (a, b), at in zip(BOTH, (LAT_AT, CTX_AT)):
                    ins = dve.scalar_tensor_tensor(V[:, 2 * i + s // 2, at:at + b - a], prog.PS[:, s - 1, a:b],
                                                   prog.prm("b_pw1", 4 * i + s - 1), sig[:, s // 2, a:b], ALU.add, ALU.mult)
                ins.then_inc(gated, 1)
            run_units(dve, g.n, step)

        @block.tensor
        def _(pe):
            def step(i, s):
                if s % 2 == 0:
                    pe.wait_ge(gated, 2 * i + s // 2 + 1)
                multiply(prog, pe, g, i, s, prog.XNH, prog.XNL, BOTH, psum_free)
            pe.nop().then_inc(psum_free, g.n)
            run_units(pe, g.n, step)


def depthwise(prog):
    with prog.block("conv") as block:
        reg = prog.region(prog.v_end, prog.tmp)
        C = prog.C = reg.take("C", [P, KD, CLEN])
        ada = Ada(prog, 1, prog.region(prog.tmp, prog.top).take("ADAW", [P, ADA_RING, D]), prog.PS[:, 0, 0:512])
        tap_done = prog.sem("tap_done")

        @block.sync
        def _(sp):
            ada.load(sp)

        @block.tensor
        def _(pe):
            ada.multiply(pe)

        @block.vector
        def _(dve):
            steps = Steps(dve, tap_done, 2 * CONV_TAPS)
            with dve.Fori(0, KD // 2) as i:
                steps.round(i)
                for tap in range(CONV_TAPS):
                    for c in range(2):
                        v = prog.V[:, 2 * i + c, tap:tap + CLEN]
                        w = prog.prm("w_dw", (2 * i + c) * CONV_TAPS + tap)
                        out = C[:, 2 * i + c, :]
                        if tap == 0:
                            steps.did(dve.tensor_scalar(out, v, w, prog.prm("b_dw", 2 * i + c), ALU.mult, ALU.add))
                        else:
                            dve.wait_ge(tap_done, steps.base + steps.n - 1)
                            steps.did(dve.scalar_tensor_tensor(out, v, w, out, ALU.mult, ALU.add))
            ada.finish(dve).wait()


def layer_norm_silu(prog):
    with prog.block("ln") as block:
        reg = prog.region(prog.tmp, prog.top)
        tmp = reg.take("TMP", [P, 2, TOK])
        full = reg.take("FULL", [P, 2, TOK])
        rstd = reg.take("RSTD", [P, TOK])
        C = prog.C
        spans = [(0, LAT, CLAT), (LAT, TOK, CCTX)]
        mean, var = prog.PS[:, 0, 0:TOK], prog.PS[:, 1, 0:TOK]
        summed, centred, squared, sq_summed = prog.sem("summed"), prog.sem("centred"), prog.sem("squared"), prog.sem("sqs")
        root, rstd_done, normed, act_full = prog.sem("root"), prog.sem("rstd"), prog.sem("normed"), prog.sem("full")
        hi, lo = prog.sem("hi"), prog.sem("lo")

        @block.tensor
        def _(pe):
            for k in range(KD):
                for a, b, at in spans:
                    last = pe.matmul(mean[:, a:b], prog.ONES[:], C[:, k, at:at + b - a], start=(k == 0), stop=(k == KD - 1))
            last.then_inc(summed, 1)
            for k in range(KD):
                pe.wait_ge(squared, k + 1)
                for a, b in BOTH:
                    last = pe.matmul(var[:, a:b], prog.ONES[:], tmp[:, k % 2, a:b], start=(k == 0), stop=(k == KD - 1))
                last.then_inc(sq_summed, 1)

        @block.scalar
        def _(act):
            for k in range(KD):
                act.wait_ge(centred, k + 1)
                if k >= 2:
                    act.wait_ge(sq_summed, k - 1)
                for a, b, at in spans:
                    ins = act.activation(tmp[:, k % 2, a:b], C[:, k, at:at + b - a], ACT.Square)
                ins.then_inc(squared, 1)
            act.wait_ge(sq_summed, KD)
            act.activation(rstd[:], var, ACT.Sqrt, bias=prog.EPSC[:, 0:1]).then_inc(root, 1)
            for k in range(KD):
                act.wait_ge(normed, k + 1)
                if k >= 2:
                    act.wait_ge(lo, k - 1)
                act.activation(full[:, k % 2, :], tmp[:, k % 2, :], ACT.Silu, bias=prog.prm("ln_b", k),
                               scale=prog.prm("ln_g", k)).then_inc(act_full, 1)
                act.wait_ge(act_full, k + 1)
                act.activation(prog.XNH[:, k, :], full[:, k % 2, :], ACT.Copy).then_inc(hi, 1)

        @block.vector
        def _(dve):
            dve.wait_ge(summed, 1)
            for k in range(KD):
                for a, b, at in spans:
                    ins = dve.tensor_tensor(C[:, k, at:at + b - a], C[:, k, at:at + b - a], mean[:, a:b], ALU.subtract)
                ins.then_inc(centred, 1)
            dve.wait_ge(root, 1)
            dve.reciprocal(rstd[:], rstd[:]).then_inc(rstd_done, 1)
            dve.wait_ge(rstd_done, 1)
            for k in range(KD + 1):
                if k < KD:
                    if k >= 2:
                        dve.wait_ge(act_full, k - 1)
                    for a, b, at in spans:
                        ins = dve.tensor_tensor(tmp[:, k % 2, a:b], C[:, k, at:at + b - a], rstd[:, a:b], ALU.mult)
                    ins.then_inc(normed, 1)
                if k >= 1:
                    dve.wait_ge(hi, k)
                    dve.tensor_tensor(prog.XNL[:, k - 1, :], full[:, (k - 1) % 2, :], f32(prog.XNH[:, k - 1, :]),
                                      ALU.subtract).then_inc(lo, 1)


def project(prog, g, xh, xl, segments, gate=None, bias=None):
    with prog.block(g.name) as block:
        psum_free = prog.sem("psum_free")
        if bias is not None:
            tmp = prog.region(prog.tmp, prog.top).take("SCALED", [P, 2, TOK])
            scaled = prog.sem("scaled")

        @block.sync
        def _(sp):
            run_units(sp, g.n, lambda i, s: load_ahead(prog, sp, g, i, s))

        @block.scalar
        def _(act):
            def step(i, s):
                split_hi_ahead(prog, act, g, i, s)
                if bias is not None:
                    act.wait_ge(prog.unit_done, g.base + 4 * i + s + 1)
                    act.wait_ge(psum_free, 4 * i + s + 3)
                    for t, (a, b) in enumerate(segments):
                        ins = act.activation(tmp[:, s % 2, a:b], prog.PS[:, s, a:b], ACT.Identity,
                                             bias=bias(4 * i + s, t), scale=gate(4 * i + s, t))
                    ins.then_inc(scaled, 1)
            run_units(act, g.n, step)

        @block.vector
        def _(dve):
            def step(i, s):
                split_lo_ahead(prog, dve, g, i, s)
                u = 4 * i + s
                if bias is not None:
                    dve.wait_ge(scaled, u + 1)
                    a, b = segments[0][0], segments[-1][1]
                    dve.tensor_tensor(prog.X[:, u, a:b], tmp[:, s % 2, a:b], prog.X[:, u, a:b], ALU.add).then_inc(psum_free, 1)
                    return
                dve.wait_ge(prog.unit_done, g.base + u + 1)
                for t, (a, b) in enumerate(segments):
                    if gate is None:
                        ins = dve.tensor_tensor(prog.X[:, u, a:b], prog.PS[:, s, a:b], prog.X[:, u, a:b], ALU.add)
                    else:
                        ins = dve.scalar_tensor_tensor(prog.X[:, u, a:b], prog.PS[:, s, a:b], gate(u, t),
                                                       prog.X[:, u, a:b], ALU.mult, ALU.add)
                ins.then_inc(psum_free, 1)
            run_units(dve, g.n, step)

        @block.tensor
        def _(pe):
            pe.nop().then_inc(psum_free, 4)
            run_units(pe, g.n, lambda i, s: multiply(prog, pe, g, i, s, xh, xl, segments, psum_free))


def ffn_up(prog, g, layer, group, segments):
    tok = segments[-1][1]
    with prog.block("up") as block:
        reg = prog.region(prog.arena, prog.tmp)
        HH = prog.HH = reg.take("HH", [P, HID, TOK], F32R)
        HL = prog.HL = reg.take("HL", [P, HID, TOK], F32R)
        Y = prog.region(prog.tmp, prog.top).take("Y", [P, 4, tok])
        psum_free, centre, silu, hidden = prog.sem("psum_free"), prog.sem("centre"), prog.sem("silu"), prog.sem("hidden")
        hid_hi, y_free, tap = prog.sem("hid_hi"), prog.sem("y_free"), prog.sem("tap")

        def coef(i, s, n):
            return prog.prm(f"ffn{layer}", (2 * HID * group + 4 * i + s) * 4 + n)

        @block.sync
        def _(sp):
            run_units(sp, g.n, lambda i, s: load_ahead(prog, sp, g, i, s))

        @block.scalar
        def _(act):
            def step(i, s):
                split_hi_ahead(prog, act, g, i, s)
                u, j = 4 * i + s, 2 * i + s // 2
                act.wait_ge(prog.unit_done, g.base + u + 1)
                act.wait_ge(y_free, j + 1)
                act.activation(Y[:, s, :], prog.PS[:, s, 0:tok], ACT.Identity, bias=coef(i, s, 3),
                               scale=coef(i, s, 1)).then_inc(centre, 1)
                if s % 2 == 1:
                    act.wait_ge(psum_free, 4 + u)
                    act.activation(Y[:, s - 1, :], Y[:, s - 1, :], ACT.Silu).then_inc(silu, 1)
                    act.wait_ge(hidden, j + 1)
                    act.activation(HH[:, j, 0:tok], Y[:, s, :], ACT.Copy).then_inc(hid_hi, 1)
            run_units(act, g.n, step)

        @block.vector
        def _(dve):
            dve.nop().then_inc(y_free, 2)
            dve.nop().then_inc(psum_free, 4)

            def step(i, s):
                split_lo_ahead(prog, dve, g, i, s)
                u, j = 4 * i + s, 2 * i + s // 2
                dve.wait_ge(centre, u + 1)
                for a, b in segments:
                    ins = dve.scalar_tensor_tensor(Y[:, s, a + 1:b], prog.PS[:, s, a:b - 1], coef(i, s, 0),
                                                   Y[:, s, a + 1:b], ALU.mult, ALU.add)
                ins.then_inc(tap, 1)
                dve.wait_ge(tap, u + 1)
                for a, b in segments:
                    ins = dve.scalar_tensor_tensor(Y[:, s, a:b - 1], prog.PS[:, s, a + 1:b], coef(i, s, 2),
                                                   Y[:, s, a:b - 1], ALU.mult, ALU.add)
                ins.then_inc(psum_free, 1)
                if s % 2 == 1:
                    dve.wait_ge(silu, j + 1)
                    dve.wait_ge(psum_free, 4 + u + 1)
                    dve.tensor_tensor(Y[:, s, :], Y[:, s - 1, :], Y[:, s, :], ALU.mult).then_inc(hidden, 1)
                    dve.wait_ge(hid_hi, j + 1)
                    dve.tensor_tensor(HL[:, j, 0:tok], Y[:, s, :], f32(HH[:, j, 0:tok]), ALU.subtract).then_inc(y_free, 1)
            run_units(dve, g.n, step)

        @block.tensor
        def _(pe):
            run_units(pe, g.n, lambda i, s: multiply(prog, pe, g, i, s, prog.XNH, prog.XNL, segments, psum_free))


def collect(prog, g, segments_of, dest_of, loads=()):
    with prog.block(g.name) as block:
        psum_free, loaded = prog.sem("psum_free"), prog.sem("loaded")

        @block.sync
        def _(sp):
            for to, src in loads:
                sp.dma_start(to, src).then_inc(loaded, 16)
            run_units(sp, g.n, lambda i, s: load_ahead(prog, sp, g, i, s))
            if loads:
                sp.wait_ge(loaded, 16 * len(loads))

        @block.scalar
        def _(act):
            def step(i, s):
                split_hi_ahead(prog, act, g, i, s)
                u = 4 * i + s
                a, b = segments_of(u)[0][0], segments_of(u)[-1][1]
                act.wait_ge(prog.unit_done, g.base + u + 1)
                act.activation(dest_of(u), prog.PS[:, s, a:b], ACT.Copy).then_inc(psum_free, 1)
            run_units(act, g.n, step)

        @block.vector
        def _(dve):
            run_units(dve, g.n, lambda i, s: split_lo_ahead(prog, dve, g, i, s))

        @block.tensor
        def _(pe):
            pe.nop().then_inc(psum_free, 4)
            run_units(pe, g.n, lambda i, s: multiply(prog, pe, g, i, s, prog.XNH, prog.XNL, segments_of(4 * i + s), psum_free))


def window_qkv(prog, g):
    reg = prog.attn = prog.region(prog.arena, prog.top)
    QT = prog.QT = reg.take("QT", [P, KD, LAT])
    KT = prog.KT = reg.take("KT", [P, 2, TOK])
    V = prog.VF = reg.take("VF", [P, 2, TOK])
    prog.VT = reg.take("VT", [P, TOK // P, KV_HEADS * HEAD_DIM])
    prog.AXIAL = reg.take("AXIAL", [P, 2, LAT])
    prog.MASKS = reg.take("MASKS", [P, 2, BLOCK])
    prog.ROT = reg.take("ROT", [P, P])

    def kind(u):
        return u if isinstance(u, int) and u >= KD else 0

    def dest(u):
        if kind(u) == 0:
            return QT[:, u, :]
        return KT[:, u - KD, :] if u < KD + 2 else V[:, u - KD - 2, :]

    collect(prog, g, lambda u: BOTH if kind(u) else LATENT, dest, [(prog.AXIAL[:], prog.dram["axial"]), (prog.MASKS[:], prog.dram["masks"]), (prog.ROT[:], prog.dram["rot_head"])])


def window_rope(prog):
    with prog.block("rope") as block:
        reg = prog.region(prog.attn.at_, prog.top)
        part = reg.take("PART", [P, 2, LAT])
        turned = reg.take("TURNED", [P, 2, LAT])
        v_turned, v_kept = prog.sem("v_turned"), prog.sem("v_kept")
        rotated, cosined, sined, summed = prog.sem("rotated"), prog.sem("cosined"), prog.sem("sined"), prog.sem("summed")
        tiles = [prog.QT[:, k, :] for k in range(KD)] + [prog.KT[:, k, 0:LAT] for k in range(2)]

        @block.tensor
        def _(pe):
            for n, t in enumerate(tiles):
                if n >= 4:
                    pe.wait_ge(sined, n - 3)
                pe.matmul(prog.PS[:, n % 4, 0:LAT], prog.ROT[:], t, start=True, stop=True).then_inc(rotated, 1)
            for c in range(TOK // P):
                if c >= 4:
                    pe.wait_ge(v_kept, c - 3)
                for h in range(2):
                    last = pe.transpose(prog.PS[:, c % 4, LAT + h * P:LAT + (h + 1) * P], prog.VF[:, h, c * P:(c + 1) * P],
                                        prog.IDENT[:])
                last.then_inc(v_turned, 1)

        @block.scalar
        def _(act):
            for c in range(TOK // P):
                act.wait_ge(v_turned, c + 1)
                act.activation(prog.VT[:, c, :], prog.PS[:, c % 4, LAT:LAT + 2 * P], ACT.Copy).then_inc(v_kept, 1)

        @block.gpsimd
        def _(pool):
            for n, t in enumerate(tiles):
                if n >= 2:
                    pool.wait_ge(summed, n - 1)
                pool.tensor_tensor(part[:, n % 2, :], t, prog.AXIAL[:, 0, :], ALU.mult).then_inc(cosined, 1)

        @block.vector
        def _(dve):
            for n, t in enumerate(tiles):
                dve.wait_ge(rotated, n + 1)
                if n >= 2:
                    dve.wait_ge(summed, n - 1)
                dve.tensor_tensor(turned[:, n % 2, :], prog.PS[:, n % 4, 0:LAT], prog.AXIAL[:, 1, :],
                                  ALU.mult).then_inc(sined, 1)
                dve.wait_ge(cosined, n + 1)
                dve.wait_ge(sined, n + 1)
                dve.tensor_tensor(t, part[:, n % 2, :], turned[:, n % 2, :], ALU.add).then_inc(summed, 1)


def window_attention(prog):
    with prog.block("attn") as block:
        reg = prog.region(prog.attn.at_, prog.top)
        QS = reg.take("QS", [P, 2, 2, LAT])
        probs = reg.take("PROBS", [P, 2, 640])
        probsT = reg.take("PROBST", [P, 2, 640])
        stats = reg.take("STATS", [P, 2, 8])
        nsink = reg.take("NSINK", [P, HEADS])
        scale = HEAD_DIM ** -0.5
        NB = LAT // BLOCK
        UNITS = 2 * NB
        PS = prog.PS
        staged, scored, bias_ready, exped = prog.sem("staged"), prog.sem("scored"), prog.sem("bias"), prog.sem("exped")
        sunk, normed, turned, copied = prog.sem("sunk"), prog.sem("normed"), prog.sem("turned"), prog.sem("copied")
        cleared = prog.sem("cleared")
        attended, out_hi, out_free, step = prog.sem("attended"), prog.sem("out_hi"), prog.sem("out_free"), prog.sem("step")

        def keys(b):
            return [kb for kb in (b - 1, b, b + 1) if 0 <= kb < NB]

        def width(n):
            return CTX + BLOCK * len(keys(n % NB))

        def each_tile(eng, body):
            for p in range(2):
                with eng.Fori(0, NB // 2) as i:
                    for buf in range(2):
                        body(p, NB * p + 2 * i + buf, buf)

        @block.gpsimd
        def _(pool):
            def body(p, t, buf):
                pool.wait_ge(attended, t + 1)
                for half in range(2):
                    rows = slice(64 * half, 64 * half + 64)
                    ins = pool.tensor_copy(QS[rows, buf, half, :], prog.QT[rows, t, :])
                ins.then_inc(staged, 1)
            pool.memset(QS[:], 0.0).then_inc(cleared, 1)
            pool.wait_ge(cleared, 1)
            each_tile(pool, body)

        @block.tensor
        def _(pe):
            pe.nop().then_inc(attended, 2)
            pe.nop().then_inc(exped, 2)
            pe.nop().then_inc(copied, 1)
            pe.nop().then_inc(out_free, 1)
            pe.nop().then_inc(turned, 2)

            def scores(p, t, n, buf):
                half, b = n // NB, n % NB
                q = QS[:, buf, half, b * BLOCK:(b + 1) * BLOCK]
                k = prog.KT[:, p, :]
                S = PS[:, n % 2, :]
                kb = keys(b)
                pe.wait_ge(exped, UNITS * t + n + 1)
                pe.matmul(S[:, 0:CTX], q, k[:, LAT:TOK], start=True, stop=True)
                near = kb[:2]
                pe.matmul(S[:, CTX:CTX + 2 * BLOCK], q, k[:, near[0] * BLOCK:(near[0] + 2) * BLOCK], start=True, stop=False)
                m = 0 if near[0] < b else 1
                last = pe.matmul(S[:, CTX + m * BLOCK:CTX + (m + 1) * BLOCK], prog.IDENT[:], prog.MASKS[:, m, :],
                                 start=False, stop=True)
                if len(kb) == 3:
                    pe.matmul(S[:, 512:640], q, k[:, kb[2] * BLOCK:(kb[2] + 1) * BLOCK], start=True, stop=False)
                    last = pe.matmul(S[:, 512:640], prog.IDENT[:], prog.MASKS[:, 1, :], start=False, stop=True)
                last.then_inc(scored, 1)
                return last

            def transposes(t, n):
                pe.wait_ge(normed, UNITS * t + n + 1)
                pe.wait_ge(copied, UNITS * t + n + 1)
                for c in range(width(n) // P):
                    last = pe.transpose(PS[:, 2, c * P:(c + 1) * P], probs[:, n % 2, c * P:(c + 1) * P], prog.IDENT[:])
                last.then_inc(turned, 1)

            def values(p, t, n):
                half, b = n // NB, n % NB
                chunks = [NB, NB + 1] + keys(b)
                g = 2 * p + half
                if n == 0:
                    pe.wait_ge(out_free, t + 1)
                pe.wait_ge(copied, 1 + UNITS * t + n + 1)
                for c, v in enumerate(chunks):
                    last = pe.matmul(PS[64 * half:64 * half + 64, 3, b * BLOCK:(b + 1) * BLOCK],
                                     prog.VT[:, v, g * HEAD_DIM:(g + 1) * HEAD_DIM], probsT[:, n % 2, c * P:(c + 1) * P],
                                     start=(c == 0), stop=(c == len(chunks) - 1))
                return last

            def body(p, t, buf):
                pe.wait_ge(staged, t + 1)
                scores(p, t, 0, buf)
                scores(p, t, 1, buf)
                for n in range(UNITS):
                    transposes(t, n)
                    if n + 2 < UNITS:
                        scores(p, t, n + 2, buf)
                    last = values(p, t, n)
                last.then_inc(attended, 1)
            each_tile(pe, body)

        @block.vector
        def _(dve):
            steps = Steps(dve, step, 3 * UNITS)
            dve.tensor_scalar(nsink[:], prog.prm("sink", 0, HEADS), -1.0, None, ALU.mult).then_inc(sunk, 1)
            dve.wait_ge(sunk, 1)

            def maxima(t, n):
                dve.wait_ge(scored, UNITS * t + n + 1)
                st = stats[:, n % 2, :]
                steps.did(dve.reduce_max(st[:, 0:1], PS[:, n % 2, 0:width(n)], AX.X))
                steps.wait()
                dve.tensor_scalar(st[:, 1:2], st[:, 0:1], -scale, nsink[:, bass.ds(2 * t + n // NB, 1)], ALU.mult,
                                  ALU.min).then_inc(bias_ready, 1)

            def normalise(t, n):
                st = stats[:, n % 2, :]
                dve.wait_ge(exped, 2 + UNITS * t + n + 1)
                dve.wait_ge(sunk, 1 + UNITS * t + n + 1)
                steps.did(dve.tensor_tensor(st[:, 4:5], st[:, 2:3], st[:, 3:4], ALU.add))
                steps.wait()
                steps.did(dve.reciprocal(st[:, 5:6], st[:, 4:5]))
                steps.wait()
                dve.tensor_scalar(probs[:, n % 2, 0:width(n)], probs[:, n % 2, 0:width(n)], st[:, 5:6], None,
                                  ALU.mult).then_inc(normed, 1)

            def body(p, t, buf):
                steps.round(t)
                maxima(t, 0)
                maxima(t, 1)
                for n in range(UNITS):
                    normalise(t, n)
                    if n + 2 < UNITS:
                        maxima(t, n + 2)
                assert steps.n == steps.per_round
                dve.wait_ge(out_hi, t + 1)
                dve.tensor_tensor(prog.XNL[:, t, 0:LAT], PS[:, 3, 0:LAT], f32(prog.XNH[:, t, 0:LAT]),
                                  ALU.subtract).then_inc(out_free, 1)
            each_tile(dve, body)

        @block.scalar
        def _(act):
            def exponentials(t, n):
                st = stats[:, n % 2, :]
                act.wait_ge(bias_ready, UNITS * t + n + 1)
                act.wait_ge(turned, UNITS * t + n + 1)
                act.activation(probs[:, n % 2, 0:width(n)], PS[:, n % 2, 0:width(n)], ACT.Exp, bias=st[:, 1:2], scale=scale,
                               accum_out=st[:, 2:3]).then_inc(exped, 1)
                act.activation(st[:, 3:4], st[:, 1:2], ACT.Exp,
                               bias=prog.prm("sink", 2 * t + n // NB)).then_inc(sunk, 1)

            def copy(t, n):
                act.wait_ge(turned, 2 + UNITS * t + n + 1)
                act.activation(probsT[:, n % 2, 0:width(n)], PS[:, 2, 0:width(n)], ACT.Copy).then_inc(copied, 1)

            def body(p, t, buf):
                exponentials(t, 0)
                exponentials(t, 1)
                for n in range(UNITS):
                    copy(t, n)
                    if n + 2 < UNITS:
                        exponentials(t, n + 2)
                act.wait_ge(attended, 2 + t + 1)
                act.activation(prog.XNH[:, t, 0:LAT], PS[:, 3, 0:LAT], ACT.Copy).then_inc(out_hi, 1)
            each_tile(act, body)


def rescale(prog, gain, out=None):
    with prog.block("final") as block:
        reg = prog.region(prog.tmp, prog.top)
        sq = reg.take("SQ", [P, 2, LAT])
        rstd = reg.take("RSTD", [P, LAT])
        mean = prog.PS[:, 0, 0:LAT]
        squared, summed, root, scaled = prog.sem("squared"), prog.sem("summed"), prog.sem("root"), prog.sem("scaled")
        loaded, rescaled = prog.sem("loaded"), prog.sem("rescaled")

        @block.sync
        def _(sp):
            if out is None:
                sp.dma_start(prog.X[:, :, LAT:TOK], prog.dram["memT"]).then_inc(loaded, 16)
                sp.wait_ge(loaded, 16)
                return
            for k in range(0, KD, 2):
                sp.wait_ge(rescaled, k + 2)
                sp.dma_start(out[:, k:k + 2, :], prog.X[:, k:k + 2, 0:LAT]).then_inc(loaded, 16)
            sp.wait_ge(loaded, 16 * KD // 2)

        @block.scalar
        def _(act):
            for k in range(KD):
                if k >= 2:
                    act.wait_ge(summed, k - 1)
                act.activation(sq[:, k % 2, :], prog.X[:, k, 0:LAT], ACT.Square).then_inc(squared, 1)
            act.wait_ge(summed, KD)
            act.activation(rstd[:], mean, ACT.Sqrt, bias=prog.EPSC[:, 0:1]).then_inc(root, 1)

        @block.tensor
        def _(pe):
            for k in range(KD):
                pe.wait_ge(squared, k + 1)
                pe.matmul(mean, prog.ONES[:], sq[:, k % 2, :], start=(k == 0), stop=(k == KD - 1)).then_inc(summed, 1)

        @block.vector
        def _(dve):
            dve.wait_ge(root, 1)
            dve.reciprocal(rstd[:], rstd[:]).then_inc(scaled, 1)
            dve.wait_ge(scaled, 1)
            for k in range(KD):
                dve.scalar_tensor_tensor(prog.X[:, k, 0:LAT], prog.X[:, k, 0:LAT], gain[:, k:k + 1], rstd[:], ALU.mult,
                                         ALU.mult).then_inc(rescaled, 1)



MLA_HEADS, NOPE, ROPE, V_DIM = 8, 64, 32, 64
QK = NOPE + ROPE
Q_RANK, KV_RANK = 384, 256
MLA_PAIR = 2 * (Q_RANK // P * QK + KV_RANK // P * (QK + V_DIM))
MEM_HEADS, MEM_DIM = 4, 256
EXPERTS, CAPACITY = 16, 64
TWO_PI = (6.28125, 0.0019350051879882812, float(2 * np.pi - 6.28125 - 0.0019350051879882812))
SIN_LIMIT = 3.1415925


def mixing_input(prog, g):
    reg = prog.mix = prog.region(prog.arena, prog.top)
    UT = prog.UT = reg.take("UT", [P, g.n, LAT])
    prog.KRR = reg.take("KRR", [P, LAT])
    prog.COS = reg.take("COS", [P, LAT])
    prog.SIN = reg.take("SIN", [P, LAT])
    prog.ROT_ROPE = reg.take("ROTROPE", [P, QK])
    prog.mix_end = reg.at_
    prog.POS = reg.take("POS", [P, LAT], I32)
    prog.GROUP_DFT = reg.take("GROUPDFT", [P, 2, P])
    prog.WF = reg.take("WF", [P, 4, P])
    prog.DFT = reg.take("DFT", [P, LAT // P, 2, LAT])
    prog.fourier_at = reg.at_
    collect(prog, g, lambda u: LATENT, lambda u: UT[:, u, :], loads=[
        (prog.ROT_ROPE[0:QK, :], prog.dram["rot_rope"]), (prog.POS[0:QK, :], prog.dram["positions"]),
        (prog.GROUP_DFT[:], prog.dram["group_dft"]), (prog.WF[:], prog.dram["w_fourier"]),
        (prog.DFT[:], prog.dram["dft"])])


def fourier(prog):
    with prog.block("fourier") as block:
        reg = prog.region(prog.fourier_at, prog.top)
        M = reg.take("M", [P, 4, 2, P])
        PT = reg.take("PT", [P, LAT // P, 4, 2, P])
        PS = prog.PS
        mixed, m_kept = prog.sem("mixed"), prog.sem("m_kept")
        projected, p_kept = prog.sem("projected"), prog.sem("p_kept")
        summed, hi, lo = prog.sem("summed"), prog.sem("hi"), prog.sem("lo")
        slots = [1, 2, 3, 0]

        @block.tensor
        def _(pe):
            for c in range(4):
                for n in range(2):
                    last = pe.matmul(PS[:, 0, (2 * c + n) * P:(2 * c + n + 1) * P], prog.GROUP_DFT[:, n, :],
                                     prog.WF[:, c, :], start=True, stop=True)
            last.then_inc(mixed, 1)
            pe.wait_ge(m_kept, 1)
            for t in range(LAT // P):
                for c in range(4):
                    last = pe.matmul(PS[:, slots[t], c * 2 * P:(c + 1) * 2 * P], prog.UT[:, c, t * P:(t + 1) * P],
                                     M[:, c, :, :].rearrange("p a b -> p (a b)"), start=True, stop=True)
                last.then_inc(projected, 1)
            for c in range(4):
                pe.wait_ge(p_kept, LAT // P)
                for t in range(LAT // P):
                    for n in range(2):
                        last = pe.matmul(PS[:, c, 0:LAT], PT[:, t, c, n, :], prog.DFT[:, t, n, :],
                                         start=(t == 0 and n == 0), stop=(t == LAT // P - 1 and n == 1))
                last.then_inc(summed, 1)

        @block.scalar
        def _(act):
            act.wait_ge(mixed, 1)
            act.activation(M[:].rearrange("p a b c -> p (a b c)"), PS[:, 0, :], ACT.Copy).then_inc(m_kept, 1)
            for t in range(LAT // P):
                act.wait_ge(projected, t + 1)
                act.activation(PT[:, t, :, :, :].rearrange("p a b c -> p (a b c)"), PS[:, slots[t], :],
                               ACT.Copy).then_inc(p_kept, 1)
            for c in range(4):
                act.wait_ge(summed, c + 1)
                act.activation(prog.XNH[:, c, 0:LAT], PS[:, c, 0:LAT], ACT.Copy).then_inc(hi, 1)

        @block.vector
        def _(dve):
            for c in range(4):
                dve.wait_ge(hi, c + 1)
                dve.tensor_tensor(prog.XNL[:, c, 0:LAT], PS[:, c, 0:LAT], f32(prog.XNH[:, c, 0:LAT]),
                                  ALU.subtract).then_inc(lo, 1)


def latents(prog):
    with prog.block("latents") as block:
        reg = prog.region(prog.fourier_at, prog.top)
        sq = reg.take("SQ", [P, 5, LAT])
        rstd = reg.take("RSTD", [P, 2, LAT])
        ang = reg.take("ANG", [P, LAT])
        turns = reg.take("TURNS", [P, LAT])
        whole = reg.take("WHOLE", [P, LAT], I32)
        wrap = reg.take("WRAP", [P, 2, LAT])
        arg = reg.take("ARG", [P, 2, LAT])
        U, PS = prog.UT, prog.PS
        squared, summed, root, done = prog.sem("squared"), prog.sem("summed"), prog.sem("root"), prog.sem("done")
        args_ready, tables, turned = prog.sem("args"), prog.sem("tables"), prog.sem("turned")
        parts = [(0, 3, Q_RANK, "g_q"), (3, 5, KV_RANK, "g_kv")]
        r = slice(0, QK)

        @block.scalar
        def _(act):
            act.activation(sq[:], U[:, 4:9, :], ACT.Square).then_inc(squared, 1)
            act.wait_ge(summed, 1)
            for n, (a, b, rank, _) in enumerate(parts):
                ins = act.activation(rstd[:, n, :], PS[:, n, 0:LAT], ACT.Sqrt, bias=prog.EPSC[:, 0:1], scale=D / rank)
            ins.then_inc(root, 1)
            act.wait_ge(args_ready, 1)
            act.activation(prog.SIN[r, :], arg[r, 0, :], ACT.Sin)
            act.activation(prog.COS[r, :], arg[r, 1, :], ACT.Sin).then_inc(tables, 1)

        @block.tensor
        def _(pe):
            pe.wait_ge(squared, 1)
            for n, (a, b, _, _) in enumerate(parts):
                for k in range(a, b):
                    last = pe.matmul(PS[:, n, 0:LAT], prog.ONES[:], sq[:, k, :], start=(k == a), stop=(k == b - 1))
            last.then_inc(summed, 1)
            pe.matmul(PS[r, 2, 0:LAT], prog.ROT_ROPE[r, :], U[r, 9, :], start=True, stop=True).then_inc(turned, 1)

        @block.vector
        def _(dve):
            step = Steps(dve, done)

            def then(instruction):
                step.did(instruction)
                step.wait()
            then(dve.tensor_copy(turns[r, :], prog.POS[r, :]))
            then(dve.tensor_scalar(ang[r, :], turns[r, :], prog.prm("freq")[r, :], None, ALU.mult))
            then(dve.tensor_scalar(whole[r, :], ang[r, :], 1 / (2 * math.pi), None, ALU.mult))
            then(dve.tensor_copy(turns[r, :], whole[r, :]))
            for part in TWO_PI:
                then(dve.scalar_tensor_tensor(ang[r, :], turns[r, :], -part, ang[r, :], ALU.mult, ALU.add))
            dve.tensor_copy(arg[r, 0, :], ang[r, :])
            then(dve.tensor_scalar(arg[r, 1, :], ang[r, :], math.pi / 2, None, ALU.add))
            for compare, by in ((ALU.is_gt, -2 * math.pi), (ALU.is_lt, 2 * math.pi)):
                then(dve.tensor_scalar(wrap[r, :, :], arg[r, :, :], math.pi if by < 0 else -math.pi, by, compare, ALU.mult))
                then(dve.tensor_tensor(arg[r, :, :], arg[r, :, :], wrap[r, :, :], ALU.add))
            dve.tensor_scalar(arg[r, :, :], arg[r, :, :], SIN_LIMIT, -SIN_LIMIT, ALU.min, ALU.max).then_inc(args_ready, 1)
            dve.wait_ge(root, 1)
            then(dve.reciprocal(rstd[:], rstd[:]))
            for n, (a, b, _, gain) in enumerate(parts):
                for k in range(a, b):
                    dve.scalar_tensor_tensor(U[:, 4 + k, :], U[:, 4 + k, :], prog.prm(gain, k - a), rstd[:, n, :],
                                             ALU.mult, ALU.mult)
            dve.wait_ge(tables, 1)
            dve.wait_ge(turned, 1)
            step.did(dve.tensor_tensor(turns[r, :], PS[r, 2, 0:LAT], prog.SIN[r, :], ALU.mult))
            then(dve.tensor_tensor(ang[r, :], U[r, 9, :], prog.COS[r, :], ALU.mult))
            then(dve.tensor_tensor(prog.KRR[r, :], turns[r, :], ang[r, :], ALU.add))


def latent_attention(prog):
    with prog.block("mla") as block:
        reg = prog.region(prog.mix_end, prog.top)
        W = reg.take("W", [P, MLA_PAIR])
        nq, nkv = Q_RANK // P, KV_RANK // P
        WQ = W[:, 0:nq * 2 * QK].rearrange("p (k m) -> p k m", m=2 * QK)
        WK = W[:, nq * 2 * QK:(nq + nkv) * 2 * QK].rearrange("p (k m) -> p k m", m=2 * QK)
        WV = W[:, (nq + nkv) * 2 * QK:].rearrange("p (k m) -> p k m", m=2 * V_DIM)
        QS, QC, QR, KS, TS = (reg.take(n, [P, 2, LAT]) for n in ("QS", "QC", "QR", "KS", "TS"))
        VS = reg.take("VS", [P, LAT // P, 2 * V_DIM])
        probs, probsT = reg.take("PROBS", [P, 2, LAT]), reg.take("PROBST", [P, 2, LAT])
        stats = reg.take("STATS", [P, 2, 8])
        scale = QK ** -0.5
        NB = LAT // BLOCK
        UNITS, PAIRS = 2 * NB, MLA_HEADS // 2
        U, PS = prog.UT, prog.PS
        r = slice(0, QK)
        w_landed, q_made, k_made, v_made = (prog.sem(n) for n in ("w_landed", "q_made", "k_made", "v_made"))
        q_kept, k_kept, v_kept, rotated = (prog.sem(n) for n in ("q_kept", "k_kept", "v_kept", "rotated"))
        cosined, sined, roped = prog.sem("cosined"), prog.sem("sined"), prog.sem("roped")
        scored, bias_ready, exped, normed = (prog.sem(n) for n in ("scored", "bias", "exped", "normed"))
        turned, copied, attended = prog.sem("turned"), prog.sem("copied"), prog.sem("attended")
        out_hi, out_free, step = prog.sem("out_hi"), prog.sem("out_free"), prog.sem("step")

        def two(slot):
            return PS[r, slot, :].rearrange("p (h t) -> p h t", h=2)

        @block.sync
        def _(sp):
            sp.dma_start(W[:], prog.dram["mla"][0]).then_inc(w_landed, 16)
            with sp.Fori(1, PAIRS) as p:
                sp.wait_ge(v_made, p)
                sp.dma_start(W[:], prog.dram["mla"][p]).then_inc(w_landed, 16)

        @block.gpsimd
        def _(pool):
            with pool.Fori(0, PAIRS) as p:
                pool.wait_ge(q_kept, p + 1)
                pool.wait_ge(roped, p + 1)
                pool.tensor_tensor(QC[r, :, :], QS[r, :, :], prog.COS[r, :].unsqueeze(1).to_broadcast([QK, 2, LAT]),
                                   ALU.mult).then_inc(cosined, 1)

        @block.tensor
        def _(pe):
            pe.nop().then_inc(exped, 2)
            pe.nop().then_inc(copied, 1)
            pe.nop().then_inc(out_free, 1)
            pe.nop().then_inc(turned, 2)

            def scores(p, n):
                h, b = n // NB, n % NB
                pe.wait_ge(exped, UNITS * p + n + 1)
                pe.matmul(PS[:, n % 2, 0:LAT], QR[r, h, b * BLOCK:(b + 1) * BLOCK], KS[r, h, :], start=True,
                          stop=True).then_inc(scored, 1)

            def transposes(p, n):
                pe.wait_ge(normed, UNITS * p + n + 1)
                pe.wait_ge(copied, UNITS * p + n + 1)
                for c in range(LAT // P):
                    last = pe.transpose(PS[:, 2, c * P:(c + 1) * P], probs[:, n % 2, c * P:(c + 1) * P], prog.IDENT[:])
                last.then_inc(turned, 1)

            def values(p, n):
                h, b = n // NB, n % NB
                pe.wait_ge(copied, 1 + UNITS * p + n + 1)
                for c in range(LAT // P):
                    last = pe.matmul(PS[64 * h:64 * h + 64, 3, b * BLOCK:(b + 1) * BLOCK], VS[:, c, h * V_DIM:(h + 1) * V_DIM],
                                     probsT[:, n % 2, c * P:(c + 1) * P], start=(c == 0), stop=(c == LAT // P - 1))
                return last

            with pe.Fori(0, PAIRS) as p:
                pe.wait_ge(w_landed, 16 * p + 16)
                pe.wait_ge(exped, 2 + UNITS * p)
                pe.wait_ge(copied, 1 + UNITS * p)
                for h in range(2):
                    for k in range(nq):
                        last = pe.matmul(two(0)[:, h, :], WQ[:, k, h * QK:(h + 1) * QK], U[:, 4 + k, :], start=(k == 0),
                                         stop=(k == nq - 1))
                last.then_inc(q_made, 1)
                for h in range(2):
                    for k in range(nkv):
                        last = pe.matmul(two(1)[:, h, :], WK[:, k, h * QK:(h + 1) * QK], U[:, 7 + k, :], start=(k == 0),
                                         stop=(k == nkv - 1))
                last.then_inc(k_made, 1)
                for t in range(LAT // P):
                    for k in range(nkv):
                        last = pe.matmul(PS[:, 2, t * P:(t + 1) * P], U[:, 7 + k, t * P:(t + 1) * P], WV[:, k, :],
                                         start=(k == 0), stop=(k == nkv - 1))
                last.then_inc(v_made, 1)
                pe.wait_ge(q_kept, p + 1)
                pe.wait_ge(out_free, p + 1)
                for h in range(2):
                    last = pe.matmul(two(3)[:, h, :], prog.ROT_ROPE[r, :], QS[r, h, :], start=True, stop=True)
                last.then_inc(rotated, 1)
                pe.wait_ge(roped, 1 + p + 1)
                pe.wait_ge(k_kept, p + 1)
                pe.wait_ge(v_kept, p + 1)
                scores(p, 0)
                scores(p, 1)
                for n in range(UNITS):
                    transposes(p, n)
                    if n + 2 < UNITS:
                        scores(p, n + 2)
                    last = values(p, n)
                last.then_inc(attended, 1)

        @block.vector
        def _(dve):
            steps = Steps(dve, step, 2 * UNITS)
            dve.nop().then_inc(roped, 1)

            def maxima(p, n):
                dve.wait_ge(scored, UNITS * p + n + 1)
                st = stats[:, n % 2, :]
                steps.did(dve.reduce_max(st[:, 0:1], PS[:, n % 2, 0:LAT], AX.X))
                steps.wait()
                dve.wait_ge(exped, UNITS * p + n + 1)
                dve.tensor_scalar(st[:, 1:2], st[:, 0:1], -scale, None, ALU.mult).then_inc(bias_ready, 1)

            def normalise(p, n):
                st = stats[:, n % 2, :]
                dve.wait_ge(exped, 2 + UNITS * p + n + 1)
                steps.did(dve.reciprocal(st[:, 3:4], st[:, 2:3]))
                steps.wait()
                dve.tensor_scalar(probs[:, n % 2, :], probs[:, n % 2, :], st[:, 3:4], None, ALU.mult).then_inc(normed, 1)

            with dve.Fori(0, PAIRS) as p:
                steps.round(p)
                dve.wait_ge(k_made, p + 1)
                dve.tensor_tensor(KS[r, :, :], two(1), prog.KRR[r, :].unsqueeze(1).to_broadcast([QK, 2, LAT]),
                                  ALU.add).then_inc(k_kept, 1)
                dve.wait_ge(rotated, p + 1)
                dve.tensor_tensor(TS[r, :, :], two(3), prog.SIN[r, :].unsqueeze(1).to_broadcast([QK, 2, LAT]),
                                  ALU.mult).then_inc(sined, 1)
                dve.wait_ge(sined, p + 1)
                dve.wait_ge(cosined, p + 1)
                dve.tensor_tensor(QR[r, :, :], TS[r, :, :], QC[r, :, :], ALU.add).then_inc(roped, 1)
                maxima(p, 0)
                maxima(p, 1)
                for n in range(UNITS):
                    normalise(p, n)
                    if n + 2 < UNITS:
                        maxima(p, n + 2)
                assert steps.n == steps.per_round
                dve.wait_ge(out_hi, p + 1)
                dve.tensor_tensor(prog.XNL[:, 4 + p, 0:LAT], PS[:, 3, 0:LAT], f32(prog.XNH[:, 4 + p, 0:LAT]),
                                  ALU.subtract).then_inc(out_free, 1)

        @block.scalar
        def _(act):
            def exponentials(p, n):
                st = stats[:, n % 2, :]
                act.wait_ge(bias_ready, UNITS * p + n + 1)
                act.wait_ge(turned, UNITS * p + n + 1)
                act.activation(probs[:, n % 2, :], PS[:, n % 2, 0:LAT], ACT.Exp, bias=st[:, 1:2], scale=scale,
                               accum_out=st[:, 2:3]).then_inc(exped, 1)

            def copy(p, n):
                act.wait_ge(turned, 2 + UNITS * p + n + 1)
                act.activation(probsT[:, n % 2, :], PS[:, 2, 0:LAT], ACT.Copy).then_inc(copied, 1)

            with act.Fori(0, PAIRS) as p:
                act.wait_ge(q_made, p + 1)
                act.wait_ge(roped, p + 1)
                act.activation(QS[r, :, :], two(0), ACT.Copy).then_inc(q_kept, 1)
                act.wait_ge(v_made, p + 1)
                act.activation(VS[:].rearrange("p a b -> p (a b)"), PS[:, 2, 0:LAT], ACT.Copy).then_inc(v_kept, 1)
                exponentials(p, 0)
                exponentials(p, 1)
                for n in range(UNITS):
                    copy(p, n)
                    if n + 2 < UNITS:
                        exponentials(p, n + 2)
                act.wait_ge(attended, p + 1)
                act.activation(prog.XNH[:, 4 + p, 0:LAT], PS[:, 3, 0:LAT], ACT.Copy).then_inc(out_hi, 1)


def memory_attention(prog):
    with prog.block("mem") as block:
        reg = prog.region(prog.memory_at, prog.top)
        QS = reg.take("QS", [P, 2, LAT])
        VF, VS = reg.take("VF", [P, 2, CTX]), reg.take("VS", [P, 2, MEM_DIM])
        probs, probsT = reg.take("PROBS", [P, 2, CTX]), reg.take("PROBST", [P, 2, CTX])
        stats = reg.take("STATS", [P, 2, 8])
        scale = MEM_DIM ** -0.5
        NB = LAT // BLOCK
        PS = prog.PS
        staged, scored, bias_ready, exped, normed = (prog.sem(n) for n in ("staged", "scored", "bias", "exped", "normed"))
        v_turned, v_kept = prog.sem("v_turned"), prog.sem("v_kept")
        turned, copied, attended = prog.sem("turned"), prog.sem("copied"), prog.sem("attended")
        out_hi, out_free, step = prog.sem("out_hi"), prog.sem("out_free"), prog.sem("step")
        out = PS[:, 3, :].rearrange("p (d t) -> p d t", d=2)

        @block.gpsimd
        def _(pool):
            with pool.Fori(0, MEM_HEADS) as h:
                pool.wait_ge(attended, h + 1)
                pool.tensor_copy(VF[:], prog.VM[:, bass.ds(2 * h, 2), :]).then_inc(staged, 1)
                pool.tensor_copy(QS[:], prog.QM[:, bass.ds(2 * h, 2), :]).then_inc(staged, 1)

        @block.tensor
        def _(pe):
            pe.nop().then_inc(attended, 1)
            pe.nop().then_inc(exped, 2)
            pe.nop().then_inc(copied, 1)
            pe.nop().then_inc(out_free, 1)
            pe.nop().then_inc(turned, 2)

            def scores(h, b):
                pe.wait_ge(exped, NB * h + b + 1)
                for d in range(2):
                    last = pe.matmul(PS[:, b % 2, 0:CTX], QS[:, d, b * BLOCK:(b + 1) * BLOCK], prog.KM[:, 2 * h + d, :],
                                     start=(d == 0), stop=(d == 1))
                last.then_inc(scored, 1)

            def transposes(h, b):
                pe.wait_ge(normed, NB * h + b + 1)
                pe.wait_ge(copied, NB * h + b + 1)
                if b == 0:
                    pe.wait_ge(v_kept, h + 1)
                for c in range(CTX // P):
                    last = pe.transpose(PS[:, 2, c * P:(c + 1) * P], probs[:, b % 2, c * P:(c + 1) * P], prog.IDENT[:])
                last.then_inc(turned, 1)

            def values(h, b):
                if b == 0:
                    pe.wait_ge(out_free, h + 1)
                pe.wait_ge(copied, 1 + NB * h + b + 1)
                for d in range(2):
                    for c in range(CTX // P):
                        last = pe.matmul(out[:, d, b * BLOCK:(b + 1) * BLOCK], VS[:, c, d * P:(d + 1) * P],
                                         probsT[:, b % 2, c * P:(c + 1) * P], start=(c == 0), stop=(c == CTX // P - 1))
                return last

            with pe.Fori(0, MEM_HEADS) as h:
                pe.wait_ge(staged, 2 * h + 1)
                pe.wait_ge(copied, 1 + NB * h)
                for c in range(CTX // P):
                    for d in range(2):
                        last = pe.transpose(PS[:, 2, (2 * c + d) * P:(2 * c + d + 1) * P], VF[:, d, c * P:(c + 1) * P],
                                            prog.IDENT[:])
                last.then_inc(v_turned, 1)
                pe.wait_ge(staged, 2 * h + 2)
                scores(h, 0)
                scores(h, 1)
                for b in range(NB):
                    transposes(h, b)
                    if b + 2 < NB:
                        scores(h, b + 2)
                    last = values(h, b)
                last.then_inc(attended, 1)

        @block.vector
        def _(dve):
            steps = Steps(dve, step, 2 * NB)

            def maxima(h, b):
                dve.wait_ge(scored, NB * h + b + 1)
                st = stats[:, b % 2, :]
                steps.did(dve.reduce_max(st[:, 0:1], PS[:, b % 2, 0:CTX], AX.X))
                steps.wait()
                dve.wait_ge(exped, NB * h + b + 1)
                dve.tensor_scalar(st[:, 1:2], st[:, 0:1], -scale, None, ALU.mult).then_inc(bias_ready, 1)

            def normalise(h, b):
                st = stats[:, b % 2, :]
                dve.wait_ge(exped, 2 + NB * h + b + 1)
                steps.did(dve.reciprocal(st[:, 3:4], st[:, 2:3]))
                steps.wait()
                dve.tensor_scalar(probs[:, b % 2, :], probs[:, b % 2, :], st[:, 3:4], None, ALU.mult).then_inc(normed, 1)

            with dve.Fori(0, MEM_HEADS) as h:
                steps.round(h)
                maxima(h, 0)
                maxima(h, 1)
                for b in range(NB):
                    normalise(h, b)
                    if b + 2 < NB:
                        maxima(h, b + 2)
                assert steps.n == steps.per_round
                dve.wait_ge(out_hi, h + 1)
                dve.tensor_tensor(prog.XNL[:, bass.ds(2 * h, 2), 0:LAT], out, f32(prog.XNH[:, bass.ds(2 * h, 2), 0:LAT]),
                                  ALU.subtract).then_inc(out_free, 1)

        @block.scalar
        def _(act):
            def exponentials(h, b):
                st = stats[:, b % 2, :]
                act.wait_ge(bias_ready, NB * h + b + 1)
                act.wait_ge(turned, NB * h + b + 1)
                act.activation(probs[:, b % 2, :], PS[:, b % 2, 0:CTX], ACT.Exp, bias=st[:, 1:2], scale=scale,
                               accum_out=st[:, 2:3]).then_inc(exped, 1)

            def copy(h, b):
                act.wait_ge(turned, 2 + NB * h + b + 1)
                act.activation(probsT[:, b % 2, :], PS[:, 2, 0:CTX], ACT.Copy).then_inc(copied, 1)

            with act.Fori(0, MEM_HEADS) as h:
                act.wait_ge(v_turned, h + 1)
                act.activation(VS[:].rearrange("p a b -> p (a b)"), PS[:, 2, 0:2 * MEM_DIM], ACT.Copy).then_inc(v_kept, 1)
                exponentials(h, 0)
                exponentials(h, 1)
                for b in range(NB):
                    copy(h, b)
                    if b + 2 < NB:
                        exponentials(h, b + 2)
                act.wait_ge(attended, 1 + h + 1)
                act.activation(prog.XNH[:, bass.ds(2 * h, 2), 0:LAT], out, ACT.Copy).then_inc(out_hi, 1)


def memory_inputs(prog, gemms):
    reg = prog.region(prog.arena, prog.top)
    QM = prog.QM = reg.take("QM", [P, KD, LAT])
    KM = prog.KM = reg.take("KM", [P, KD, CTX])
    VM = prog.VM = reg.take("VM", [P, KD, CTX])
    prog.memory_at = reg.at_
    collect(prog, gemms["memq"], lambda u: LATENT, lambda u: QM[:, u, :])
    collect(prog, gemms["memk"], lambda u: CONTEXT, lambda u: KM[:, u, :])
    collect(prog, gemms["memv"], lambda u: CONTEXT, lambda u: VM[:, u, :])


MOE_UNITS = 12
HALF_K = KD // 2


class Moe:
    def __init__(self, prog):
        at = prog.small_end + 24576
        self.XS = prog.at("XS", [P, EXPERTS, KD, P], F32R, at)
        at += EXPERTS * KD * P * 4
        self.RAW = prog.at("RAWM", [P, RAWS, HALF_K * 512], F32, at)
        at += RAWS * HALF_K * 512 * 4
        self.WHI = prog.at("WHIM", [P, 2 * SPLITS, HALF_K * 256], F32R, at)
        self.S = prog.at("SLOTS", [P, LAT // P, EXPERTS * CAPACITY], F32R, at)
        at += SPLITS * HALF_K * 512 * 4
        self.WLO = prog.at("WLOM", [P, 2 * SPLITS, HALF_K * 256], F32R, at)
        at += SPLITS * HALF_K * 512 * 4
        self.scratch = at


def router(prog):
    moe = prog.moe = Moe(prog)
    with prog.block("router") as block:
        reg = prog.region(moe.scratch, prog.top)
        NT = LAT // P
        HTH = prog.HTH = reg.take("HTH", [P, NT, D], F32R)
        HTL = prog.HTL = reg.take("HTL", [P, NT, D], F32R)
        prog.SLOT_T = reg.take("SLOTT", [P, NT, EXPERTS])
        prog.IOTA = reg.take("IOTA", [P, CAPACITY])
        spare = prog.region(prog.small_end + 3 * 24576, prog.small_end + 3 * 24576 + 16384)
        R = spare.take("R", [P, KD, P])
        RH, RL = spare.take("RH", [P, KD, P], F32R), spare.take("RL", [P, KD, P], F32R)
        LT = spare.take("LT", [P, LAT])
        L, stats = reg.take("L", [P, NT, EXPERTS]), reg.take("STATS", [P, 2, NT])
        ROW, WORK = reg.take("ROW", [P, 2, LAT]), reg.take("WORK", [P, LAT])
        SEL, RANK, ZERO = reg.take("SEL", [P, LAT]), reg.take("RANK", [P, LAT]), reg.take("ZERO", [P, LAT])
        TOP = reg.take("TOP", [P, 8])
        loaded, r_hi, r_lo, logits, step = (prog.sem(n) for n in ("loaded", "r_hi", "r_lo", "logits", "step"))
        exped, probs, rows, rows_kept = (prog.sem(n) for n in ("exped", "probs", "rows", "rows_kept"))
        turned, hT_kept, slots, slot_turned, stored = (prog.sem(n) for n in ("turned", "ht", "slots", "sturned", "stored"))
        logitsT, logits_kept = prog.sem("logitsT"), prog.sem("logits_kept")
        PS, E = prog.PS, slice(0, EXPERTS)
        halves = [(x, t, h) for t in range(NT) for x in range(2) for h in range(2)]

        @block.sync
        def _(sp):
            sp.dma_start(R[:], prog.dram["router"]).then_inc(loaded, 16)
            sp.dma_start(prog.IOTA[:], prog.dram["iota"]).then_inc(loaded, 16)
            for j in range(RAWS):
                sp.dma_start(moe.RAW[:, j, :], prog.dram["experts"][0, j]).then_inc(prog.expert_landed[j], 16)
            sp.wait_ge(slots, 1)
            sp.dma_start(prog.dram["rows"], ROW[E, :, :]).then_inc(stored, 16)
            sp.wait_ge(stored, 16)

        @block.tensor
        def _(pe):
            pe.wait_ge(r_lo, 1)
            for k in range(KD):
                for n, (x, w) in enumerate(((prog.XNH, RH), (prog.XNH, RL), (prog.XNL, RH), (prog.XNL, RL))):
                    last = pe.matmul(PS[:, 1, 0:LAT], w[:, k, :], x[:, k, 0:LAT], start=(k == 0 and n == 0),
                                     stop=(k == KD - 1 and n == 3))
            last.then_inc(logitsT, 1)
            pe.wait_ge(logits_kept, 1)
            for t in range(NT):
                last = pe.transpose(PS[:, 0, t * EXPERTS:(t + 1) * EXPERTS], LT[E, t * P:(t + 1) * P], prog.IDENT[E, E])
            last.then_inc(logits, 1)
            pe.wait_ge(probs, 1)
            for t in range(NT):
                last = pe.transpose(PS[E, 1, t * P:(t + 1) * P], L[:, t, :], prog.IDENT[:])
            last.then_inc(rows, 1)
            for n, (x, t, h) in enumerate(halves):
                if n >= 4:
                    pe.wait_ge(hT_kept, n - 3)
                src = (prog.XNH, prog.XNL)[x]
                for k in range(4):
                    at = n % 2 * 512 + k * P
                    last = pe.transpose(PS[:, 2 + n // 2 % 2, at:at + P], f32(src[:, 4 * h + k, t * P:(t + 1) * P]),
                                        prog.IDENT[:])
                last.then_inc(turned, 1)
            pe.wait_ge(slots, 1)
            for t in range(NT):
                last = pe.transpose(PS[:, 0, t * EXPERTS:(t + 1) * EXPERTS], ROW[E, 0, t * P:(t + 1) * P],
                                    prog.IDENT[E, E])
            last.then_inc(slot_turned, 1)

        @block.scalar
        def _(act):
            act.wait_ge(loaded, 32)
            act.activation(RH[:], R[:], ACT.Copy).then_inc(r_hi, 1)
            act.wait_ge(logitsT, 1)
            act.activation(LT[E, :], PS[E, 1, 0:LAT], ACT.Copy).then_inc(logits_kept, 1)
            act.wait_ge(step, 2)
            act.activation(L[:], L[:], ACT.Exp).then_inc(exped, 1)
            act.wait_ge(rows, 1)
            act.activation(ROW[E, 1, :], PS[E, 1, 0:LAT], ACT.Copy).then_inc(rows_kept, 1)
            for n, (x, t, h) in enumerate(halves):
                act.wait_ge(turned, n + 1)
                act.activation((HTH, HTL)[x][:, t, h * 512:(h + 1) * 512], PS[:, 2 + n // 2 % 2, n % 2 * 512:n % 2 * 512 + 512],
                               ACT.Copy).then_inc(hT_kept, 1)
            act.wait_ge(slot_turned, 1)
            act.activation(prog.SLOT_T[:].rearrange("p a b -> p (a b)"), PS[:, 0, 0:NT * EXPERTS], ACT.Copy)

        @block.vector
        def _(dve):
            steps = Steps(dve, step)

            def then(instruction):
                steps.did(instruction)
                steps.wait()
            dve.memset(ZERO[E, :], 0.0)
            dve.wait_ge(r_hi, 1)
            dve.tensor_tensor(RL[:], R[:], f32(RH[:]), ALU.subtract).then_inc(r_lo, 1)
            dve.wait_ge(logits, 1)
            pl = PS[:, 0, 0:NT * EXPERTS].rearrange("p (t e) -> p t e", e=EXPERTS)
            wide = lambda s: s.unsqueeze(2).to_broadcast([P, NT, EXPERTS])
            then(dve.reduce_max(stats[:, 0, :], pl, AX.X))
            then(dve.tensor_tensor(L[:], pl, wide(stats[:, 0, :]), ALU.subtract))
            dve.wait_ge(exped, 1)
            then(dve.reduce_sum(stats[:, 0, :], L[:], AX.X))
            then(dve.reciprocal(stats[:, 1, :], stats[:, 0, :]))
            dve.tensor_tensor(L[:], L[:], wide(stats[:, 1, :]), ALU.mult).then_inc(probs, 1)
            dve.wait_ge(rows_kept, 1)
            then(dve.tensor_copy(WORK[E, :], ROW[E, 1, :]))
            for _ in range(CAPACITY // 8):
                then(dve.max(TOP[E, :], WORK[E, :]))
                then(dve.match_replace(WORK[E, :], TOP[E, :], WORK[E, :], -1.0))
            then(dve.tensor_scalar(SEL[E, :], WORK[E, :], 0.0, None, ALU.is_lt))
            then(dve.tensor_tensor_scan(RANK[E, :], SEL[E, :], ZERO[E, :], 0.0, ALU.add, ALU.add))
            dve.tensor_tensor(ROW[E, 0, :], RANK[E, :], SEL[E, :], ALU.mult).then_inc(slots, 1)


def gather(prog):
    moe = prog.moe
    with prog.block("gather") as block:
        NT = LAT // P
        hot, gathered = prog.sem("hot"), prog.sem("gathered")
        kept = [prog.sem("kept_by_act"), prog.sem("kept_by_dve")]
        work = [(k, x) for k in range(KD) for x in range(2)]

        @block.vector
        def _(dve):
            for t in range(NT):
                dve.tensor_tensor(moe.S[:, t, :].rearrange("p (e s) -> p e s", s=CAPACITY),
                                  prog.IOTA[:].unsqueeze(1).to_broadcast([P, EXPERTS, CAPACITY]),
                                  prog.SLOT_T[:, t, :].unsqueeze(2).to_broadcast([P, EXPERTS, CAPACITY]),
                                  ALU.is_equal).then_inc(hot, 1)
            for n, (k, x) in enumerate(work):
                if n % 2 == 1:
                    dve.wait_ge(gathered, n + 1)
                    dve.tensor_copy(moe.XS[:, :, k, x * 64:(x + 1) * 64],
                                    prog.PS[:, n % 4, :].rearrange("p (e s) -> p e s", s=CAPACITY)).then_inc(kept[1], 1)

        @block.scalar
        def _(act):
            for n, (k, x) in enumerate(work):
                if n % 2 == 0:
                    act.wait_ge(gathered, n + 1)
                    act.activation(moe.XS[:, :, k, x * 64:(x + 1) * 64],
                                   prog.PS[:, n % 4, :].rearrange("p (e s) -> p e s", s=CAPACITY), ACT.Copy).then_inc(kept[0], 1)

        @block.tensor
        def _(pe):
            for n, (k, x) in enumerate(work):
                if n >= 4:
                    pe.wait_ge(kept[n % 2], n // 2 - 1)
                src = (prog.HTH, prog.HTL)[x]
                for t in range(NT):
                    if n == 0:
                        pe.wait_ge(hot, t + 1)
                    for half in range(2):
                        last = pe.matmul(prog.PS[:, n % 4, half * 512:(half + 1) * 512], src[:, t, k * P:(k + 1) * P],
                                         moe.S[:, t, half * 512:(half + 1) * 512], start=(t == 0), stop=(t == NT - 1))
                last.then_inc(gathered, 1)


def experts(prog):
    moe = prog.moe
    with prog.block("moe") as block:
        reg = prog.region(moe.scratch, prog.top)
        ROWS = reg.take("ROWS", [P, 2, LAT])
        XSB = reg.take("XSB", [P, KD, P], F32R)
        HT = reg.take("HT", [P, KD, P], F32R)
        HS = reg.take("HS", [P, KD, CAPACITY])
        SIL = reg.take("SIL", [P, KD, CAPACITY])
        AB = reg.take("AB", [P, 2, D])
        YH, YL = reg.take("YH", [P, D], F32R), reg.take("YL", [P, D], F32R)
        ST = reg.take("ST", [P, LAT], F32R)
        prod = reg.take("PROD", [P, LAT])
        gate = reg.take("GATE", [P, 2])
        SUM2 = reg.take("SUM2", [P, P])
        RAW, WHI, WLO, XS, PS, X = moe.RAW, moe.WHI, moe.WLO, moe.XS, prog.PS, prog.X
        w_hi, w_lo, done, staged = (prog.sem(n) for n in ("w_hi", "w_lo", "done", "staged"))
        rows_landed, hot, gated, turned = (prog.sem(n) for n in ("rows_landed", "hot", "gated", "turned"))
        a_kept, b_kept = prog.sem("a_kept"), prog.sem("b_kept")
        silu, hidden, h_hi, h_lo, y_hi, y_lo = (prog.sem(n) for n in ("silu", "hidden", "h_hi", "h_lo", "y_hi", "y_lo"))
        scattered, added, consts, zeroed = prog.sem("scattered"), prog.sem("added"), prog.sem("consts"), prog.sem("zeroed")
        N, last_e = 2 * MOE_UNITS, EXPERTS - 1
        RING = 2 * SPLITS
        A_SLOT, B_SLOT, Y_SLOT, TURN_SLOTS = 0, 1, 1, (2, 3)
        QUARTERS = (2, 3, 3, 0)

        def rounds(eng, body):
            with eng.Fori(0, last_e) as e:
                body(e, False)
            body(last_e, True)

        @block.sync
        def _(sp):
            sp.dma_start(SUM2[:], prog.dram["sum2"]).then_inc(consts, 16)

            def load_rows(e):
                sp.dma_start(ROWS[:], prog.dram["rows"][e].partition_broadcast(P)).then_inc(rows_landed, 16)
            load_rows(0)

            def body(e, last):
                for j in range(MOE_UNITS):
                    if last and j + RAWS >= MOE_UNITS:
                        continue
                    sp.wait_ge(w_lo, N * e + 2 * j + 2)
                    to = (e, j + RAWS) if j + RAWS < MOE_UNITS else (e + 1, j + RAWS - MOE_UNITS)
                    sp.dma_start(RAW[:, j % RAWS, :], prog.dram["experts"][to[0], to[1]]).then_inc(prog.expert_landed[j % RAWS], 16)
                    if j == 9 and not last:
                        sp.wait_ge(gated, e + 1)
                        load_rows(e + 1)
            rounds(sp, body)

        @block.gpsimd
        def _(pool):
            pool.tensor_copy(XSB[:], XS[:, 0, :, :]).then_inc(staged, 1)
            with pool.Fori(1, EXPERTS) as e:
                pool.wait_ge(done, N * e - N + 16)
                pool.tensor_copy(XSB[:], XS[:, e, :, :]).then_inc(staged, 1)

        @block.tensor
        def _(pe):
            def half_unit(e, h, x, slot):
                j = h // 2
                out_half, k0 = j % 4 // 2, HALF_K * (j % 2) + 2 * (h % 2)
                pe.wait_ge(w_lo, N * e + h + 1)
                for k in range(2):
                    for n, w in enumerate((WHI, WLO)):
                        last = pe.matmul(PS[:, slot, out_half * 512:(out_half + 1) * 512], x[:, k0 + k, :],
                                         w[:, h % RING, k * 512:(k + 1) * 512], start=(k0 + k == 0 and n == 0),
                                         stop=(k0 + k == KD - 1 and n == 1))
                last.then_inc(done, 1)

            def turn(n):
                for k in range(KD):
                    last = pe.matmul(PS[:, TURN_SLOTS[n], k * P:(k + 1) * P], AB[:, n, k * P:(k + 1) * P], SUM2[:],
                                     start=True, stop=True)
                last.then_inc(turned, 1)

            def scatter(quarter):
                for k in range(2):
                    for n, y in enumerate((YH, YL)):
                        last = pe.matmul(PS[:, QUARTERS[quarter], k * 512:(k + 1) * 512],
                                         y[:, (2 * quarter + k) * P:(2 * quarter + k + 1) * P], ST[:], start=(n == 0), stop=(n == 1))
                last.then_inc(scattered, 1)

            def body(e, last):
                pe.wait_ge(staged, e + 1)
                for h in range(16):
                    if h == 0:
                        pe.wait_ge(added, 4 * e + 1)
                    if h == 8:
                        pe.wait_ge(y_lo, e + 1)
                    half_unit(e, h, XSB, (A_SLOT, B_SLOT)[h // 8])
                    if h == 3:
                        pe.wait_ge(hot, e + 1)
                        pe.wait_ge(y_lo, e + 1)
                        pe.wait_ge(h_lo, e + 1)
                        scatter(0)
                        scatter(1)
                    if h == 11:
                        pe.wait_ge(a_kept, e + 1)
                        pe.wait_ge(added, 4 * e + 2)
                        turn(0)
                        pe.wait_ge(added, 4 * e + 3)
                        scatter(2)
                scatter(3)
                pe.wait_ge(b_kept, e + 1)
                pe.wait_ge(added, 4 * e + 4)
                turn(1)
                pe.wait_ge(h_lo, e + 2)
                for h in range(16, N):
                    half_unit(e, h, HT, Y_SLOT)
            pe.wait_ge(consts, 16)
            pe.wait_ge(zeroed, 3)
            pe.nop().then_inc(added, 1)
            pe.nop().then_inc(h_lo, 1)
            rounds(pe, body)
            pe.wait_ge(hot, EXPERTS + 1)
            pe.wait_ge(y_lo, EXPERTS + 1)
            for quarter in range(4):
                if quarter == 0:
                    pe.wait_ge(added, 4 * EXPERTS + 1)
                if quarter == 2:
                    pe.wait_ge(added, 4 * EXPERTS + 3)
                scatter(quarter)

        @block.scalar
        def _(act):
            def split(e, h):
                at, h = (e, h) if h < N else (e + 1, h - N)
                j = h // 2
                act.wait_ge(prog.expert_landed[j % RAWS], 16 * (MOE_UNITS // RAWS) * at + 16 * (j // RAWS) + 16)
                if not (isinstance(at, int) and at == 0 and h < RING):
                    act.wait_ge(done, N * at + h - RING + 1)
                act.activation(WHI[:, h % RING, :], RAW[:, j % RAWS, h % 2 * 1024:h % 2 * 1024 + 1024], ACT.Copy).then_inc(w_hi, 1)

            def body(e, last):
                for h in range(N):
                    if not (last and h + RING >= N):
                        split(e, h + RING)
                    if h == 7:
                        act.wait_ge(done, N * e + 8)
                        act.activation(AB[:, 0, :], PS[:, A_SLOT, :], ACT.Copy).then_inc(a_kept, 1)
                    if h == 13:
                        act.wait_ge(turned, 2 * e + 1)
                        act.activation(SIL[:], PS[:, TURN_SLOTS[0], :].rearrange("p (k s) -> p k s", s=P)[:, :, 0:CAPACITY],
                                       ACT.Silu).then_inc(silu, 1)
                    if h == 15:
                        act.wait_ge(done, N * e + 16)
                        act.activation(AB[:, 1, :], PS[:, B_SLOT, :], ACT.Copy).then_inc(b_kept, 1)
                        act.wait_ge(hidden, e + 1)
                        act.activation(HT[:, :, 0:CAPACITY], HS[:], ACT.Copy).then_inc(h_hi, 1)
                act.wait_ge(done, N * e + N)
                act.wait_ge(gated, e + 1)
                act.activation(YH[:], PS[:, Y_SLOT, :], ACT.Copy, scale=gate[:, 0:1]).then_inc(y_hi, 1)
            act.wait_ge(zeroed, 1)
            act.activation(YH[:], AB[:, 0, :], ACT.Copy).then_inc(zeroed, 1)
            act.activation(YL[:], AB[:, 0, :], ACT.Copy).then_inc(zeroed, 1)
            for h in range(RING):
                split(0, h)
            rounds(act, body)

        @block.vector
        def _(dve):
            def split(e, h):
                at, h = (e, h) if h < N else (e + 1, h - N)
                j = h // 2
                dve.wait_ge(w_hi, N * at + h + 1)
                if not (isinstance(at, int) and at == 0 and h < RING):
                    dve.wait_ge(done, N * at + h - RING + 1)
                dve.tensor_tensor(WLO[:, h % RING, :], RAW[:, j % RAWS, h % 2 * 1024:h % 2 * 1024 + 1024],
                                  f32(WHI[:, h % RING, :]), ALU.subtract).then_inc(w_lo, 1)

            def add(e, quarter):
                dve.wait_ge(scattered, 4 * e + quarter + 1)
                dve.tensor_tensor(X[:, 2 * quarter:2 * quarter + 2, 0:LAT],
                                  PS[:, QUARTERS[quarter], :].rearrange("p (k t) -> p k t", k=2),
                                  X[:, 2 * quarter:2 * quarter + 2, 0:LAT], ALU.add).then_inc(added, 1)

            def body(e, last):
                for h in range(N):
                    if not (last and h + RING >= N):
                        split(e, h + RING)
                    if h == 5:
                        add(e, 0)
                    if h == 6:
                        add(e, 1)
                    if h == 13:
                        add(e, 2)
                    if h == 15:
                        add(e, 3)
                        dve.wait_ge(turned, 2 * e + 2)
                        dve.wait_ge(silu, e + 1)
                        dve.tensor_tensor(HS[:], PS[:, TURN_SLOTS[1], :].rearrange("p (k s) -> p k s", s=P)[:, :, 0:CAPACITY],
                                          SIL[:], ALU.mult).then_inc(hidden, 1)
                        dve.wait_ge(h_hi, e + 1)
                        dve.tensor_tensor(HT[:, :, CAPACITY:P], HS[:], f32(HT[:, :, 0:CAPACITY]), ALU.subtract).then_inc(h_lo, 1)
                    if h == 17:
                        dve.wait_ge(rows_landed, 16 * e + 16)
                        dve.tensor_scalar(ST[:], ROWS[:, 0, :], prog.prm("slot"), None, ALU.is_equal).then_inc(hot, 1)
                        dve.wait_ge(hot, e + 2)
                        dve.tensor_tensor_reduce(prod[:], f32(ST[:]), ROWS[:, 1, :], 1.0, 0.0, ALU.mult, ALU.add,
                                                 gate[:, 0:1]).then_inc(gated, 1)
                dve.wait_ge(y_hi, e + 1)
                dve.scalar_tensor_tensor(YL[:], PS[:, Y_SLOT, :], gate[:, 0:1], f32(YH[:]), ALU.mult, ALU.subtract).then_inc(y_lo, 1)
            dve.memset(AB[:, 0, :], 0.0).then_inc(zeroed, 1)
            dve.wait_ge(zeroed, 3)
            dve.tensor_copy(ST[:], AB[:, 0, 0:LAT]).then_inc(hot, 1)
            dve.nop().then_inc(y_lo, 1)
            for h in range(RING):
                split(0, h)
            rounds(dve, body)
            for quarter in range(4):
                add(EXPERTS, quarter)



def build(nc, dram, out):
    prog = Program(nc, dram)
    gemms = {n: Gemm(n, dram[n], k) for n, k in GEMMS}
    order = list(gemms.values())
    for a, b in zip(order, order[1:]):
        b.base, a.next = a.base + a.n, b

    def mod(layer, section):
        m = prog.MOD[layer]
        return lambda u, t: m[:, bass.ds(8 * section + u, 1), t]

    def shift(layer, section):
        return prog.MOD[layer][:, 8 * section:8 * section + 8, :]

    stages = []
    add = lambda name, f: stages.append((name, f))
    add("start", lambda: start(prog, order))
    add("ada", lambda: condition(prog))
    add("norm1", lambda: norm(prog, prog.GAIN[0][0], shift(0, 0), BOTH))
    add("pw1", lambda: gated_projection(prog, gemms["pw1"]))
    add("conv", lambda: depthwise(prog))
    add("ln", lambda: layer_norm_silu(prog))
    add("pw2", lambda: project(prog, gemms["pw2"], prog.XNH, prog.XNL, BOTH, mod(0, 2),
                               lambda u, t: prog.G1B[:, bass.ds(u, 1), t]))
    add("norm2", lambda: norm(prog, prog.GAIN[0][1], shift(0, 3), BOTH))
    for grp in range(2):
        add(f"up0{grp}", lambda grp=grp: ffn_up(prog, gemms[f"up0{grp}"], 0, grp, BOTH))
        add(f"down0{grp}", lambda grp=grp: project(prog, gemms[f"down0{grp}"], prog.HH, prog.HL, BOTH, mod(0, 5)))
    add("norm1_1", lambda: norm(prog, prog.GAIN[1][0], shift(1, 0), BOTH))
    add("qkv", lambda: window_qkv(prog, gemms["qkv"]))
    add("rope", lambda: window_rope(prog))
    add("attn", lambda: window_attention(prog))
    add("wo", lambda: project(prog, gemms["wo"], prog.XNH, prog.XNL, LATENT, mod(1, 2)))
    add("norm2_1", lambda: norm(prog, prog.GAIN[1][1], shift(1, 3), LATENT))
    for grp in range(2):
        add(f"up1{grp}", lambda grp=grp: ffn_up(prog, gemms[f"up1{grp}"], 1, grp, LATENT))
        add(f"down1{grp}", lambda grp=grp: project(prog, gemms[f"down1{grp}"], prog.HH, prog.HL, LATENT, mod(1, 5)))
    add("final_1", lambda: rescale(prog, prog.prm("final_1", 0, 8)))
    add("norm_mix", lambda: norm(prog, prog.prm3("g_mix", 2), None, LATENT))
    add("w_in", lambda: mixing_input(prog, gemms["w_in"]))
    add("fourier", lambda: fourier(prog))
    add("latents", lambda: latents(prog))
    add("mla", lambda: latent_attention(prog))
    add("w_out", lambda: project(prog, gemms["w_out"], prog.XNH, prog.XNL, LATENT))
    add("norm_mem", lambda: norm(prog, prog.prm3("g_mem", 2), None, BOTH))
    add("mem_in", lambda: memory_inputs(prog, gemms))
    add("mem_attn", lambda: memory_attention(prog))
    add("mem_o", lambda: project(prog, gemms["mem_o"], prog.XNH, prog.XNL, LATENT))
    add("norm_moe", lambda: norm(prog, prog.prm3("g_ffn", 2), None, LATENT))
    add("router", lambda: router(prog))
    add("gather", lambda: gather(prog))
    add("moe", lambda: experts(prog))
    add("end", lambda: rescale(prog, prog.prm("final_2", 0, 8), out))
    for _, stage in stages:
        stage()


SCRATCH = {"rows": (EXPERTS, 2, LAT)}

GEMMS = [("pw1", 8), ("pw2", 8), ("up00", 8), ("down00", HID), ("up01", 8), ("down01", HID), ("qkv", 8), ("wo", 8),
         ("up10", 8), ("down10", HID), ("up11", 8), ("down11", HID), ("w_in", 8), ("w_out", 8), ("memq", 8), ("memk", 8), ("memv", 8),
         ("mem_o", 8)]



def units(w):
    k, m = w.shape
    return np.ascontiguousarray(w.reshape(k // P, P, m // P, P).transpose(2, 1, 0, 3).reshape(m // P, P, k))


def columns(v):
    return v.reshape(-1, P).T


def both(a, b):
    return np.stack([a, b], axis=-1).reshape(P, -1)


def pairs(w):
    k, m = w.shape
    return w.reshape(k, 2, m // 2 // P, P).transpose(0, 2, 1, 3).reshape(k, m)


def features(x):
    return x.T.reshape(-1, P, x.shape[0]).transpose(1, 0, 2)


def axial_tables():
    t = np.arange(LAT)
    n = HEAD_DIM // 4
    inv = np.float32(10000.0) ** (-np.arange(n, dtype=np.float32) / np.float32(n))
    row, col = (t // 64).astype(np.float32), (t % 64).astype(np.float32)
    ang = np.concatenate([row[:, None] * inv, col[:, None] * inv], axis=-1).T
    return np.stack([np.tile(np.cos(ang), (4, 1)), np.tile(np.sin(ang), (4, 1))], axis=1).astype(np.float32)


def rotation(size, at, half):
    r = np.zeros((size, size), np.float32)
    for m in range(at, size):
        if (m - at) % (2 * half) < half:
            r[m + half, m] = -1.0
        else:
            r[m - half, m] = 1.0
    return r


def window_order():
    group = HEADS // KV_HEADS
    return [group * (2 * p + half) + j for p in range(2) for j in range(group) for half in range(2)]


def layouts(x, c, ctx, c_ctx, ada_w, ada_b, norm1_g, norm2_g, final_g, conv_w_pw1, conv_b_pw1, conv_w_dw, conv_b_dw,
            conv_ln_g, conv_ln_b, conv_w_pw2, conv_b_pw2, attn_w_qkv, attn_w_o, attn_sink, ffn_w_up, ffn_w_dw, ffn_b_dw,
            ffn_w_down, mem_2, positions_2, g_mix_2, w_in_2, g_q_lat_2, w_q_up_2, g_kv_lat_2, w_kv_up_2, w_fourier_2,
            w_out_2, g_mem_q_2, g_mem_kv_2, w_mem_q_2, w_mem_kv_2, w_mem_o_2, g_ffn_2, w_router_2, w_exp_gate_2,
            w_exp_up_2, w_exp_down_2, g_final_2):
    a = {}
    a["xT"] = np.concatenate([features(x[0]), features(ctx[0])], axis=2)
    a["ada"] = np.concatenate([units(ada_w[0]), units(ada_w[1])])
    a["pw1"] = units(pairs(conv_w_pw1[0]))
    a["pw2"] = units(conv_w_pw2[0])
    for l in range(2):
        up = pairs(ffn_w_up[l])
        for grp in range(2):
            a[f"up{l}{grp}"] = units(up[:, grp * 2 * HID * P:(grp + 1) * 2 * HID * P])
            a[f"down{l}{grp}"] = units(ffn_w_down[l][grp * HID * P:(grp + 1) * HID * P])
    heads = window_order()
    q = attn_w_qkv[0][:, :D].reshape(D, HEADS, HEAD_DIM)[:, heads].reshape(D, D)
    a["qkv"] = np.concatenate([units(q), units(attn_w_qkv[0][:, D:])])
    a["wo"] = units(attn_w_o[0].reshape(HEADS, HEAD_DIM, D)[heads].reshape(D, D))
    a["memT"] = features(mem_2[0])
    a["ident"] = np.eye(P, dtype=np.float32)
    a["axial"] = axial_tables()
    a["rot_head"] = rotation(P, 0, HEAD_DIM // 2)
    r, j = np.mgrid[0:BLOCK, 0:BLOCK]
    a["masks"] = np.stack([np.where(j >= r, 0, NEG), np.where(j <= r, 0, NEG)], axis=1).astype(np.float32)
    prm = {}
    prm["sink"] = np.tile(attn_sink[0][heads], (P, 1))
    prm["final_1"] = columns(final_g)
    for l in range(2):
        prm[f"norm1_{l}"] = both(columns(norm1_g[l]), columns(norm1_g[l]))
        prm[f"norm2_{l}"] = both(columns(norm2_g[l]), columns(norm2_g[l]))
        prm[f"ada_b{l}"] = both(columns(ada_b[l]), columns(ada_b[l]))
        taps = np.stack([columns(pairs(v[None])[0]) for v in (*ffn_w_dw[l], ffn_b_dw[l])], axis=-1)
        prm[f"ffn{l}"] = taps.reshape(P, -1)
    prm["b_pw1"] = columns(pairs(conv_b_pw1)[0])
    prm["w_dw"] = np.stack([columns(v) for v in conv_w_dw[0]], axis=-1).reshape(P, -1)
    prm["b_dw"], prm["ln_g"], prm["ln_b"], prm["b_pw2"] = map(columns, (conv_b_dw[0], conv_ln_g[0], conv_ln_b[0], conv_b_pw2[0]))
    w_in = np.zeros((D, 10 * P), np.float32)
    w_in[:, 0:9 * P] = w_in_2[0][:, 0:9 * P]
    w_in[:, 9 * P + NOPE:9 * P + QK] = w_in_2[0][:, 9 * P:]
    a["w_in"] = units(w_in)
    a["w_out"], a["memq"], a["mem_o"] = units(w_out_2[0]), units(w_mem_q_2[0]), units(w_mem_o_2[0])
    a["memk"], a["memv"] = units(w_mem_kv_2[0][:, :D]), units(w_mem_kv_2[0][:, D:])
    n = np.arange(LAT)
    turn = np.outer(n, n) % LAT * (2 * np.pi / LAT)
    dft = np.stack([np.cos(turn), -np.sin(turn)], axis=1) / np.sqrt(LAT)
    a["dft"] = dft.reshape(LAT // P, P, 2, LAT).transpose(1, 0, 2, 3).astype(np.float32)
    turn = np.outer(n[:64], n[:64]) % 64 * (2 * np.pi / 64)
    a["group_dft"] = np.stack([np.kron(np.eye(2), np.cos(turn)), np.kron(np.eye(2), np.sin(turn))], axis=1).astype(np.float32) / 8
    a["w_fourier"] = np.zeros((P, 4, P), np.float32)
    for grp in range(8):
        h = grp % 2 * 64
        a["w_fourier"][h:h + 64, grp // 2, h:h + 64] = w_fourier_2[0][grp]
    a["rot_rope"] = rotation(QK, NOPE, ROPE // 2)
    a["positions"] = np.tile(positions_2, (QK, 1))
    wq = w_q_up_2[0].reshape(Q_RANK // P, P, MLA_HEADS // 2, 2 * QK)
    wkv = w_kv_up_2[0].reshape(KV_RANK // P, P, MLA_HEADS // 2, 2, NOPE + V_DIM)
    wk = np.zeros(wkv.shape[:4] + (QK,), np.float32)
    wk[..., :NOPE] = wkv[..., :NOPE]
    a["mla"] = np.concatenate([w.transpose(2, 1, 0, *range(3, w.ndim)).reshape(MLA_HEADS // 2, P, -1)
                               for w in (wq, wk, wkv[..., NOPE:])], axis=2)
    a["router"] = np.zeros((P, KD, P), np.float32)
    a["router"][:, :, :EXPERTS] = w_router_2[0].reshape(KD, P, EXPERTS).transpose(1, 0, 2)
    a["iota"] = np.tile(np.arange(1, CAPACITY + 1, dtype=np.float32), (P, 1))
    a["sum2"] = np.tile(np.eye(CAPACITY, dtype=np.float32), (2, 2))
    w = np.stack([w_exp_gate_2[0], w_exp_up_2[0], w_exp_down_2[0]], axis=1)
    a["experts"] = w.reshape(EXPERTS, 3, 2, HALF_K, P, 2, 512).transpose(0, 1, 5, 2, 4, 3, 6).reshape(EXPERTS, MOE_UNITS, P, HALF_K * 512)
    for name, v, w in (("g_mix", g_mix_2, g_mix_2), ("g_mem", g_mem_q_2, g_mem_kv_2), ("g_ffn", g_ffn_2, g_ffn_2)):
        prm[name] = both(columns(v[0]), columns(w[0]))
    prm["g_q"], prm["g_kv"], prm["final_2"] = columns(g_q_lat_2[0]), columns(g_kv_lat_2[0]), columns(g_final_2)
    freq = np.float32(1) / np.float32(10000.0) ** (np.arange(0, ROPE, 2, dtype=np.float32) / np.float32(ROPE))
    prm["freq"] = np.concatenate([np.zeros(NOPE), freq, freq, np.zeros(P - QK)])[:, None]
    prm["slot"] = (np.arange(P) % CAPACITY + 1.0)[:, None]
    prm["cond"] = both(columns(c[0]), columns(c_ctx))
    table = np.zeros((P, N_PARAMS), np.float32)
    for name, v in prm.items():
        at, n = PARAMS[name]
        table[:, at:at + n] = v
    a["params"] = table
    return {k: np.ascontiguousarray(v) for k, v in a.items()}


def kernel(**inputs):
    import concourse.bacc as _bacc
    from concourse.bass_utils import run_bass_kernel_spmd as _run

    nc = _bacc.Bacc("TRN2", target_bir_lowering=False, num_devices=1)
    arrays = layouts(**{name: np.asarray(v) for name, v in inputs.items()})
    dram = {n: nc.dram_tensor(n, a.shape, mybir.dt.from_np(a.dtype), kind="ExternalInput").ap() for n, a in arrays.items()}
    for n, shape in SCRATCH.items():
        dram[n] = nc.dram_tensor(n, shape, F32, kind="Internal").ap()
    out = nc.dram_tensor("out", (P, KD, LAT), F32, kind="ExternalOutput").ap()
    build(nc, dram, out)
    r = _run(nc, [arrays], core_ids=[0]).results[0]["out"]
    return np.ascontiguousarray(r.transpose(2, 1, 0).reshape(1, LAT, D))
```

```python
import math
from contextlib import contextmanager

import numpy as np

import concourse.bass as bass
from concourse import mybir

F32 = mybir.dt.float32
F32R = mybir.dt.float32r
I32 = mybir.dt.int32
ACT = mybir.ActivationFunctionType
ALU = mybir.AluOpType
AX = mybir.AxisListType

P = 128
D = 1024
KD = D // P
HALF_K = KD // 2
LAT, CTX = 512, 256
TOK = LAT + CTX
EPS = 1e-6
CONV_TAPS = 31
PAD = (CONV_TAPS - 1) // 2
LAT_AT, CTX_AT = PAD, PAD + LAT + 2 * PAD
VLEN = CTX_AT + CTX + PAD
CLEN = VLEN - 2 * PAD
CLAT, CCTX = 0, LAT + 2 * PAD
D_FF = 2816
HID = D_FF // P // 2
HEADS, KV_HEADS, HEAD_DIM = 16, 4, 64
BLOCK = 128
NEG = -1e30
SLOT = HID * P
RAWS, SPLITS = 4, 2
STAGE_SEMS = 40
EARLY_CHUNKS = 3
LATENT, BOTH, CONTEXT = [(0, LAT)], [(0, LAT), (LAT, TOK)], [(LAT, TOK)]

PARAMS = {}
_at = 0
for _name, _n in (("norm1_0", 16), ("norm2_0", 16), ("norm1_1", 16), ("norm2_1", 16), ("ada_b0", 96), ("ada_b1", 96),
                  ("b_pw1", 16), ("w_dw", 8 * CONV_TAPS), ("b_dw", 8), ("ln_g", 8), ("ln_b", 8), ("b_pw2", 8),
                  ("ffn0", 44 * 4), ("ffn1", 44 * 4), ("sink", HEADS), ("g_mix", 16), ("g_mem", 16), ("g_ffn", 16),
                  ("g_q", 3), ("g_kv", 2), ("cond", 16), ("final_1", 8), ("freq", 1), ("slot", 1), ("final_2", 8)):
    PARAMS[_name] = (_at, _n)
    _at += _n
N_PARAMS = _at


class Gemm:
    def __init__(self, name, src, k):
        self.name, self.src, self.k = name, src, k
        self.n, self.length = src.shape[0], k * P
        self.base, self.next = 0, None


class Steps:
    def __init__(self, eng, sem, per_round=0):
        self.eng, self.sem, self.per_round = eng, sem, per_round
        self.base, self.n = 0, 0

    def round(self, i):
        self.base, self.n = self.per_round * i, 0

    def did(self, instruction):
        instruction.then_inc(self.sem, 1)
        self.n += 1

    def wait(self):
        self.eng.wait_ge(self.sem, self.base + self.n)


class Program:
    def __init__(self, nc, dram):
        self.nc, self.dram = nc, dram
        self.stage_no = 0
        self.stage_sems = []
        nc_sem = nc.alloc_semaphore
        self.raw_landed = [nc_sem(f"raw_landed{i}") for i in range(RAWS)]
        self.weights_hi = nc_sem("weights_hi")
        self.weights_lo = nc_sem("weights_lo")
        self.unit_done = nc_sem("unit_done")
        self.x_landed = nc_sem("x_landed")
        self.expert_landed = [nc_sem(f"expert_landed{i}") for i in range(RAWS)]
        first = self.expert_landed[-1].num + 1
        self.banks = [first, first + STAGE_SEMS]
        base = (nc.sbuf_base + 63) // 64 * 64
        self.top = nc.sbuf_usable_end // 64 * 64
        self.small = base
        self.small_end = base + 8192
        at = self.small_end
        self.X = self.at("X", [P, KD, TOK], F32, at)
        self.XNH = self.at("XNH", [P, KD, TOK], F32R, at + 24576)
        self.XNL = self.at("XNL", [P, KD, TOK], F32R, at + 2 * 24576)
        at += 3 * 24576
        self.RAW = self.at("RAW", [P, RAWS, SLOT], F32, at)
        at += RAWS * SLOT * 4
        self.WHI = self.at("WHI", [P, SPLITS, SLOT], F32R, at)
        at += SPLITS * SLOT * 4
        self.WLO = self.at("WLO", [P, SPLITS, SLOT], F32R, at)
        at += SPLITS * SLOT * 4
        self.arena = at
        self.tmp = at + 2 * HID * TOK * 4
        self.PRM = self.keep("PRM", [P, N_PARAMS], F32)
        self.ONES = self.keep("ONES", [P, P], F32)
        self.EPSC = self.keep("EPSC", [P, 1], F32)
        self.WARM, self.warmed = self.keep("WARM", [P, 8], F32), 0
        self.IDENT = self.keep("IDENT", [P, P], F32)
        self.MOD = [self.keep(f"MOD{l}", [P, 48, 2], F32) for l in range(2)]
        self.GAIN = [[self.keep(f"GAIN{l}{n}", [P, KD, 2], F32) for n in range(2)] for l in range(2)]
        self.G1B = self.keep("G1B", [P, KD, 2], F32)
        self.SC = self.keep("SC", [P, KD, 2], F32)
        self.PS = nc.alloc_psum_tensor("PS", [P, 4, 1024], F32)

    def at(self, name, shape, dtype, offset):
        size = 4 * math.prod(shape[1:])
        assert offset % 32 == 0 and offset + size <= self.top, (name, offset, size, self.top)
        return self.nc.alloc_sbuf_tensor_at(name, shape, dtype, offset=offset)

    def keep(self, name, shape, dtype):
        t = self.at(name, shape, dtype, self.small)
        self.small += (4 * math.prod(shape[1:]) + 31) // 32 * 32
        assert self.small <= self.small_end, (name, self.small - self.small_end)
        return t

    def use_table_of(self, act, function):
        act.activation(self.WARM[:, self.warmed:self.warmed + 1], self.EPSC[:], function)
        self.warmed += 1

    def region(self, start, end):
        return Region(self, start, end)

    def sem(self, name):
        s = self.nc.alloc_semaphore(f"{name}_{self.stage_no}", num=self.banks[self.stage_no % 2] + len(self.stage_sems))
        self.stage_sems.append(s)
        assert len(self.stage_sems) <= STAGE_SEMS
        return s

    @contextmanager
    def block(self, name):
        with self.nc.Block(f"{name}{self.stage_no}") as block:
            yield block
        self.nc.clear_and_free_semaphores(self.stage_sems)
        self.stage_sems = []
        self.stage_no += 1

    def prm(self, name, index=0, n=1):
        a = PARAMS[name][0]
        return self.PRM[:, bass.ds(a + index, n)]

    def prm3(self, name, width):
        a, n = PARAMS[name]
        return self.PRM[:, a:a + n].rearrange("p (k w) -> p k w", w=width)


class Region:
    def __init__(self, prog, start, end):
        self.prog, self.at_, self.end = prog, (start + 31) // 32 * 32, end

    def take(self, name, shape, dtype=F32):
        t = self.prog.at(f"{name}_{self.prog.stage_no}", shape, dtype, self.at_)
        self.at_ += (4 * math.prod(shape[1:]) + 31) // 32 * 32
        assert self.at_ <= self.end, (name, self.at_ - self.end)
        return t


def f32(ap):
    return ap.bitcast(F32)



def run_units(eng, n, step):
    rounds = max((n - 4) // 4, 0)
    if rounds > 1:
        with eng.Fori(0, rounds) as i:
            for s in range(4):
                step(i, s)
    elif rounds == 1:
        for s in range(4):
            step(0, s)
    for u in range(4 * rounds, n):
        step(u // 4, u % 4)


def ahead(g, i, s, by):
    if isinstance(i, int) and 4 * i + s + by >= g.n:
        if g.next is None:
            return None, None
        return g.next, 4 * i + s + by - g.n
    return g, 4 * i + s + by


def load_ahead(prog, sp, g, i, s):
    to, u = ahead(g, i, s, RAWS)
    if to is None:
        return
    slot = (g.base + s) % RAWS
    sp.wait_ge(prog.weights_lo, g.base + 4 * i + s + 1)
    sp.dma_start(prog.RAW[:, slot, 0:to.length], to.src[u]).then_inc(prog.raw_landed[slot], 16)


def split_hi_ahead(prog, act, g, i, s):
    to, _ = ahead(g, i, s, SPLITS)
    if to is None:
        return
    at = g.base + s + SPLITS
    act.wait_ge(prog.raw_landed[at % RAWS], 16 * (i + at // RAWS + 1))
    act.wait_ge(prog.unit_done, g.base + 4 * i + s + 1)
    act.activation(prog.WHI[:, at % SPLITS, 0:to.length], prog.RAW[:, at % RAWS, 0:to.length],
                   ACT.Copy).then_inc(prog.weights_hi, 1)


def split_lo_ahead(prog, dve, g, i, s):
    to, _ = ahead(g, i, s, SPLITS)
    if to is None:
        return
    at = g.base + s + SPLITS
    dve.wait_ge(prog.weights_hi, g.base + 4 * i + s + SPLITS + 1)
    dve.wait_ge(prog.unit_done, g.base + 4 * i + s + 1)
    dve.tensor_tensor(prog.WLO[:, at % SPLITS, 0:to.length], prog.RAW[:, at % RAWS, 0:to.length],
                      f32(prog.WHI[:, at % SPLITS, 0:to.length]), ALU.subtract).then_inc(prog.weights_lo, 1)


def multiply(prog, pe, g, i, s, xh, xl, segments, psum_free):
    slot = (g.base + s) % SPLITS
    pe.wait_ge(prog.weights_lo, g.base + 4 * i + s + 1)
    pe.wait_ge(psum_free, 4 * i + s + 1)
    last = None
    for k in range(g.k):
        wh = prog.WHI[:, slot, k * P:(k + 1) * P]
        wl = prog.WLO[:, slot, k * P:(k + 1) * P]
        for n, (w, x) in enumerate(((wh, xh), (wh, xl), (wl, xh))):
            for a, b in segments:
                last = pe.matmul(prog.PS[:, s, a:b], w, x[:, k, a:b], start=(k == 0 and n == 0),
                                 stop=(k == g.k - 1 and n == 2))
    last.then_inc(prog.unit_done, 1)


def multiply_all(prog, pe, g, xh, xl, segments, psum_free, before, wait=lambda i, s: None):
    def step(i, s):
        wait(i, s)
        multiply(prog, pe, g, i, s, xh, xl, segments(4 * i + s), psum_free)
    if before is None:
        run_units(pe, g.n, step)
        return
    for s in range(2):
        pe.wait_ge(prog.weights_lo, g.base + s + 1)
        wait(0, s)
        pe.wait_ge(psum_free, s + 1)
    for k in range(g.k):
        pe.wait_ge(before.lo, k + 1)
        for s in range(2):
            slot = (g.base + s) % SPLITS
            wh, wl = (w[:, slot, k * P:(k + 1) * P] for w in (prog.WHI, prog.WLO))
            for n, (w, x) in enumerate(((wh, xh), (wh, xl), (wl, xh))):
                for a, b in segments(s):
                    last = pe.matmul(prog.PS[:, s, a:b], w, x[:, k, a:b], start=(k == 0 and n == 0),
                                     stop=(k == g.k - 1 and n == 2))
            if k == g.k - 1:
                last.then_inc(prog.unit_done, 1)
    rounds = max((g.n - 4) // 4, 0)
    for s in range(2, 4):
        step(0, s)
    if rounds > 1:
        with pe.Fori(1, rounds) as i:
            for s in range(4):
                step(i, s)
    for u in range(4 * max(rounds, 1), g.n):
        step(u // 4, u % 4)



def start(prog):
    loaded, consts, silu = prog.sem("loaded"), prog.sem("consts"), prog.sem("silu")
    with prog.block("start") as block:
        @block.sync
        def _(sp):
            sp.dma_start(prog.PRM[:], prog.dram["params"]).then_inc(loaded, 16)
            sp.dma_start(prog.IDENT[:], prog.dram["ident"]).then_inc(loaded, 16)

        @block.scalar
        def _(act):
            act.wait_ge(loaded, 32)
            act.activation(prog.SC[:], prog.prm3("cond", 2), ACT.Silu).then_inc(silu, 1)

        @block.vector
        def _(dve):
            dve.memset(prog.ONES[:], 1.0 / D).then_inc(consts, 1)
            dve.memset(prog.EPSC[:], EPS).then_inc(consts, 1)


ADA_RING = 4
ADA_SLICES = 6 * D // 512


class Ada:
    def __init__(self, prog, first, end, ring, rows):
        self.prog, self.first, self.rounds = prog, first, (end - first) // 2
        self.ring, self.rows = ring, rows
        self.src = prog.dram["ada"]
        self.landed = [prog.sem(f"ada_landed{s}") for s in range(ADA_RING)]
        self.used, self.kept, self.turned = prog.sem("ada_used"), prog.sem("ada_kept"), prog.sem("ada_turned")
        self.step = prog.sem("ada_step")

    def load(self, sp):
        at = 2 * self.first
        for s in range(ADA_RING):
            sp.dma_start(self.ring[:, s, :], self.src[at + s]).then_inc(self.landed[s], 16)
        with sp.Fori(1, self.rounds) as i:
            for s in range(ADA_RING):
                sp.wait_ge(self.used, ADA_RING * i - ADA_RING + s + 1)
                sp.dma_start(self.ring[:, s, :], self.src[at + ADA_RING * i + s]).then_inc(self.landed[s], 16)

    def multiply(self, pe):
        prog, PS = self.prog, self.prog.PS
        pe.nop().then_inc(self.kept, 2)
        with pe.Fori(0, self.rounds) as i:
            for b in range(2):
                pe.wait_ge(self.kept, 2 * i + b + 1)
                for half in range(2):
                    pe.wait_ge(self.landed[2 * b + half], 16 * i + 16)
                    for k in range(HALF_K):
                        last = pe.matmul(PS[0:2, b, 0:512], prog.SC[:, HALF_K * half + k, :],
                                         self.ring[:, 2 * b + half, k * 512:(k + 1) * 512],
                                         start=(half == 0 and k == 0), stop=(half == 1 and k == HALF_K - 1))
                    last.then_inc(self.used, 1)
            for b in range(2):
                pe.wait_ge(self.kept, 2 + 2 * i + b + 1)
                for c in range(4):
                    last = pe.matmul(PS[:, 2, bass.ds(8 * self.first + 16 * i + 8 * b + 2 * c, 2)],
                                     self.rows[0:2, b, c * P:(c + 1) * P], prog.IDENT[0:2, 0:2], start=True, stop=True)
                last.then_inc(self.turned, 1)

    def keep(self, act):
        act.nop().then_inc(self.turned, 2)
        with act.Fori(0, self.rounds) as i:
            for b in range(2):
                act.wait_ge(self.used, 4 * i + 2 * b + 2)
                act.wait_ge(self.turned, 2 * i + b + 1)
                act.activation(self.rows[0:2, b, :], self.prog.PS[0:2, b, 0:512], ACT.Copy).then_inc(self.kept, 1)

    def finish(self, dve, parts, gains):
        prog = self.prog
        step = Steps(dve, self.step)
        dve.wait_ge(self.turned, 2 + 2 * self.rounds)
        for l, a, b in parts:
            bias = PARAMS[f"ada_b{l}"][0]
            step.did(dve.tensor_tensor(prog.MOD[l][:, 8 * a:8 * b, :].rearrange("p a b -> p (a b)"),
                                       prog.PS[:, 2, 96 * l + 16 * a:96 * l + 16 * b],
                                       prog.PRM[:, bias + 16 * a:bias + 16 * b], ALU.add))
        step.wait()
        for l, n in gains:
            step.did(dve.scalar_tensor_tensor(prog.GAIN[l][n][:], prog.MOD[l][:, 24 * n + 8:24 * n + 16, :], 1.0,
                                              prog.prm3(f"norm{n + 1}_{l}", 2), ALU.add, ALU.mult))
        if (0, 2, 6) in parts:
            for t in range(2):
                step.did(dve.tensor_tensor(prog.G1B[:, :, t], prog.MOD[0][:, 16:24, t], prog.prm("b_pw2", 0, 8), ALU.mult))
        return step


def condition(prog, first):
    with prog.block("ada") as block:
        reg = prog.region(prog.arena, prog.tmp)
        ada = Ada(prog, 0, 4, reg.take("ADAW", [P, ADA_RING, 4 * 512]), reg.take("ADAR", [2, 2, 512]))

        @block.sync
        def _(sp):
            ada.load(sp)
            sp.dma_start(prog.X[:], prog.dram["xT"]).then_inc(prog.x_landed, 16)
            for u in range(RAWS):
                sp.dma_start(prog.RAW[:, u, 0:first.length], first.src[u]).then_inc(prog.raw_landed[u], 16)
            sp.wait_ge(prog.x_landed, 16)

        @block.tensor
        def _(pe):
            ada.multiply(pe)

        @block.scalar
        def _(act):
            ada.keep(act)
            for u in range(SPLITS):
                act.wait_ge(prog.raw_landed[u], 16)
                act.activation(prog.WHI[:, u, 0:first.length], prog.RAW[:, u, 0:first.length],
                               ACT.Copy).then_inc(prog.weights_hi, 1)

        @block.vector
        def _(dve):
            ada.finish(dve, [(0, 0, 2)], [(0, 0)]).wait()
            for u in range(SPLITS):
                dve.wait_ge(prog.weights_hi, u + 1)
                dve.tensor_tensor(prog.WLO[:, u, 0:first.length], prog.RAW[:, u, 0:first.length],
                                  f32(prog.WHI[:, u, 0:first.length]), ALU.subtract).then_inc(prog.weights_lo, 1)


class Norm:
    def __init__(self, prog, gain, shift, segments):
        self.prog, self.gain, self.shift, self.segments = prog, gain, shift, segments
        self.tok = tok = segments[-1][1]
        self.out_hi, self.out_lo = prog.XNH, prog.XNL
        reg = prog.region(prog.tmp, prog.top)
        self.sq = reg.take("SQ", [P, 2, tok])
        self.scaled = reg.take("SCALED", [P, 2, tok])
        self.rstd = reg.take("RSTD", [P, tok])
        self.mean = prog.PS[:, 0, 0:tok]
        self.squared, self.summed, self.root = prog.sem("squared"), prog.sem("summed"), prog.sem("root")
        self.rstd_done, self.normed, self.full = prog.sem("rstd"), prog.sem("normed"), prog.sem("full")
        self.hi, self.lo = prog.sem("hi"), prog.sem("lo")

    def on_scalar(self, act):
        for k in range(KD):
            if k >= 2:
                act.wait_ge(self.summed, k - 1)
            act.activation(self.sq[:, k % 2, :], self.prog.X[:, k, 0:self.tok], ACT.Square).then_inc(self.squared, 1)
        act.wait_ge(self.summed, KD)
        act.activation(self.rstd[:], self.mean, ACT.Sqrt, bias=self.prog.EPSC[:, 0:1]).then_inc(self.root, 1)
        for k in range(KD):
            act.wait_ge(self.normed, k + 1)
            if k >= 2:
                act.wait_ge(self.lo, k - 1)
            for t, (a, b) in enumerate(self.segments):
                ins = act.activation(self.scaled[:, k % 2, a:b], self.sq[:, k % 2, a:b], ACT.Identity,
                                     bias=0.0 if self.shift is None else self.shift[:, k, t:t + 1], scale=self.gain[:, k, t:t + 1])
            ins.then_inc(self.full, 1)
            act.wait_ge(self.full, k + 1)
            act.activation(self.out_hi[:, k, 0:self.tok], self.scaled[:, k % 2, :], ACT.Copy).then_inc(self.hi, 1)

    def on_tensor(self, pe):
        for k in range(KD):
            pe.wait_ge(self.squared, k + 1)
            for a, b in self.segments:
                last = pe.matmul(self.mean[:, a:b], self.prog.ONES[:], self.sq[:, k % 2, a:b], start=(k == 0), stop=(k == KD - 1))
            last.then_inc(self.summed, 1)

    def on_vector(self, dve):
        dve.wait_ge(self.root, 1)
        dve.reciprocal(self.rstd[:], self.rstd[:]).then_inc(self.rstd_done, 1)
        dve.wait_ge(self.rstd_done, 1)
        for k in range(KD + 1):
            if k < KD:
                if k >= 2:
                    dve.wait_ge(self.full, k - 1)
                dve.tensor_tensor(self.sq[:, k % 2, :], self.prog.X[:, k, 0:self.tok], self.rstd[:], ALU.mult).then_inc(self.normed, 1)
            if k >= 1:
                dve.wait_ge(self.hi, k)
                dve.tensor_tensor(self.out_lo[:, k - 1, 0:self.tok], self.scaled[:, (k - 1) % 2, :],
                                  f32(self.out_hi[:, k - 1, 0:self.tok]), ALU.subtract).then_inc(self.lo, 1)


def norm(prog, gain, shift, segments):
    with prog.block("norm") as block:
        n = Norm(prog, gain, shift, segments)

        @block.scalar
        def _(act):
            n.on_scalar(act)

        @block.tensor
        def _(pe):
            n.on_tensor(pe)

        @block.vector
        def _(dve):
            n.on_vector(dve)


def conv_tap(prog, dve, steps, chunk, tap, others=0):
    v = prog.V[:, chunk, tap:tap + CLEN]
    w = prog.prm("w_dw", chunk * CONV_TAPS + tap)
    out = prog.C[:, chunk, :]
    if tap == 0:
        steps.did(dve.tensor_scalar(out, v, w, prog.prm("b_dw", chunk), ALU.mult, ALU.add))
    else:
        dve.wait_ge(steps.sem, steps.base + steps.n - others)
        steps.did(dve.scalar_tensor_tensor(out, v, w, out, ALU.mult, ALU.add))


def gated_convolution(prog, g, before):
    with prog.block("pw1") as block:
        before = before()
        reg = prog.region(prog.arena, prog.tmp)
        V = prog.V = reg.take("V", [P, KD, VLEN])
        C = prog.C = reg.take("C", [P, KD, CLEN])
        tmp = prog.region(prog.tmp, prog.top)
        sig = tmp.take("SIG", [P, 2, TOK])
        psum_free, sigmoid, gated, padded = prog.sem("psum_free"), prog.sem("sigmoid"), prog.sem("gated"), prog.sem("pad")
        tap_done, late_tap = prog.sem("tap_done"), prog.sem("late_tap")
        ring = prog.at("ADAW_2", [P, ADA_RING, 4 * 512], F32, prog.small_end + 2 * 24576 - 8192)
        ada = Ada(prog, 4, 2 * ADA_SLICES, ring, tmp.take("ADAR", [2, 2, 512]))

        @block.sync
        def _(sp):
            run_units(sp, g.n, lambda i, s: load_ahead(prog, sp, g, i, s))
            sp.wait_ge(prog.unit_done, g.base + g.n)
            ada.load(sp)

        @block.scalar
        def _(act):
            before.on_scalar(act)
            prog.use_table_of(act, ACT.Sigmoid)
            def step(i, s):
                split_hi_ahead(prog, act, g, i, s)
                if s % 2 == 0:
                    return
                act.wait_ge(prog.unit_done, g.base + 4 * i + s + 1)
                act.wait_ge(gated, 2 * i + s // 2 + 1)
                act.activation(sig[:, s // 2, :], prog.PS[:, s, 0:TOK], ACT.Sigmoid,
                               bias=prog.prm("b_pw1", 4 * i + s)).then_inc(sigmoid, 1)
            run_units(act, g.n, step)
            ada.keep(act)

        @block.vector
        def _(dve):
            dve.nop().then_inc(gated, 2)
            before.on_vector(dve)
            for a, b in ((0, LAT_AT), (LAT_AT + LAT, CTX_AT), (CTX_AT + CTX, VLEN)):
                dve.memset(V[:, :, a:b], 0.0).then_inc(padded, 1)

            def step(i, s):
                split_lo_ahead(prog, dve, g, i, s)
                if s % 2 == 0:
                    return
                dve.wait_ge(sigmoid, 2 * i + s // 2 + 1)
                for (a, b), at in zip(BOTH, (LAT_AT, CTX_AT)):
                    ins = dve.scalar_tensor_tensor(V[:, 2 * i + s // 2, at:at + b - a], prog.PS[:, s - 1, a:b],
                                                   prog.prm("b_pw1", 4 * i + s - 1), sig[:, s // 2, a:b], ALU.add, ALU.mult)
                ins.then_inc(gated, 1)

            taps = Steps(dve, tap_done, CONV_TAPS)

            def round_with_taps(i):
                taps.round(i - 1)
                for s in range(4):
                    step(i, s)
                    for tap in range(8 * s, min(8 * s + 8, CONV_TAPS)):
                        if tap == 0:
                            dve.wait_ge(gated, 2 + 2 * i - 1)
                            dve.wait_ge(padded, 3)
                        conv_tap(prog, dve, taps, i - 1, tap)
            for s in range(4):
                step(0, s)
            with dve.Fori(1, EARLY_CHUNKS) as i:
                round_with_taps(i)
            round_with_taps(EARLY_CHUNKS)
            late = Steps(dve, late_tap, 2 * CONV_TAPS)
            dve.wait_ge(gated, 2 + g.n // 2)
            with dve.Fori(0, (KD - EARLY_CHUNKS) // 2) as i:
                late.round(i)
                for tap in range(CONV_TAPS):
                    for c in range(2):
                        conv_tap(prog, dve, late, EARLY_CHUNKS + 2 * i + c, tap, 1)
            late.round((KD - EARLY_CHUNKS) // 2)
            for tap in range(CONV_TAPS):
                conv_tap(prog, dve, late, KD - 1, tap)
            ada.finish(dve, [(0, 2, 6), (1, 0, 6)], [(0, 1), (1, 0), (1, 1)]).wait()

        @block.tensor
        def _(pe):
            def wait(i, s):
                if s % 2 == 0:
                    pe.wait_ge(gated, 2 * i + s // 2 + 1)
            before.on_tensor(pe)
            pe.nop().then_inc(psum_free, g.n)
            multiply_all(prog, pe, g, prog.XNH, prog.XNL, lambda u: BOTH, psum_free, before, wait)
            pe.wait_ge(gated, 2 + g.n // 2)
            ada.multiply(pe)


class LayerNormSilu:
    def __init__(self, prog):
        self.prog = prog
        reg = prog.region(prog.tmp, prog.top)
        self.tmp = reg.take("TMP", [P, 2, TOK])
        self.full = reg.take("FULL", [P, 2, TOK])
        self.rstd = reg.take("RSTD", [P, TOK])
        self.spans = [(0, LAT, CLAT), (LAT, TOK, CCTX)]
        self.mean, self.var = prog.PS[:, 0, 0:TOK], prog.PS[:, 1, 0:TOK]
        self.summed, self.centred, self.squared = prog.sem("summed"), prog.sem("centred"), prog.sem("squared")
        self.sq_summed, self.root, self.rstd_done = prog.sem("sq_summed"), prog.sem("root"), prog.sem("rstd")
        self.normed, self.act_full = prog.sem("normed"), prog.sem("full")
        self.hi, self.lo = prog.sem("hi"), prog.sem("lo")

    def on_scalar(self, act):
        for k in range(KD):
            act.wait_ge(self.centred, k + 1)
            if k >= 2:
                act.wait_ge(self.sq_summed, k - 1)
            for a, b, at in self.spans:
                ins = act.activation(self.tmp[:, k % 2, a:b], self.prog.C[:, k, at:at + b - a], ACT.Square)
            ins.then_inc(self.squared, 1)
        act.wait_ge(self.sq_summed, KD)
        act.activation(self.rstd[:], self.var, ACT.Sqrt, bias=self.prog.EPSC[:, 0:1]).then_inc(self.root, 1)
        for k in range(KD):
            act.wait_ge(self.normed, k + 1)
            if k >= 2:
                act.wait_ge(self.lo, k - 1)
            act.activation(self.full[:, k % 2, :], self.tmp[:, k % 2, :], ACT.Silu, bias=self.prog.prm("ln_b", k),
                           scale=self.prog.prm("ln_g", k)).then_inc(self.act_full, 1)
            act.wait_ge(self.act_full, k + 1)
            act.activation(self.prog.XNH[:, k, :], self.full[:, k % 2, :], ACT.Copy).then_inc(self.hi, 1)

    def on_tensor(self, pe):
        for k in range(KD):
            for a, b, at in self.spans:
                last = pe.matmul(self.mean[:, a:b], self.prog.ONES[:], self.prog.C[:, k, at:at + b - a], start=(k == 0), stop=(k == KD - 1))
        last.then_inc(self.summed, 1)
        for k in range(KD):
            pe.wait_ge(self.squared, k + 1)
            for a, b in BOTH:
                last = pe.matmul(self.var[:, a:b], self.prog.ONES[:], self.tmp[:, k % 2, a:b], start=(k == 0), stop=(k == KD - 1))
            last.then_inc(self.sq_summed, 1)

    def on_vector(self, dve):
        dve.wait_ge(self.summed, 1)
        for k in range(KD):
            for a, b, at in self.spans:
                ins = dve.tensor_tensor(self.prog.C[:, k, at:at + b - a], self.prog.C[:, k, at:at + b - a], self.mean[:, a:b], ALU.subtract)
            ins.then_inc(self.centred, 1)
        dve.wait_ge(self.root, 1)
        dve.reciprocal(self.rstd[:], self.rstd[:]).then_inc(self.rstd_done, 1)
        dve.wait_ge(self.rstd_done, 1)
        for k in range(KD + 1):
            if k < KD:
                if k >= 2:
                    dve.wait_ge(self.act_full, k - 1)
                for a, b, at in self.spans:
                    ins = dve.tensor_tensor(self.tmp[:, k % 2, a:b], self.prog.C[:, k, at:at + b - a], self.rstd[:, a:b], ALU.mult)
                ins.then_inc(self.normed, 1)
            if k >= 1:
                dve.wait_ge(self.hi, k)
                dve.tensor_tensor(self.prog.XNL[:, k - 1, :], self.full[:, (k - 1) % 2, :], f32(self.prog.XNH[:, k - 1, :]),
                                  ALU.subtract).then_inc(self.lo, 1)


def project(prog, g, xh, xl, segments, gate=None, bias=None, before=None):
    with prog.block(g.name) as block:
        before = before and before()
        psum_free = prog.sem("psum_free")
        if bias is not None:
            tmp = prog.region(prog.tmp, prog.top).take("SCALED", [P, 2, TOK])
            scaled = prog.sem("scaled")

        @block.sync
        def _(sp):
            run_units(sp, g.n, lambda i, s: load_ahead(prog, sp, g, i, s))

        @block.scalar
        def _(act):
            def step(i, s):
                split_hi_ahead(prog, act, g, i, s)
                if bias is not None:
                    act.wait_ge(prog.unit_done, g.base + 4 * i + s + 1)
                    act.wait_ge(psum_free, 4 * i + s + 3)
                    for t, (a, b) in enumerate(segments):
                        ins = act.activation(tmp[:, s % 2, a:b], prog.PS[:, s, a:b], ACT.Identity,
                                             bias=bias(4 * i + s, t), scale=gate(4 * i + s, t))
                    ins.then_inc(scaled, 1)
            if before is not None:
                before.on_scalar(act)
            run_units(act, g.n, step)

        @block.vector
        def _(dve):
            def step(i, s):
                split_lo_ahead(prog, dve, g, i, s)
                u = 4 * i + s
                if bias is not None:
                    dve.wait_ge(scaled, u + 1)
                    a, b = segments[0][0], segments[-1][1]
                    dve.tensor_tensor(prog.X[:, u, a:b], tmp[:, s % 2, a:b], prog.X[:, u, a:b], ALU.add).then_inc(psum_free, 1)
                    return
                dve.wait_ge(prog.unit_done, g.base + u + 1)
                for t, (a, b) in enumerate(segments):
                    if gate is None:
                        ins = dve.tensor_tensor(prog.X[:, u, a:b], prog.PS[:, s, a:b], prog.X[:, u, a:b], ALU.add)
                    else:
                        ins = dve.scalar_tensor_tensor(prog.X[:, u, a:b], prog.PS[:, s, a:b], gate(u, t),
                                                       prog.X[:, u, a:b], ALU.mult, ALU.add)
                ins.then_inc(psum_free, 1)
            if before is not None:
                before.on_vector(dve)
            run_units(dve, g.n, step)

        @block.tensor
        def _(pe):
            if before is not None:
                before.on_tensor(pe)
            pe.nop().then_inc(psum_free, 4)
            multiply_all(prog, pe, g, xh, xl, lambda u: segments, psum_free, before)


def ffn_up(prog, g, layer, group, segments, before=None):
    tok = segments[-1][1]
    with prog.block("up") as block:
        before = before and before()
        reg = prog.region(prog.arena, prog.tmp)
        HH = prog.HH = reg.take("HH", [P, HID, TOK], F32R)
        HL = prog.HL = reg.take("HL", [P, HID, TOK], F32R)
        Y = prog.region(prog.tmp, prog.top).take("Y", [P, 4, tok])
        psum_free, centre, silu, hidden = prog.sem("psum_free"), prog.sem("centre"), prog.sem("silu"), prog.sem("hidden")
        hid_hi, y_free, tap = prog.sem("hid_hi"), prog.sem("y_free"), prog.sem("tap")

        def coef(i, s, n):
            return prog.prm(f"ffn{layer}", (2 * HID * group + 4 * i + s) * 4 + n)

        @block.sync
        def _(sp):
            run_units(sp, g.n, lambda i, s: load_ahead(prog, sp, g, i, s))

        @block.scalar
        def _(act):
            def step(i, s):
                split_hi_ahead(prog, act, g, i, s)
                u, j = 4 * i + s, 2 * i + s // 2
                act.wait_ge(prog.unit_done, g.base + u + 1)
                act.wait_ge(y_free, j + 1)
                act.activation(Y[:, s, :], prog.PS[:, s, 0:tok], ACT.Identity, bias=coef(i, s, 3),
                               scale=coef(i, s, 1)).then_inc(centre, 1)
                if s % 2 == 1:
                    act.wait_ge(psum_free, 4 + u)
                    act.activation(Y[:, s - 1, :], Y[:, s - 1, :], ACT.Silu).then_inc(silu, 1)
                    act.wait_ge(hidden, j + 1)
                    act.activation(HH[:, j, 0:tok], Y[:, s, :], ACT.Copy).then_inc(hid_hi, 1)
            if before is not None:
                before.on_scalar(act)
            prog.use_table_of(act, ACT.Silu)
            run_units(act, g.n, step)

        @block.vector
        def _(dve):
            dve.nop().then_inc(y_free, 2)
            dve.nop().then_inc(psum_free, 4)

            def step(i, s):
                split_lo_ahead(prog, dve, g, i, s)
                u, j = 4 * i + s, 2 * i + s // 2
                dve.wait_ge(centre, u + 1)
                for a, b in segments:
                    ins = dve.scalar_tensor_tensor(Y[:, s, a + 1:b], prog.PS[:, s, a:b - 1], coef(i, s, 0),
                                                   Y[:, s, a + 1:b], ALU.mult, ALU.add)
                ins.then_inc(tap, 1)
                dve.wait_ge(tap, u + 1)
                for a, b in segments:
                    ins = dve.scalar_tensor_tensor(Y[:, s, a:b - 1], prog.PS[:, s, a + 1:b], coef(i, s, 2),
                                                   Y[:, s, a:b - 1], ALU.mult, ALU.add)
                ins.then_inc(psum_free, 1)
                if s % 2 == 1:
                    dve.wait_ge(silu, j + 1)
                    dve.wait_ge(psum_free, 4 + u + 1)
                    dve.tensor_tensor(Y[:, s, :], Y[:, s - 1, :], Y[:, s, :], ALU.mult).then_inc(hidden, 1)
                    dve.wait_ge(hid_hi, j + 1)
                    dve.tensor_tensor(HL[:, j, 0:tok], Y[:, s, :], f32(HH[:, j, 0:tok]), ALU.subtract).then_inc(y_free, 1)
            if before is not None:
                before.on_vector(dve)
            run_units(dve, g.n, step)

        @block.tensor
        def _(pe):
            if before is not None:
                before.on_tensor(pe)
            multiply_all(prog, pe, g, prog.XNH, prog.XNL, lambda u: segments, psum_free, before)


def collect(prog, g, segments_of, dest_of, loads=(), before=None):
    with prog.block(g.name) as block:
        before = before and before()
        psum_free, loaded = prog.sem("psum_free"), prog.sem("loaded")

        @block.sync
        def _(sp):
            for to, src in loads:
                sp.dma_start(to, src).then_inc(loaded, 16)
            run_units(sp, g.n, lambda i, s: load_ahead(prog, sp, g, i, s))
            if loads:
                sp.wait_ge(loaded, 16 * len(loads))

        @block.scalar
        def _(act):
            def step(i, s):
                split_hi_ahead(prog, act, g, i, s)
                u = 4 * i + s
                a, b = segments_of(u)[0][0], segments_of(u)[-1][1]
                act.wait_ge(prog.unit_done, g.base + u + 1)
                act.activation(dest_of(u), prog.PS[:, s, a:b], ACT.Copy).then_inc(psum_free, 1)
            if before is not None:
                before.on_scalar(act)
            run_units(act, g.n, step)

        @block.vector
        def _(dve):
            if before is not None:
                before.on_vector(dve)
            run_units(dve, g.n, lambda i, s: split_lo_ahead(prog, dve, g, i, s))

        @block.tensor
        def _(pe):
            if before is not None:
                before.on_tensor(pe)
            pe.nop().then_inc(psum_free, 4)
            multiply_all(prog, pe, g, prog.XNH, prog.XNL, segments_of, psum_free, before)


def window_qkv(prog, g, before):
    reg = prog.attn = prog.region(prog.arena, prog.top)
    QT = prog.QT = reg.take("QT", [P, KD, LAT])
    KT = prog.KT = reg.take("KT", [P, 2, TOK])
    V = prog.VF = reg.take("VF", [P, 2, TOK])
    prog.VT = reg.take("VT", [P, TOK // P, KV_HEADS * HEAD_DIM])
    prog.AXIAL = reg.take("AXIAL", [P, 2, LAT])
    prog.MASKS = reg.take("MASKS", [P, 2, BLOCK])
    prog.ROT = reg.take("ROT", [P, P])

    def kind(u):
        return u if isinstance(u, int) and u >= KD else 0

    def dest(u):
        if kind(u) == 0:
            return QT[:, u, :]
        return KT[:, u - KD, :] if u < KD + 2 else V[:, u - KD - 2, :]

    collect(prog, g, lambda u: BOTH if kind(u) else LATENT, dest, [(prog.AXIAL[:], prog.dram["axial"]), (prog.MASKS[:], prog.dram["masks"]), (prog.ROT[:], prog.dram["rot_head"])], before)


def window_rope(prog):
    with prog.block("rope") as block:
        reg = prog.region(prog.attn.at_, prog.top)
        part = reg.take("PART", [P, 2, LAT])
        turned = reg.take("TURNED", [P, 2, LAT])
        v_turned, v_kept = prog.sem("v_turned"), prog.sem("v_kept")
        rotated, cosined, sined, summed = prog.sem("rotated"), prog.sem("cosined"), prog.sem("sined"), prog.sem("summed")
        tiles = [prog.QT[:, k, :] for k in range(KD)] + [prog.KT[:, k, 0:LAT] for k in range(2)]

        @block.tensor
        def _(pe):
            for n, t in enumerate(tiles):
                if n >= 4:
                    pe.wait_ge(sined, n - 3)
                pe.matmul(prog.PS[:, n % 4, 0:LAT], prog.ROT[:], t, start=True, stop=True).then_inc(rotated, 1)
            for c in range(TOK // P):
                if c >= 4:
                    pe.wait_ge(v_kept, c - 3)
                for h in range(2):
                    last = pe.transpose(prog.PS[:, c % 4, LAT + h * P:LAT + (h + 1) * P], prog.VF[:, h, c * P:(c + 1) * P],
                                        prog.IDENT[:])
                last.then_inc(v_turned, 1)

        @block.scalar
        def _(act):
            for c in range(TOK // P):
                act.wait_ge(v_turned, c + 1)
                act.activation(prog.VT[:, c, :], prog.PS[:, c % 4, LAT:LAT + 2 * P], ACT.Copy).then_inc(v_kept, 1)

        @block.gpsimd
        def _(pool):
            for n, t in enumerate(tiles):
                if n >= 2:
                    pool.wait_ge(summed, n - 1)
                pool.tensor_tensor(part[:, n % 2, :], t, prog.AXIAL[:, 0, :], ALU.mult).then_inc(cosined, 1)

        @block.vector
        def _(dve):
            for n, t in enumerate(tiles):
                dve.wait_ge(rotated, n + 1)
                if n >= 2:
                    dve.wait_ge(summed, n - 1)
                dve.tensor_tensor(turned[:, n % 2, :], prog.PS[:, n % 4, 0:LAT], prog.AXIAL[:, 1, :],
                                  ALU.mult).then_inc(sined, 1)
                dve.wait_ge(cosined, n + 1)
                dve.wait_ge(sined, n + 1)
                dve.tensor_tensor(t, part[:, n % 2, :], turned[:, n % 2, :], ALU.add).then_inc(summed, 1)


def window_attention(prog):
    with prog.block("attn") as block:
        reg = prog.region(prog.attn.at_, prog.top)
        QS = reg.take("QS", [P, 2, 2, LAT])
        probs = reg.take("PROBS", [P, 2, 640])
        probsT = reg.take("PROBST", [P, 2, 640])
        stats = reg.take("STATS", [P, 2, 8])
        nsink = reg.take("NSINK", [P, HEADS])
        scale = HEAD_DIM ** -0.5
        NB = LAT // BLOCK
        UNITS = 2 * NB
        PS = prog.PS
        staged, scored, bias_ready, exped = prog.sem("staged"), prog.sem("scored"), prog.sem("bias"), prog.sem("exped")
        sunk, normed, turned, copied = prog.sem("sunk"), prog.sem("normed"), prog.sem("turned"), prog.sem("copied")
        cleared = prog.sem("cleared")
        attended, out_hi, out_free, step = prog.sem("attended"), prog.sem("out_hi"), prog.sem("out_free"), prog.sem("step")

        def keys(b):
            return [kb for kb in (b - 1, b, b + 1) if 0 <= kb < NB]

        def width(n):
            return CTX + BLOCK * len(keys(n % NB))

        def each_tile(eng, body):
            for p in range(2):
                with eng.Fori(0, NB // 2) as i:
                    for buf in range(2):
                        body(p, NB * p + 2 * i + buf, buf)

        @block.gpsimd
        def _(pool):
            def body(p, t, buf):
                pool.wait_ge(attended, t + 1)
                for half in range(2):
                    rows = slice(64 * half, 64 * half + 64)
                    ins = pool.tensor_copy(QS[rows, buf, half, :], prog.QT[rows, t, :])
                ins.then_inc(staged, 1)
            pool.memset(QS[:], 0.0).then_inc(cleared, 1)
            pool.wait_ge(cleared, 1)
            each_tile(pool, body)

        @block.tensor
        def _(pe):
            pe.nop().then_inc(attended, 2)
            pe.nop().then_inc(exped, 2)
            pe.nop().then_inc(copied, 1)
            pe.nop().then_inc(out_free, 1)
            pe.nop().then_inc(turned, 2)

            def scores(p, t, n, buf):
                half, b = n // NB, n % NB
                q = QS[:, buf, half, b * BLOCK:(b + 1) * BLOCK]
                k = prog.KT[:, p, :]
                S = PS[:, n % 2, :]
                kb = keys(b)
                pe.wait_ge(exped, UNITS * t + n + 1)
                pe.matmul(S[:, 0:CTX], q, k[:, LAT:TOK], start=True, stop=True)
                near = kb[:2]
                pe.matmul(S[:, CTX:CTX + 2 * BLOCK], q, k[:, near[0] * BLOCK:(near[0] + 2) * BLOCK], start=True, stop=False)
                m = 0 if near[0] < b else 1
                last = pe.matmul(S[:, CTX + m * BLOCK:CTX + (m + 1) * BLOCK], prog.IDENT[:], prog.MASKS[:, m, :],
                                 start=False, stop=True)
                if len(kb) == 3:
                    pe.matmul(S[:, 512:640], q, k[:, kb[2] * BLOCK:(kb[2] + 1) * BLOCK], start=True, stop=False)
                    last = pe.matmul(S[:, 512:640], prog.IDENT[:], prog.MASKS[:, 1, :], start=False, stop=True)
                last.then_inc(scored, 1)
                return last

            def transposes(t, n):
                pe.wait_ge(normed, UNITS * t + n + 1)
                pe.wait_ge(copied, UNITS * t + n + 1)
                for c in range(width(n) // P):
                    last = pe.transpose(PS[:, 2, c * P:(c + 1) * P], probs[:, n % 2, c * P:(c + 1) * P], prog.IDENT[:])
                last.then_inc(turned, 1)

            def values(p, t, n):
                half, b = n // NB, n % NB
                chunks = [NB, NB + 1] + keys(b)
                g = 2 * p + half
                if n == 0:
                    pe.wait_ge(out_free, t + 1)
                pe.wait_ge(copied, 1 + UNITS * t + n + 1)
                for c, v in enumerate(chunks):
                    last = pe.matmul(PS[64 * half:64 * half + 64, 3, b * BLOCK:(b + 1) * BLOCK],
                                     prog.VT[:, v, g * HEAD_DIM:(g + 1) * HEAD_DIM], probsT[:, n % 2, c * P:(c + 1) * P],
                                     start=(c == 0), stop=(c == len(chunks) - 1))
                return last

            def body(p, t, buf):
                pe.wait_ge(staged, t + 1)
                scores(p, t, 0, buf)
                scores(p, t, 1, buf)
                for n in range(UNITS):
                    transposes(t, n)
                    if n + 2 < UNITS:
                        scores(p, t, n + 2, buf)
                    last = values(p, t, n)
                last.then_inc(attended, 1)
            each_tile(pe, body)

        @block.vector
        def _(dve):
            steps = Steps(dve, step, 3 * UNITS)
            dve.tensor_scalar(nsink[:], prog.prm("sink", 0, HEADS), -1.0, None, ALU.mult).then_inc(sunk, 1)
            dve.wait_ge(sunk, 1)

            def maxima(t, n):
                dve.wait_ge(scored, UNITS * t + n + 1)
                st = stats[:, n % 2, :]
                steps.did(dve.reduce_max(st[:, 0:1], PS[:, n % 2, 0:width(n)], AX.X))
                steps.wait()
                dve.tensor_scalar(st[:, 1:2], st[:, 0:1], -scale, nsink[:, bass.ds(2 * t + n // NB, 1)], ALU.mult,
                                  ALU.min).then_inc(bias_ready, 1)

            def normalise(t, n):
                st = stats[:, n % 2, :]
                dve.wait_ge(exped, 2 + UNITS * t + n + 1)
                dve.wait_ge(sunk, 1 + UNITS * t + n + 1)
                steps.did(dve.tensor_tensor(st[:, 4:5], st[:, 2:3], st[:, 3:4], ALU.add))
                steps.wait()
                steps.did(dve.reciprocal(st[:, 5:6], st[:, 4:5]))
                steps.wait()
                dve.tensor_scalar(probs[:, n % 2, 0:width(n)], probs[:, n % 2, 0:width(n)], st[:, 5:6], None,
                                  ALU.mult).then_inc(normed, 1)

            def body(p, t, buf):
                steps.round(t)
                for n in range(UNITS):
                    maxima(t, n)
                    normalise(t, n)
                assert steps.n == steps.per_round
                dve.wait_ge(out_hi, t + 1)
                dve.tensor_tensor(prog.XNL[:, t, 0:LAT], PS[:, 3, 0:LAT], f32(prog.XNH[:, t, 0:LAT]),
                                  ALU.subtract).then_inc(out_free, 1)
            each_tile(dve, body)

        @block.scalar
        def _(act):
            def exponentials(t, n):
                st = stats[:, n % 2, :]
                act.wait_ge(bias_ready, UNITS * t + n + 1)
                act.wait_ge(turned, UNITS * t + n + 1)
                act.activation(probs[:, n % 2, 0:width(n)], PS[:, n % 2, 0:width(n)], ACT.Exp, bias=st[:, 1:2], scale=scale,
                               accum_out=st[:, 2:3]).then_inc(exped, 1)
                act.activation(st[:, 3:4], st[:, 1:2], ACT.Exp,
                               bias=prog.prm("sink", 2 * t + n // NB)).then_inc(sunk, 1)

            def copy(t, n):
                act.wait_ge(turned, 2 + UNITS * t + n + 1)
                act.activation(probsT[:, n % 2, 0:width(n)], PS[:, 2, 0:width(n)], ACT.Copy).then_inc(copied, 1)

            def body(p, t, buf):
                exponentials(t, 0)
                exponentials(t, 1)
                for n in range(UNITS):
                    copy(t, n)
                    if n + 2 < UNITS:
                        exponentials(t, n + 2)
                act.wait_ge(attended, 2 + t + 1)
                act.activation(prog.XNH[:, t, 0:LAT], PS[:, 3, 0:LAT], ACT.Copy).then_inc(out_hi, 1)
            each_tile(act, body)


def rescale(prog, gain, out=None):
    with prog.block("final") as block:
        reg = prog.region(prog.tmp, prog.top)
        sq = reg.take("SQ", [P, 2, LAT])
        rstd = reg.take("RSTD", [P, LAT])
        mean = prog.PS[:, 0, 0:LAT]
        squared, summed, root, scaled = prog.sem("squared"), prog.sem("summed"), prog.sem("root"), prog.sem("scaled")
        loaded, rescaled = prog.sem("loaded"), prog.sem("rescaled")

        @block.sync
        def _(sp):
            if out is None:
                sp.dma_start(prog.X[:, :, LAT:TOK], prog.dram["memT"]).then_inc(loaded, 16)
                sp.wait_ge(loaded, 16)
                return
            for k in range(0, KD, 2):
                sp.wait_ge(rescaled, k + 2)
                sp.dma_start(out[:, k:k + 2, :], prog.X[:, k:k + 2, 0:LAT]).then_inc(loaded, 16)
            sp.wait_ge(loaded, 16 * KD // 2)

        @block.scalar
        def _(act):
            for k in range(KD):
                if k >= 2:
                    act.wait_ge(summed, k - 1)
                act.activation(sq[:, k % 2, :], prog.X[:, k, 0:LAT], ACT.Square).then_inc(squared, 1)
            act.wait_ge(summed, KD)
            act.activation(rstd[:], mean, ACT.Sqrt, bias=prog.EPSC[:, 0:1]).then_inc(root, 1)

        @block.tensor
        def _(pe):
            for k in range(KD):
                pe.wait_ge(squared, k + 1)
                pe.matmul(mean, prog.ONES[:], sq[:, k % 2, :], start=(k == 0), stop=(k == KD - 1)).then_inc(summed, 1)

        @block.vector
        def _(dve):
            dve.wait_ge(root, 1)
            dve.reciprocal(rstd[:], rstd[:]).then_inc(scaled, 1)
            dve.wait_ge(scaled, 1)
            for k in range(KD):
                dve.scalar_tensor_tensor(prog.X[:, k, 0:LAT], prog.X[:, k, 0:LAT], gain[:, k:k + 1], rstd[:], ALU.mult,
                                         ALU.mult).then_inc(rescaled, 1)



MLA_HEADS, NOPE, ROPE, V_DIM = 8, 64, 32, 64
QK = NOPE + ROPE
Q_RANK, KV_RANK = 384, 256
MLA_PAIR = 2 * (Q_RANK // P * QK + KV_RANK // P * (QK + V_DIM))
MEM_HEADS, MEM_DIM = 4, 256
EXPERTS, CAPACITY = 16, 64
TWO_PI = (6.28125, 0.0019350051879882812, float(2 * np.pi - 6.28125 - 0.0019350051879882812))
SIN_LIMIT = 3.1415925


def mixing_input(prog, g, before):
    reg = prog.mix = prog.region(prog.arena, prog.top)
    UT = prog.UT = reg.take("UT", [P, g.n, LAT])
    prog.KRR = reg.take("KRR", [P, LAT])
    prog.COS = reg.take("COS", [P, LAT])
    prog.SIN = reg.take("SIN", [P, LAT])
    prog.ROT_ROPE = reg.take("ROTROPE", [P, QK])
    prog.mix_end = reg.at_
    prog.POS = reg.take("POS", [P, LAT], I32)
    prog.GROUP_DFT = reg.take("GROUPDFT", [P, 2, P])
    prog.WF = reg.take("WF", [P, 4, P])
    prog.DFT = reg.take("DFT", [P, LAT // P, 2, LAT])
    prog.fourier_at = reg.at_
    collect(prog, g, lambda u: LATENT, lambda u: UT[:, u, :], loads=[
        (prog.ROT_ROPE[0:QK, :], prog.dram["rot_rope"]), (prog.POS[0:QK, :], prog.dram["positions"]),
        (prog.GROUP_DFT[:], prog.dram["group_dft"]), (prog.WF[:], prog.dram["w_fourier"]),
        (prog.DFT[:], prog.dram["dft"])], before=before)


def fourier(prog):
    with prog.block("fourier") as block:
        reg = prog.region(prog.fourier_at, prog.top)
        M = reg.take("M", [P, 4, 2, P])
        PT = reg.take("PT", [P, LAT // P, 4, 2, P])
        PS = prog.PS
        mixed, m_kept = prog.sem("mixed"), prog.sem("m_kept")
        projected, p_kept = prog.sem("projected"), prog.sem("p_kept")
        summed, hi, lo = prog.sem("summed"), prog.sem("hi"), prog.sem("lo")
        slots = [1, 2, 3, 0]

        @block.tensor
        def _(pe):
            for c in range(4):
                for n in range(2):
                    last = pe.matmul(PS[:, 0, (2 * c + n) * P:(2 * c + n + 1) * P], prog.GROUP_DFT[:, n, :],
                                     prog.WF[:, c, :], start=True, stop=True)
            last.then_inc(mixed, 1)
            pe.wait_ge(m_kept, 1)
            for t in range(LAT // P):
                for c in range(4):
                    last = pe.matmul(PS[:, slots[t], c * 2 * P:(c + 1) * 2 * P], prog.UT[:, c, t * P:(t + 1) * P],
                                     M[:, c, :, :].rearrange("p a b -> p (a b)"), start=True, stop=True)
                last.then_inc(projected, 1)
            for c in range(4):
                pe.wait_ge(p_kept, LAT // P)
                for t in range(LAT // P):
                    for n in range(2):
                        last = pe.matmul(PS[:, c, 0:LAT], PT[:, t, c, n, :], prog.DFT[:, t, n, :],
                                         start=(t == 0 and n == 0), stop=(t == LAT // P - 1 and n == 1))
                last.then_inc(summed, 1)

        @block.scalar
        def _(act):
            act.wait_ge(mixed, 1)
            act.activation(M[:].rearrange("p a b c -> p (a b c)"), PS[:, 0, :], ACT.Copy).then_inc(m_kept, 1)
            for t in range(LAT // P):
                act.wait_ge(projected, t + 1)
                act.activation(PT[:, t, :, :, :].rearrange("p a b c -> p (a b c)"), PS[:, slots[t], :],
                               ACT.Copy).then_inc(p_kept, 1)
            for c in range(4):
                act.wait_ge(summed, c + 1)
                act.activation(prog.XNH[:, c, 0:LAT], PS[:, c, 0:LAT], ACT.Copy).then_inc(hi, 1)

        @block.vector
        def _(dve):
            for c in range(4):
                dve.wait_ge(hi, c + 1)
                dve.tensor_tensor(prog.XNL[:, c, 0:LAT], PS[:, c, 0:LAT], f32(prog.XNH[:, c, 0:LAT]),
                                  ALU.subtract).then_inc(lo, 1)


def latents(prog):
    with prog.block("latents") as block:
        reg = prog.region(prog.fourier_at, prog.top)
        sq = reg.take("SQ", [P, 5, LAT])
        rstd = reg.take("RSTD", [P, 2, LAT])
        ang = reg.take("ANG", [P, LAT])
        turns = reg.take("TURNS", [P, LAT])
        whole = reg.take("WHOLE", [P, LAT], I32)
        wrap = reg.take("WRAP", [P, 2, LAT])
        arg = reg.take("ARG", [P, 2, LAT])
        U, PS = prog.UT, prog.PS
        squared, summed, root, done = prog.sem("squared"), prog.sem("summed"), prog.sem("root"), prog.sem("done")
        args_ready, tables, turned = prog.sem("args"), prog.sem("tables"), prog.sem("turned")
        parts = [(0, 3, Q_RANK, "g_q"), (3, 5, KV_RANK, "g_kv")]
        r = slice(0, QK)

        @block.scalar
        def _(act):
            act.activation(sq[:], U[:, 4:9, :], ACT.Square).then_inc(squared, 1)
            act.wait_ge(summed, 1)
            for n, (a, b, rank, _) in enumerate(parts):
                ins = act.activation(rstd[:, n, :], PS[:, n, 0:LAT], ACT.Sqrt, bias=prog.EPSC[:, 0:1], scale=D / rank)
            ins.then_inc(root, 1)
            act.wait_ge(args_ready, 1)
            act.activation(prog.SIN[r, :], arg[r, 0, :], ACT.Sin)
            act.activation(prog.COS[r, :], arg[r, 1, :], ACT.Sin).then_inc(tables, 1)

        @block.tensor
        def _(pe):
            pe.wait_ge(squared, 1)
            for n, (a, b, _, _) in enumerate(parts):
                for k in range(a, b):
                    last = pe.matmul(PS[:, n, 0:LAT], prog.ONES[:], sq[:, k, :], start=(k == a), stop=(k == b - 1))
            last.then_inc(summed, 1)
            pe.matmul(PS[r, 2, 0:LAT], prog.ROT_ROPE[r, :], U[r, 9, :], start=True, stop=True).then_inc(turned, 1)

        @block.vector
        def _(dve):
            step = Steps(dve, done)

            def then(instruction):
                step.did(instruction)
                step.wait()
            then(dve.tensor_copy(turns[r, :], prog.POS[r, :]))
            then(dve.tensor_scalar(ang[r, :], turns[r, :], prog.prm("freq")[r, :], None, ALU.mult))
            then(dve.tensor_scalar(whole[r, :], ang[r, :], 1 / (2 * math.pi), None, ALU.mult))
            then(dve.tensor_copy(turns[r, :], whole[r, :]))
            for part in TWO_PI:
                then(dve.scalar_tensor_tensor(ang[r, :], turns[r, :], -part, ang[r, :], ALU.mult, ALU.add))
            dve.tensor_copy(arg[r, 0, :], ang[r, :])
            then(dve.tensor_scalar(arg[r, 1, :], ang[r, :], math.pi / 2, None, ALU.add))
            for compare, by in ((ALU.is_gt, -2 * math.pi), (ALU.is_lt, 2 * math.pi)):
                then(dve.tensor_scalar(wrap[r, :, :], arg[r, :, :], math.pi if by < 0 else -math.pi, by, compare, ALU.mult))
                then(dve.tensor_tensor(arg[r, :, :], arg[r, :, :], wrap[r, :, :], ALU.add))
            dve.tensor_scalar(arg[r, :, :], arg[r, :, :], SIN_LIMIT, -SIN_LIMIT, ALU.min, ALU.max).then_inc(args_ready, 1)
            dve.wait_ge(root, 1)
            then(dve.reciprocal(rstd[:], rstd[:]))
            for n, (a, b, _, gain) in enumerate(parts):
                for k in range(a, b):
                    dve.scalar_tensor_tensor(U[:, 4 + k, :], U[:, 4 + k, :], prog.prm(gain, k - a), rstd[:, n, :],
                                             ALU.mult, ALU.mult)
            dve.wait_ge(tables, 1)
            dve.wait_ge(turned, 1)
            step.did(dve.tensor_tensor(turns[r, :], PS[r, 2, 0:LAT], prog.SIN[r, :], ALU.mult))
            then(dve.tensor_tensor(ang[r, :], U[r, 9, :], prog.COS[r, :], ALU.mult))
            then(dve.tensor_tensor(prog.KRR[r, :], turns[r, :], ang[r, :], ALU.add))


def latent_attention(prog):
    with prog.block("mla") as block:
        reg = prog.region(prog.mix_end, prog.top)
        W = reg.take("W", [P, MLA_PAIR])
        nq, nkv = Q_RANK // P, KV_RANK // P
        WQ = W[:, 0:nq * 2 * QK].rearrange("p (k m) -> p k m", m=2 * QK)
        WK = W[:, nq * 2 * QK:(nq + nkv) * 2 * QK].rearrange("p (k m) -> p k m", m=2 * QK)
        WV = W[:, (nq + nkv) * 2 * QK:].rearrange("p (k m) -> p k m", m=2 * V_DIM)
        QS, QC, QR, KS, TS = (reg.take(n, [P, 2, LAT]) for n in ("QS", "QC", "QR", "KS", "TS"))
        VS = reg.take("VS", [P, LAT // P, 2 * V_DIM])
        probs, probsT = reg.take("PROBS", [P, 2, LAT]), reg.take("PROBST", [P, 2, LAT])
        stats = reg.take("STATS", [P, 2, 8])
        scale = QK ** -0.5
        NB = LAT // BLOCK
        UNITS, PAIRS = 2 * NB, MLA_HEADS // 2
        U, PS = prog.UT, prog.PS
        r = slice(0, QK)
        w_landed, q_made, k_made, v_made = (prog.sem(n) for n in ("w_landed", "q_made", "k_made", "v_made"))
        q_kept, k_kept, v_kept, rotated = (prog.sem(n) for n in ("q_kept", "k_kept", "v_kept", "rotated"))
        cosined, sined, roped = prog.sem("cosined"), prog.sem("sined"), prog.sem("roped")
        scored, bias_ready, exped, normed = (prog.sem(n) for n in ("scored", "bias", "exped", "normed"))
        turned, copied, attended = prog.sem("turned"), prog.sem("copied"), prog.sem("attended")
        out_hi, out_free, step = prog.sem("out_hi"), prog.sem("out_free"), prog.sem("step")

        def two(slot):
            return PS[r, slot, :].rearrange("p (h t) -> p h t", h=2)

        @block.sync
        def _(sp):
            sp.dma_start(W[:], prog.dram["mla"][0]).then_inc(w_landed, 16)
            with sp.Fori(1, PAIRS) as p:
                sp.wait_ge(v_made, p)
                sp.dma_start(W[:], prog.dram["mla"][p]).then_inc(w_landed, 16)

        @block.gpsimd
        def _(pool):
            with pool.Fori(0, PAIRS) as p:
                pool.wait_ge(q_kept, p + 1)
                pool.wait_ge(roped, p + 1)
                pool.tensor_tensor(QC[r, :, :], QS[r, :, :], prog.COS[r, :].unsqueeze(1).to_broadcast([QK, 2, LAT]),
                                   ALU.mult).then_inc(cosined, 1)

        @block.tensor
        def _(pe):
            pe.nop().then_inc(exped, 2)
            pe.nop().then_inc(copied, 1)
            pe.nop().then_inc(out_free, 1)
            pe.nop().then_inc(turned, 2)

            def scores(p, n):
                h, b = n // NB, n % NB
                pe.wait_ge(exped, UNITS * p + n + 1)
                pe.matmul(PS[:, n % 2, 0:LAT], QR[r, h, b * BLOCK:(b + 1) * BLOCK], KS[r, h, :], start=True,
                          stop=True).then_inc(scored, 1)

            def transposes(p, n):
                pe.wait_ge(normed, UNITS * p + n + 1)
                pe.wait_ge(copied, UNITS * p + n + 1)
                for c in range(LAT // P):
                    last = pe.transpose(PS[:, 2, c * P:(c + 1) * P], probs[:, n % 2, c * P:(c + 1) * P], prog.IDENT[:])
                last.then_inc(turned, 1)

            def values(p, n):
                h, b = n // NB, n % NB
                pe.wait_ge(copied, 1 + UNITS * p + n + 1)
                for c in range(LAT // P):
                    last = pe.matmul(PS[64 * h:64 * h + 64, 3, b * BLOCK:(b + 1) * BLOCK], VS[:, c, h * V_DIM:(h + 1) * V_DIM],
                                     probsT[:, n % 2, c * P:(c + 1) * P], start=(c == 0), stop=(c == LAT // P - 1))
                return last

            with pe.Fori(0, PAIRS) as p:
                pe.wait_ge(w_landed, 16 * p + 16)
                pe.wait_ge(exped, 2 + UNITS * p)
                pe.wait_ge(copied, 1 + UNITS * p)
                for h in range(2):
                    for k in range(nq):
                        last = pe.matmul(two(0)[:, h, :], WQ[:, k, h * QK:(h + 1) * QK], U[:, 4 + k, :], start=(k == 0),
                                         stop=(k == nq - 1))
                last.then_inc(q_made, 1)
                for h in range(2):
                    for k in range(nkv):
                        last = pe.matmul(two(1)[:, h, :], WK[:, k, h * QK:(h + 1) * QK], U[:, 7 + k, :], start=(k == 0),
                                         stop=(k == nkv - 1))
                last.then_inc(k_made, 1)
                for t in range(LAT // P):
                    for k in range(nkv):
                        last = pe.matmul(PS[:, 2, t * P:(t + 1) * P], U[:, 7 + k, t * P:(t + 1) * P], WV[:, k, :],
                                         start=(k == 0), stop=(k == nkv - 1))
                last.then_inc(v_made, 1)
                pe.wait_ge(q_kept, p + 1)
                pe.wait_ge(out_free, p + 1)
                for h in range(2):
                    last = pe.matmul(two(3)[:, h, :], prog.ROT_ROPE[r, :], QS[r, h, :], start=True, stop=True)
                last.then_inc(rotated, 1)
                pe.wait_ge(roped, 1 + p + 1)
                pe.wait_ge(k_kept, p + 1)
                pe.wait_ge(v_kept, p + 1)
                scores(p, 0)
                scores(p, 1)
                for n in range(UNITS):
                    transposes(p, n)
                    if n + 2 < UNITS:
                        scores(p, n + 2)
                    last = values(p, n)
                last.then_inc(attended, 1)

        @block.vector
        def _(dve):
            steps = Steps(dve, step, 2 * UNITS)
            dve.nop().then_inc(roped, 1)

            def maxima(p, n):
                dve.wait_ge(scored, UNITS * p + n + 1)
                st = stats[:, n % 2, :]
                steps.did(dve.reduce_max(st[:, 0:1], PS[:, n % 2, 0:LAT], AX.X))
                steps.wait()
                dve.wait_ge(exped, UNITS * p + n + 1)
                dve.tensor_scalar(st[:, 1:2], st[:, 0:1], -scale, None, ALU.mult).then_inc(bias_ready, 1)

            def normalise(p, n):
                st = stats[:, n % 2, :]
                dve.wait_ge(exped, 2 + UNITS * p + n + 1)
                steps.did(dve.reciprocal(st[:, 3:4], st[:, 2:3]))
                steps.wait()
                dve.tensor_scalar(probs[:, n % 2, :], probs[:, n % 2, :], st[:, 3:4], None, ALU.mult).then_inc(normed, 1)

            with dve.Fori(0, PAIRS) as p:
                steps.round(p)
                dve.wait_ge(k_made, p + 1)
                dve.tensor_tensor(KS[r, :, :], two(1), prog.KRR[r, :].unsqueeze(1).to_broadcast([QK, 2, LAT]),
                                  ALU.add).then_inc(k_kept, 1)
                dve.wait_ge(rotated, p + 1)
                dve.tensor_tensor(TS[r, :, :], two(3), prog.SIN[r, :].unsqueeze(1).to_broadcast([QK, 2, LAT]),
                                  ALU.mult).then_inc(sined, 1)
                dve.wait_ge(sined, p + 1)
                dve.wait_ge(cosined, p + 1)
                dve.tensor_tensor(QR[r, :, :], TS[r, :, :], QC[r, :, :], ALU.add).then_inc(roped, 1)
                for n in range(UNITS):
                    maxima(p, n)
                    normalise(p, n)
                assert steps.n == steps.per_round
                dve.wait_ge(out_hi, p + 1)
                dve.tensor_tensor(prog.XNL[:, 4 + p, 0:LAT], PS[:, 3, 0:LAT], f32(prog.XNH[:, 4 + p, 0:LAT]),
                                  ALU.subtract).then_inc(out_free, 1)

        @block.scalar
        def _(act):
            def exponentials(p, n):
                st = stats[:, n % 2, :]
                act.wait_ge(bias_ready, UNITS * p + n + 1)
                act.wait_ge(turned, UNITS * p + n + 1)
                act.activation(probs[:, n % 2, :], PS[:, n % 2, 0:LAT], ACT.Exp, bias=st[:, 1:2], scale=scale,
                               accum_out=st[:, 2:3]).then_inc(exped, 1)

            def copy(p, n):
                act.wait_ge(turned, 2 + UNITS * p + n + 1)
                act.activation(probsT[:, n % 2, :], PS[:, 2, 0:LAT], ACT.Copy).then_inc(copied, 1)

            with act.Fori(0, PAIRS) as p:
                act.wait_ge(q_made, p + 1)
                act.wait_ge(roped, p + 1)
                act.activation(QS[r, :, :], two(0), ACT.Copy).then_inc(q_kept, 1)
                act.wait_ge(v_made, p + 1)
                act.activation(VS[:].rearrange("p a b -> p (a b)"), PS[:, 2, 0:LAT], ACT.Copy).then_inc(v_kept, 1)
                exponentials(p, 0)
                exponentials(p, 1)
                for n in range(UNITS):
                    copy(p, n)
                    if n + 2 < UNITS:
                        exponentials(p, n + 2)
                act.wait_ge(attended, p + 1)
                act.activation(prog.XNH[:, 4 + p, 0:LAT], PS[:, 3, 0:LAT], ACT.Copy).then_inc(out_hi, 1)


def memory_attention(prog):
    with prog.block("mem") as block:
        reg = prog.region(prog.memory_at, prog.top)
        QS = reg.take("QS", [P, 2, LAT])
        VF, VS = reg.take("VF", [P, 2, CTX]), reg.take("VS", [P, 2, MEM_DIM])
        probs, probsT = reg.take("PROBS", [P, 2, CTX]), reg.take("PROBST", [P, 2, CTX])
        stats = reg.take("STATS", [P, 2, 8])
        scale = MEM_DIM ** -0.5
        NB = LAT // BLOCK
        PS = prog.PS
        staged, scored, bias_ready, exped, normed = (prog.sem(n) for n in ("staged", "scored", "bias", "exped", "normed"))
        v_turned, v_kept = prog.sem("v_turned"), prog.sem("v_kept")
        turned, copied, attended = prog.sem("turned"), prog.sem("copied"), prog.sem("attended")
        out_hi, out_free, step = prog.sem("out_hi"), prog.sem("out_free"), prog.sem("step")
        out = PS[:, 3, :].rearrange("p (d t) -> p d t", d=2)

        @block.gpsimd
        def _(pool):
            with pool.Fori(0, MEM_HEADS) as h:
                pool.wait_ge(attended, h + 1)
                pool.tensor_copy(VF[:], prog.VM[:, bass.ds(2 * h, 2), :]).then_inc(staged, 1)
                pool.tensor_copy(QS[:], prog.QM[:, bass.ds(2 * h, 2), :]).then_inc(staged, 1)

        @block.tensor
        def _(pe):
            pe.nop().then_inc(attended, 1)
            pe.nop().then_inc(exped, 2)
            pe.nop().then_inc(copied, 1)
            pe.nop().then_inc(out_free, 1)
            pe.nop().then_inc(turned, 2)

            def scores(h, b):
                pe.wait_ge(exped, NB * h + b + 1)
                for d in range(2):
                    last = pe.matmul(PS[:, b % 2, 0:CTX], QS[:, d, b * BLOCK:(b + 1) * BLOCK], prog.KM[:, 2 * h + d, :],
                                     start=(d == 0), stop=(d == 1))
                last.then_inc(scored, 1)

            def transposes(h, b):
                pe.wait_ge(normed, NB * h + b + 1)
                pe.wait_ge(copied, NB * h + b + 1)
                if b == 0:
                    pe.wait_ge(v_kept, h + 1)
                for c in range(CTX // P):
                    last = pe.transpose(PS[:, 2, c * P:(c + 1) * P], probs[:, b % 2, c * P:(c + 1) * P], prog.IDENT[:])
                last.then_inc(turned, 1)

            def values(h, b):
                if b == 0:
                    pe.wait_ge(out_free, h + 1)
                pe.wait_ge(copied, 1 + NB * h + b + 1)
                for d in range(2):
                    for c in range(CTX // P):
                        last = pe.matmul(out[:, d, b * BLOCK:(b + 1) * BLOCK], VS[:, c, d * P:(d + 1) * P],
                                         probsT[:, b % 2, c * P:(c + 1) * P], start=(c == 0), stop=(c == CTX // P - 1))
                return last

            with pe.Fori(0, MEM_HEADS) as h:
                pe.wait_ge(staged, 2 * h + 1)
                pe.wait_ge(copied, 1 + NB * h)
                for c in range(CTX // P):
                    for d in range(2):
                        last = pe.transpose(PS[:, 2, (2 * c + d) * P:(2 * c + d + 1) * P], VF[:, d, c * P:(c + 1) * P],
                                            prog.IDENT[:])
                last.then_inc(v_turned, 1)
                pe.wait_ge(staged, 2 * h + 2)
                scores(h, 0)
                scores(h, 1)
                for b in range(NB):
                    transposes(h, b)
                    if b + 2 < NB:
                        scores(h, b + 2)
                    last = values(h, b)
                last.then_inc(attended, 1)

        @block.vector
        def _(dve):
            steps = Steps(dve, step, 2 * NB)

            def maxima(h, b):
                dve.wait_ge(scored, NB * h + b + 1)
                st = stats[:, b % 2, :]
                steps.did(dve.reduce_max(st[:, 0:1], PS[:, b % 2, 0:CTX], AX.X))
                steps.wait()
                dve.wait_ge(exped, NB * h + b + 1)
                dve.tensor_scalar(st[:, 1:2], st[:, 0:1], -scale, None, ALU.mult).then_inc(bias_ready, 1)

            def normalise(h, b):
                st = stats[:, b % 2, :]
                dve.wait_ge(exped, 2 + NB * h + b + 1)
                steps.did(dve.reciprocal(st[:, 3:4], st[:, 2:3]))
                steps.wait()
                dve.tensor_scalar(probs[:, b % 2, :], probs[:, b % 2, :], st[:, 3:4], None, ALU.mult).then_inc(normed, 1)

            with dve.Fori(0, MEM_HEADS) as h:
                steps.round(h)
                for b in range(NB):
                    maxima(h, b)
                    normalise(h, b)
                assert steps.n == steps.per_round
                dve.wait_ge(out_hi, h + 1)
                dve.tensor_tensor(prog.XNL[:, bass.ds(2 * h, 2), 0:LAT], out, f32(prog.XNH[:, bass.ds(2 * h, 2), 0:LAT]),
                                  ALU.subtract).then_inc(out_free, 1)

        @block.scalar
        def _(act):
            def exponentials(h, b):
                st = stats[:, b % 2, :]
                act.wait_ge(bias_ready, NB * h + b + 1)
                act.wait_ge(turned, NB * h + b + 1)
                act.activation(probs[:, b % 2, :], PS[:, b % 2, 0:CTX], ACT.Exp, bias=st[:, 1:2], scale=scale,
                               accum_out=st[:, 2:3]).then_inc(exped, 1)

            def copy(h, b):
                act.wait_ge(turned, 2 + NB * h + b + 1)
                act.activation(probsT[:, b % 2, :], PS[:, 2, 0:CTX], ACT.Copy).then_inc(copied, 1)

            with act.Fori(0, MEM_HEADS) as h:
                act.wait_ge(v_turned, h + 1)
                act.activation(VS[:].rearrange("p a b -> p (a b)"), PS[:, 2, 0:2 * MEM_DIM], ACT.Copy).then_inc(v_kept, 1)
                exponentials(h, 0)
                exponentials(h, 1)
                for b in range(NB):
                    copy(h, b)
                    if b + 2 < NB:
                        exponentials(h, b + 2)
                act.wait_ge(attended, 1 + h + 1)
                act.activation(prog.XNH[:, bass.ds(2 * h, 2), 0:LAT], out, ACT.Copy).then_inc(out_hi, 1)


def memory_inputs(prog, gemms, before):
    reg = prog.region(prog.arena, prog.top)
    QM = prog.QM = reg.take("QM", [P, KD, LAT])
    KM = prog.KM = reg.take("KM", [P, KD, CTX])
    VM = prog.VM = reg.take("VM", [P, KD, CTX])
    prog.memory_at = reg.at_
    collect(prog, gemms["memq"], lambda u: LATENT, lambda u: QM[:, u, :], before=before)
    collect(prog, gemms["memk"], lambda u: CONTEXT, lambda u: KM[:, u, :])
    collect(prog, gemms["memv"], lambda u: CONTEXT, lambda u: VM[:, u, :])


MOE_UNITS = 12


class Moe:
    def __init__(self, prog):
        at = prog.small_end + 24576
        self.XS = prog.at("XS", [P, EXPERTS, KD, P], F32R, at)
        at += EXPERTS * KD * P * 4
        self.RAW = prog.at("RAWM", [P, RAWS, HALF_K * 512], F32, at)
        at += RAWS * HALF_K * 512 * 4
        self.WHI = prog.at("WHIM", [P, 2 * SPLITS, HALF_K * 256], F32R, at)
        self.S = prog.at("SLOTS", [P, LAT // P, EXPERTS * CAPACITY], F32R, at)
        at += SPLITS * HALF_K * 512 * 4
        self.WLO = prog.at("WLOM", [P, 2 * SPLITS, HALF_K * 256], F32R, at)
        at += SPLITS * HALF_K * 512 * 4
        self.scratch = at


def router(prog):
    moe = prog.moe = Moe(prog)
    with prog.block("router") as block:
        reg = prog.region(moe.scratch, prog.top)
        NT = LAT // P
        HTH = prog.HTH = reg.take("HTH", [P, NT, D], F32R)
        HTL = prog.HTL = reg.take("HTL", [P, NT, D], F32R)
        prog.SLOT_T = reg.take("SLOTT", [P, NT, EXPERTS])
        prog.IOTA = reg.take("IOTA", [P, CAPACITY])
        spare = prog.region(prog.small_end + 3 * 24576, prog.small_end + 3 * 24576 + 16384)
        R = spare.take("R", [P, KD, P])
        RH, RL = spare.take("RH", [P, KD, P], F32R), spare.take("RL", [P, KD, P], F32R)
        LT = spare.take("LT", [P, LAT])
        L, stats = reg.take("L", [P, NT, EXPERTS]), reg.take("STATS", [P, 2, NT])
        ROW, WORK = reg.take("ROW", [P, 2, LAT]), reg.take("WORK", [P, LAT])
        SEL, RANK, ZERO = reg.take("SEL", [P, LAT]), reg.take("RANK", [P, LAT]), reg.take("ZERO", [P, LAT])
        TOP = reg.take("TOP", [P, 8])
        loaded, r_hi, r_lo, logits, step = (prog.sem(n) for n in ("loaded", "r_hi", "r_lo", "logits", "step"))
        exped, probs, rows, rows_kept = (prog.sem(n) for n in ("exped", "probs", "rows", "rows_kept"))
        turned, hT_kept, slots, slot_turned, stored = (prog.sem(n) for n in ("turned", "ht", "slots", "sturned", "stored"))
        logitsT, logits_kept = prog.sem("logitsT"), prog.sem("logits_kept")
        PS, E = prog.PS, slice(0, EXPERTS)
        halves = [(x, t, h) for t in range(NT) for x in range(2) for h in range(2)]

        @block.sync
        def _(sp):
            sp.dma_start(R[:], prog.dram["router"]).then_inc(loaded, 16)
            sp.dma_start(prog.IOTA[:], prog.dram["iota"]).then_inc(loaded, 16)
            for j in range(RAWS):
                sp.dma_start(moe.RAW[:, j, :], prog.dram["experts"][j]).then_inc(prog.expert_landed[j], 16)
            sp.wait_ge(slots, 1)
            sp.dma_start(prog.dram["rows"], ROW[E, :, :]).then_inc(stored, 16)
            sp.wait_ge(stored, 16)

        @block.tensor
        def _(pe):
            pe.wait_ge(r_lo, 1)
            for k in range(KD):
                for n, (x, w) in enumerate(((prog.XNH, RH), (prog.XNH, RL), (prog.XNL, RH), (prog.XNL, RL))):
                    last = pe.matmul(PS[:, 1, 0:LAT], w[:, k, :], x[:, k, 0:LAT], start=(k == 0 and n == 0),
                                     stop=(k == KD - 1 and n == 3))
            last.then_inc(logitsT, 1)
            pe.wait_ge(logits_kept, 1)
            for t in range(NT):
                last = pe.transpose(PS[:, 0, t * EXPERTS:(t + 1) * EXPERTS], LT[E, t * P:(t + 1) * P], prog.IDENT[E, E])
            last.then_inc(logits, 1)
            pe.wait_ge(probs, 1)
            for t in range(NT):
                last = pe.transpose(PS[E, 1, t * P:(t + 1) * P], L[:, t, :], prog.IDENT[:])
            last.then_inc(rows, 1)
            for n, (x, t, h) in enumerate(halves):
                if n >= 4:
                    pe.wait_ge(hT_kept, n - 3)
                src = (prog.XNH, prog.XNL)[x]
                for k in range(4):
                    at = n % 2 * 512 + k * P
                    last = pe.transpose(PS[:, 2 + n // 2 % 2, at:at + P], f32(src[:, 4 * h + k, t * P:(t + 1) * P]),
                                        prog.IDENT[:])
                last.then_inc(turned, 1)
            pe.wait_ge(slots, 1)
            for t in range(NT):
                last = pe.transpose(PS[:, 0, t * EXPERTS:(t + 1) * EXPERTS], ROW[E, 0, t * P:(t + 1) * P],
                                    prog.IDENT[E, E])
            last.then_inc(slot_turned, 1)

        @block.scalar
        def _(act):
            act.wait_ge(loaded, 32)
            act.activation(RH[:], R[:], ACT.Copy).then_inc(r_hi, 1)
            act.wait_ge(logitsT, 1)
            act.activation(LT[E, :], PS[E, 1, 0:LAT], ACT.Copy).then_inc(logits_kept, 1)
            act.wait_ge(step, 2)
            act.activation(L[:], L[:], ACT.Exp).then_inc(exped, 1)
            act.wait_ge(rows, 1)
            act.activation(ROW[E, 1, :], PS[E, 1, 0:LAT], ACT.Copy).then_inc(rows_kept, 1)
            for n, (x, t, h) in enumerate(halves):
                act.wait_ge(turned, n + 1)
                act.activation((HTH, HTL)[x][:, t, h * 512:(h + 1) * 512], PS[:, 2 + n // 2 % 2, n % 2 * 512:n % 2 * 512 + 512],
                               ACT.Copy).then_inc(hT_kept, 1)
            act.wait_ge(slot_turned, 1)
            act.activation(prog.SLOT_T[:].rearrange("p a b -> p (a b)"), PS[:, 0, 0:NT * EXPERTS], ACT.Copy)

        @block.vector
        def _(dve):
            steps = Steps(dve, step)

            def then(instruction):
                steps.did(instruction)
                steps.wait()
            dve.memset(ZERO[E, :], 0.0)
            dve.wait_ge(r_hi, 1)
            dve.tensor_tensor(RL[:], R[:], f32(RH[:]), ALU.subtract).then_inc(r_lo, 1)
            dve.wait_ge(logits, 1)
            pl = PS[:, 0, 0:NT * EXPERTS].rearrange("p (t e) -> p t e", e=EXPERTS)
            wide = lambda s: s.unsqueeze(2).to_broadcast([P, NT, EXPERTS])
            then(dve.reduce_max(stats[:, 0, :], pl, AX.X))
            then(dve.tensor_tensor(L[:], pl, wide(stats[:, 0, :]), ALU.subtract))
            dve.wait_ge(exped, 1)
            then(dve.reduce_sum(stats[:, 0, :], L[:], AX.X))
            then(dve.reciprocal(stats[:, 1, :], stats[:, 0, :]))
            dve.tensor_tensor(L[:], L[:], wide(stats[:, 1, :]), ALU.mult).then_inc(probs, 1)
            dve.wait_ge(rows_kept, 1)
            then(dve.tensor_copy(WORK[E, :], ROW[E, 1, :]))
            for _ in range(CAPACITY // 8):
                then(dve.max(TOP[E, :], WORK[E, :]))
                then(dve.match_replace(WORK[E, :], TOP[E, :], WORK[E, :], -1.0))
            then(dve.tensor_scalar(SEL[E, :], WORK[E, :], 0.0, None, ALU.is_lt))
            then(dve.tensor_tensor_scan(RANK[E, :], SEL[E, :], ZERO[E, :], 0.0, ALU.add, ALU.add))
            dve.tensor_tensor(ROW[E, 0, :], RANK[E, :], SEL[E, :], ALU.mult).then_inc(slots, 1)


def gather(prog):
    moe = prog.moe
    with prog.block("gather") as block:
        NT = LAT // P
        hot, gathered = prog.sem("hot"), prog.sem("gathered")
        kept = [prog.sem("kept_by_act"), prog.sem("kept_by_dve")]
        work = [(k, x) for k in range(KD) for x in range(2)]

        @block.vector
        def _(dve):
            for t in range(NT):
                dve.tensor_tensor(moe.S[:, t, :].rearrange("p (e s) -> p e s", s=CAPACITY),
                                  prog.IOTA[:].unsqueeze(1).to_broadcast([P, EXPERTS, CAPACITY]),
                                  prog.SLOT_T[:, t, :].unsqueeze(2).to_broadcast([P, EXPERTS, CAPACITY]),
                                  ALU.is_equal).then_inc(hot, 1)
            for n, (k, x) in enumerate(work):
                if n % 2 == 1:
                    dve.wait_ge(gathered, n + 1)
                    dve.tensor_copy(moe.XS[:, :, k, x * 64:(x + 1) * 64],
                                    prog.PS[:, n % 4, :].rearrange("p (e s) -> p e s", s=CAPACITY)).then_inc(kept[1], 1)

        @block.scalar
        def _(act):
            for n, (k, x) in enumerate(work):
                if n % 2 == 0:
                    act.wait_ge(gathered, n + 1)
                    act.activation(moe.XS[:, :, k, x * 64:(x + 1) * 64],
                                   prog.PS[:, n % 4, :].rearrange("p (e s) -> p e s", s=CAPACITY), ACT.Copy).then_inc(kept[0], 1)

        @block.tensor
        def _(pe):
            for n, (k, x) in enumerate(work):
                if n >= 4:
                    pe.wait_ge(kept[n % 2], n // 2 - 1)
                src = (prog.HTH, prog.HTL)[x]
                for t in range(NT):
                    if n == 0:
                        pe.wait_ge(hot, t + 1)
                    for half in range(2):
                        last = pe.matmul(prog.PS[:, n % 4, half * 512:(half + 1) * 512], src[:, t, k * P:(k + 1) * P],
                                         moe.S[:, t, half * 512:(half + 1) * 512], start=(t == 0), stop=(t == NT - 1))
                last.then_inc(gathered, 1)


def experts(prog):
    moe = prog.moe
    with prog.block("moe") as block:
        reg = prog.region(moe.scratch, prog.top)
        ROWS = reg.take("ROWS", [P, 2, LAT])
        XU, XG = reg.take("XU", [P, KD, P], F32R), reg.take("XG", [P, KD, P], F32R)
        HT = reg.take("HT", [P, KD, P], F32R)
        HS = reg.take("HS", [P, KD, CAPACITY])
        SIL = reg.take("SIL", [P, KD, CAPACITY])
        A, B = reg.take("A", [P, D]), reg.take("B", [P, D])
        YH, YL = reg.take("YH", [P, D], F32R), reg.take("YL", [P, D], F32R)
        ST = reg.take("ST", [P, LAT], F32R)
        prod = reg.take("PROD", [P, LAT])
        gate = reg.take("GATE", [P, 2])
        SUM2 = reg.take("SUM2", [P, P])
        RAW, WHI, WLO, XS, PS, X = moe.RAW, moe.WHI, moe.WLO, moe.XS, prog.PS, prog.X
        w_hi, w_lo, done = prog.sem("w_hi"), prog.sem("w_lo"), prog.sem("done")
        u_staged, g_staged = prog.sem("u_staged"), prog.sem("g_staged")
        rows_landed, hot, gated = prog.sem("rows_landed"), prog.sem("hot"), prog.sem("gated")
        a_kept, b_kept, a_turned, b_turned = (prog.sem(n) for n in ("a_kept", "b_kept", "a_turned", "b_turned"))
        silu, hidden, h_hi, h_lo, y_hi, y_lo = (prog.sem(n) for n in ("silu", "hidden", "h_hi", "h_lo", "y_hi", "y_lo"))
        scattered, added, consts, zeroed = prog.sem("scattered"), prog.sem("added"), prog.sem("consts"), prog.sem("zeroed")
        PART = 8
        ROUND, last_e = 3 * PART, EXPERTS - 1
        RING = 2 * SPLITS
        A_SLOT, B_SLOT, A_TURNED, B_TURNED, Y_SLOT = 0, 1, 2, 3, 3
        QUARTERS = (1, 2, 1, 2)

        def rounds(eng, body):
            with eng.Fori(0, last_e) as e:
                body(e, PART + ROUND * e, ROUND)
            body(last_e, PART + ROUND * last_e, 2 * PART)

        TURN_A, TURN_B = (0, 2, 4, 6), (8, 9, 10, 11)

        def scatter_at(n):
            return (14, 16, 18, 20) if n == ROUND else (8, 9, 10, 11)

        def over(e, h):
            return isinstance(e, int) and e == last_e and h >= 2 * PART

        @block.sync
        def _(sp):
            sp.dma_start(SUM2[:], prog.dram["sum2"]).then_inc(consts, 16)

            def load(unit, j):
                sp.wait_ge(w_lo, 2 * unit + 2 * j + 2)
                sp.dma_start(RAW[:, j % RAWS, :], prog.dram["experts"][unit + j + RAWS]).then_inc(prog.expert_landed[j % RAWS], 16)
            for j in range(PART // 2):
                load(0, j)

            def body(e, start, n):
                for j in range(n // 2):
                    if over(e, 2 * (j + RAWS)):
                        continue
                    load(PART // 2 + ROUND // 2 * e, j)
            rounds(sp, body)

        @block.gpsimd
        def _(pool):
            def load_rows(e):
                pool.dma_start(ROWS[:], prog.dram["rows"][e].partition_broadcast(P)).then_inc(rows_landed, 16)
            pool.tensor_copy(XG[:], XS[:, 0, :, :]).then_inc(g_staged, 1)
            pool.tensor_copy(XU[:], XS[:, 0, :, :]).then_inc(u_staged, 1)
            load_rows(0)
            pool.wait_ge(done, PART)
            pool.tensor_copy(XG[:], XS[:, 1, :, :]).then_inc(g_staged, 1)
            with pool.Fori(0, EXPERTS - 2) as e:
                pool.wait_ge(done, ROUND * e + 2 * PART)
                pool.tensor_copy(XU[:], XS[:, e + 1, :, :]).then_inc(u_staged, 1)
                pool.wait_ge(done, ROUND * e + 3 * PART)
                pool.wait_ge(gated, e + 1)
                pool.tensor_copy(XG[:], XS[:, e + 2, :, :]).then_inc(g_staged, 1)
                load_rows(e + 1)
            pool.wait_ge(done, ROUND * (EXPERTS - 2) + 2 * PART)
            pool.tensor_copy(XU[:], XS[:, EXPERTS - 1, :, :]).then_inc(u_staged, 1)
            pool.wait_ge(gated, EXPERTS - 1)
            load_rows(EXPERTS - 1)

        @block.tensor
        def _(pe):
            def half_unit(start, h, x, slot):
                part = h % PART
                out_half, k0 = part // 4, 2 * (part % 4)
                pe.wait_ge(w_lo, start + h + 1)
                for k in range(2):
                    for n, w in enumerate((WHI, WLO)):
                        last = pe.matmul(PS[:, slot, out_half * 512:(out_half + 1) * 512], x[:, k0 + k, :],
                                         w[:, h % RING, k * 512:(k + 1) * 512], start=(k0 + k == 0 and n == 0),
                                         stop=(k0 + k == KD - 1 and n == 1))
                last.then_inc(done, 1)

            def turn(x, slot, ready, quarter):
                for k in (2 * quarter, 2 * quarter + 1):
                    last = pe.matmul(PS[:, slot, k * P:(k + 1) * P], x[:, k * P:(k + 1) * P], SUM2[:], start=True, stop=True)
                last.then_inc(ready, 1)

            def turn_b(e, quarter):
                if quarter == 0:
                    pe.wait_ge(b_kept, e + 1)
                    pe.wait_ge(y_lo, e + 1)
                turn(B, B_TURNED, b_turned, quarter)

            def scatter(e, quarter):
                if quarter == 0:
                    pe.wait_ge(hot, e + 1)
                    pe.wait_ge(y_lo, e + 1)
                if quarter >= 2:
                    pe.wait_ge(added, 4 * e + quarter)
                for k in range(2):
                    for n, y in enumerate((YH, YL)):
                        last = pe.matmul(PS[:, QUARTERS[quarter], k * 512:(k + 1) * 512],
                                         y[:, (2 * quarter + k) * P:(2 * quarter + k + 1) * P], ST[:], start=(n == 0), stop=(n == 1))
                last.then_inc(scattered, 1)

            def body(e, start, n):
                pe.wait_ge(u_staged, e + 1)
                pe.wait_ge(added, 4 * e + 1)
                for h in range(n):
                    if n == ROUND and h == PART:
                        pe.wait_ge(g_staged, e + 2)
                    if h == n - PART:
                        pe.wait_ge(h_lo, e + 1)
                    if h < PART:
                        half_unit(start, h, XU, B_SLOT)
                    elif h < n - PART:
                        half_unit(start, h, XG, A_SLOT)
                    else:
                        half_unit(start, h, HT, Y_SLOT)
                    if h in TURN_A:
                        if h == 0:
                            pe.wait_ge(a_kept, e + 1)
                        turn(A, A_TURNED, a_turned, TURN_A.index(h))
                    if n == ROUND and h in TURN_B:
                        turn_b(e, TURN_B.index(h))
                    if n != ROUND and h == PART - 1:
                        for quarter in range(4):
                            turn_b(e, quarter)
                    if h in scatter_at(n):
                        pe.wait_ge(silu, e + 1)
                        scatter(e, scatter_at(n).index(h))
            pe.wait_ge(consts, 16)
            pe.wait_ge(zeroed, 3)
            pe.nop().then_inc(added, 1)
            pe.wait_ge(g_staged, 1)
            for h in range(PART):
                half_unit(0, h, XG, A_SLOT)
            rounds(pe, body)
            pe.wait_ge(added, 4 * EXPERTS + 1)
            for quarter in range(4):
                scatter(EXPERTS, quarter)

        @block.scalar
        def _(act):
            def split(units_before, start, h):
                j = h // 2
                act.wait_ge(prog.expert_landed[j % RAWS], 16 * (units_before + j // RAWS) + 16)
                if not (isinstance(start, int) and start == 0 and h < RING):
                    act.wait_ge(done, start + h - RING + 1)
                act.activation(WHI[:, h % RING, :], RAW[:, j % RAWS, h % 2 * 1024:h % 2 * 1024 + 1024], ACT.Copy).then_inc(w_hi, 1)

            def body(e, start, n):
                full = n == ROUND
                for h in range(n):
                    if not over(e, h + RING):
                        split(1 + 3 * e, start, h + RING)
                    if h == 7:
                        act.wait_ge(done, start + PART)
                        act.activation(B[:], PS[:, B_SLOT, :], ACT.Copy).then_inc(b_kept, 1)
                        act.wait_ge(a_turned, 4 * e + 4)
                        act.activation(SIL[:], PS[:, A_TURNED, :].rearrange("p (k s) -> p k s", s=P)[:, :, 0:CAPACITY],
                                       ACT.Silu).then_inc(silu, 1)
                    if h == (12 if full else 7):
                        act.wait_ge(hidden, e + 1)
                        act.activation(HT[:, :, 0:CAPACITY], HS[:], ACT.Copy).then_inc(h_hi, 1)
                    if full and h == 15:
                        act.wait_ge(done, start + 2 * PART)
                        act.activation(A[:], PS[:, A_SLOT, :], ACT.Copy).then_inc(a_kept, 1)
                act.wait_ge(done, start + n)
                act.wait_ge(gated, e + 1)
                act.activation(YH[:], PS[:, Y_SLOT, :], ACT.Copy, scale=gate[:, 0:1]).then_inc(y_hi, 1)
            act.wait_ge(zeroed, 1)
            for y in (YH, YL):
                act.activation(y[:].rearrange("p (a b) -> p a b", a=2), prod[:].unsqueeze(1).to_broadcast([P, 2, LAT]),
                               ACT.Copy).then_inc(zeroed, 1)
            for h in range(RING):
                split(0, 0, h)
            for h in range(PART):
                split(0, 0, h + RING)
            act.wait_ge(done, PART)
            act.activation(A[:], PS[:, A_SLOT, :], ACT.Copy).then_inc(a_kept, 1)
            prog.use_table_of(act, ACT.Silu)
            rounds(act, body)

        @block.vector
        def _(dve):
            def split(start, h):
                j = h // 2
                dve.wait_ge(w_hi, start + h + 1)
                if not (isinstance(start, int) and start == 0 and h < RING):
                    dve.wait_ge(done, start + h - RING + 1)
                dve.tensor_tensor(WLO[:, h % RING, :], RAW[:, j % RAWS, h % 2 * 1024:h % 2 * 1024 + 1024],
                                  f32(WHI[:, h % RING, :]), ALU.subtract).then_inc(w_lo, 1)

            def add(e, quarter):
                dve.wait_ge(scattered, 4 * e + quarter + 1)
                dve.tensor_tensor(X[:, 2 * quarter:2 * quarter + 2, 0:LAT],
                                  PS[:, QUARTERS[quarter], :].rearrange("p (k t) -> p k t", k=2),
                                  X[:, 2 * quarter:2 * quarter + 2, 0:LAT], ALU.add).then_inc(added, 1)

            def body(e, start, n):
                full = n == ROUND
                for h in range(n):
                    if not over(e, h + RING):
                        split(start, h + RING)
                    if h - 1 in scatter_at(n):
                        add(e, scatter_at(n).index(h - 1))
                    if h == (11 if full else 7):
                        dve.wait_ge(b_turned, 4 * e + 4)
                        dve.wait_ge(silu, e + 1)
                        dve.tensor_tensor(HS[:], PS[:, B_TURNED, :].rearrange("p (k s) -> p k s", s=P)[:, :, 0:CAPACITY],
                                          SIL[:], ALU.mult).then_inc(hidden, 1)
                    if h == (12 if full else 7):
                        dve.wait_ge(h_hi, e + 1)
                        dve.tensor_tensor(HT[:, :, CAPACITY:P], HS[:], f32(HT[:, :, 0:CAPACITY]), ALU.subtract).then_inc(h_lo, 1)
                    if h == min(scatter_at(n)[3] + 2, n - 1):
                        dve.wait_ge(rows_landed, 16 * e + 16)
                        dve.tensor_scalar(ST[:], ROWS[:, 0, :], prog.prm("slot"), None, ALU.is_equal).then_inc(hot, 1)
                        dve.wait_ge(hot, e + 2)
                        dve.tensor_tensor_reduce(prod[:], f32(ST[:]), ROWS[:, 1, :], 1.0, 0.0, ALU.mult, ALU.add,
                                                 gate[:, 0:1]).then_inc(gated, 1)
                dve.wait_ge(y_hi, e + 1)
                dve.scalar_tensor_tensor(YL[:], PS[:, Y_SLOT, :], gate[:, 0:1], f32(YH[:]), ALU.mult, ALU.subtract).then_inc(y_lo, 1)
            dve.memset(prod[:], 0.0).then_inc(zeroed, 1)
            dve.wait_ge(zeroed, 3)
            dve.tensor_copy(ST[:], prod[:]).then_inc(hot, 1)
            dve.nop().then_inc(y_lo, 1)
            for h in range(RING):
                split(0, h)
            for h in range(PART):
                split(0, h + RING)
            rounds(dve, body)
            for quarter in range(4):
                add(EXPERTS, quarter)



def build(nc, dram, out):
    prog = Program(nc, dram)
    gemms = {n: Gemm(n, dram[n], k) for n, k in GEMMS}
    order = list(gemms.values())
    for a, b in zip(order, order[1:]):
        b.base, a.next = a.base + a.n, b

    def mod(layer, section):
        m = prog.MOD[layer]
        return lambda u, t: m[:, bass.ds(8 * section + u, 1), t]

    def shift(layer, section):
        return prog.MOD[layer][:, 8 * section:8 * section + 8, :]

    stages = []
    add = lambda name, f: stages.append((name, f))
    add("start", lambda: start(prog))
    add("ada", lambda: condition(prog, order[0]))
    normed = lambda *a: lambda: Norm(prog, *a)
    add("pw1", lambda: gated_convolution(prog, gemms["pw1"], normed(prog.GAIN[0][0], shift(0, 0), BOTH)))
    add("pw2", lambda: project(prog, gemms["pw2"], prog.XNH, prog.XNL, BOTH, mod(0, 2),
                               lambda u, t: prog.G1B[:, bass.ds(u, 1), t],
                               before=lambda: LayerNormSilu(prog)))
    for grp in range(2):
        add(f"up0{grp}", lambda grp=grp: ffn_up(prog, gemms[f"up0{grp}"], 0, grp, BOTH,
                                                  None if grp else normed(prog.GAIN[0][1], shift(0, 3), BOTH)))
        add(f"down0{grp}", lambda grp=grp: project(prog, gemms[f"down0{grp}"], prog.HH, prog.HL, BOTH, mod(0, 5)))
    add("qkv", lambda: window_qkv(prog, gemms["qkv"], normed(prog.GAIN[1][0], shift(1, 0), BOTH)))
    add("rope", lambda: window_rope(prog))
    add("attn", lambda: window_attention(prog))
    add("wo", lambda: project(prog, gemms["wo"], prog.XNH, prog.XNL, LATENT, mod(1, 2)))
    for grp in range(2):
        add(f"up1{grp}", lambda grp=grp: ffn_up(prog, gemms[f"up1{grp}"], 1, grp, LATENT,
                                                  None if grp else normed(prog.GAIN[1][1], shift(1, 3), LATENT)))
        add(f"down1{grp}", lambda grp=grp: project(prog, gemms[f"down1{grp}"], prog.HH, prog.HL, LATENT, mod(1, 5)))
    add("final_1", lambda: rescale(prog, prog.prm("final_1", 0, 8)))
    add("w_in", lambda: mixing_input(prog, gemms["w_in"], normed(prog.prm3("g_mix", 2), None, LATENT)))
    add("fourier", lambda: fourier(prog))
    add("latents", lambda: latents(prog))
    add("mla", lambda: latent_attention(prog))
    add("w_out", lambda: project(prog, gemms["w_out"], prog.XNH, prog.XNL, LATENT))
    add("mem_in", lambda: memory_inputs(prog, gemms, normed(prog.prm3("g_mem", 2), None, BOTH)))
    add("mem_attn", lambda: memory_attention(prog))
    add("mem_o", lambda: project(prog, gemms["mem_o"], prog.XNH, prog.XNL, LATENT))
    add("norm_moe", lambda: norm(prog, prog.prm3("g_ffn", 2), None, LATENT))
    add("router", lambda: router(prog))
    add("gather", lambda: gather(prog))
    add("moe", lambda: experts(prog))
    add("end", lambda: rescale(prog, prog.prm("final_2", 0, 8), out))
    for _, stage in stages:
        stage()


SCRATCH = {"rows": (EXPERTS, 2, LAT)}

GEMMS = [("pw1", 8), ("pw2", 8), ("up00", 8), ("down00", HID), ("up01", 8), ("down01", HID), ("qkv", 8), ("wo", 8),
         ("up10", 8), ("down10", HID), ("up11", 8), ("down11", HID), ("w_in", 8), ("w_out", 8), ("memq", 8), ("memk", 8), ("memv", 8),
         ("mem_o", 8)]



def units(w):
    k, m = w.shape
    return np.ascontiguousarray(w.reshape(k // P, P, m // P, P).transpose(2, 1, 0, 3).reshape(m // P, P, k))


def columns(v):
    return v.reshape(-1, P).T


def both(a, b):
    return np.stack([a, b], axis=-1).reshape(P, -1)


def pairs(w):
    k, m = w.shape
    return w.reshape(k, 2, m // 2 // P, P).transpose(0, 2, 1, 3).reshape(k, m)


def features(x):
    return x.T.reshape(-1, P, x.shape[0]).transpose(1, 0, 2)


def axial_tables():
    t = np.arange(LAT)
    n = HEAD_DIM // 4
    inv = np.float32(10000.0) ** (-np.arange(n, dtype=np.float32) / np.float32(n))
    row, col = (t // 64).astype(np.float32), (t % 64).astype(np.float32)
    ang = np.concatenate([row[:, None] * inv, col[:, None] * inv], axis=-1).T
    return np.stack([np.tile(np.cos(ang), (4, 1)), np.tile(np.sin(ang), (4, 1))], axis=1).astype(np.float32)


def rotation(size, at, half):
    r = np.zeros((size, size), np.float32)
    for m in range(at, size):
        if (m - at) % (2 * half) < half:
            r[m + half, m] = -1.0
        else:
            r[m - half, m] = 1.0
    return r


def window_order():
    group = HEADS // KV_HEADS
    return [group * (2 * p + half) + j for p in range(2) for j in range(group) for half in range(2)]


def layouts(x, c, ctx, c_ctx, ada_w, ada_b, norm1_g, norm2_g, final_g, conv_w_pw1, conv_b_pw1, conv_w_dw, conv_b_dw,
            conv_ln_g, conv_ln_b, conv_w_pw2, conv_b_pw2, attn_w_qkv, attn_w_o, attn_sink, ffn_w_up, ffn_w_dw, ffn_b_dw,
            ffn_w_down, mem_2, positions_2, g_mix_2, w_in_2, g_q_lat_2, w_q_up_2, g_kv_lat_2, w_kv_up_2, w_fourier_2,
            w_out_2, g_mem_q_2, g_mem_kv_2, w_mem_q_2, w_mem_kv_2, w_mem_o_2, g_ffn_2, w_router_2, w_exp_gate_2,
            w_exp_up_2, w_exp_down_2, g_final_2):
    a = {}
    a["xT"] = np.concatenate([features(x[0]), features(ctx[0])], axis=2)
    a["ada"] = ada_w.reshape(2, 2, HALF_K, P, ADA_SLICES, 512).transpose(0, 4, 1, 3, 2, 5).reshape(-1, P, HALF_K * 512)
    a["pw1"] = units(pairs(conv_w_pw1[0]))
    a["pw2"] = units(conv_w_pw2[0])
    for l in range(2):
        up = pairs(ffn_w_up[l])
        for grp in range(2):
            a[f"up{l}{grp}"] = units(up[:, grp * 2 * HID * P:(grp + 1) * 2 * HID * P])
            a[f"down{l}{grp}"] = units(ffn_w_down[l][grp * HID * P:(grp + 1) * HID * P])
    heads = window_order()
    q = attn_w_qkv[0][:, :D].reshape(D, HEADS, HEAD_DIM)[:, heads].reshape(D, D)
    a["qkv"] = np.concatenate([units(q), units(attn_w_qkv[0][:, D:])])
    a["wo"] = units(attn_w_o[0].reshape(HEADS, HEAD_DIM, D)[heads].reshape(D, D))
    a["memT"] = features(mem_2[0])
    a["ident"] = np.eye(P, dtype=np.float32)
    a["axial"] = axial_tables()
    a["rot_head"] = rotation(P, 0, HEAD_DIM // 2)
    r, j = np.mgrid[0:BLOCK, 0:BLOCK]
    a["masks"] = np.stack([np.where(j >= r, 0, NEG), np.where(j <= r, 0, NEG)], axis=1).astype(np.float32)
    prm = {}
    prm["sink"] = np.tile(attn_sink[0][heads], (P, 1))
    prm["final_1"] = columns(final_g)
    for l in range(2):
        prm[f"norm1_{l}"] = both(columns(norm1_g[l]), columns(norm1_g[l]))
        prm[f"norm2_{l}"] = both(columns(norm2_g[l]), columns(norm2_g[l]))
        prm[f"ada_b{l}"] = both(columns(ada_b[l]), columns(ada_b[l]))
        taps = np.stack([columns(pairs(v[None])[0]) for v in (*ffn_w_dw[l], ffn_b_dw[l])], axis=-1)
        prm[f"ffn{l}"] = taps.reshape(P, -1)
    prm["b_pw1"] = columns(pairs(conv_b_pw1)[0])
    prm["w_dw"] = np.stack([columns(v) for v in conv_w_dw[0]], axis=-1).reshape(P, -1)
    prm["b_dw"], prm["ln_g"], prm["ln_b"], prm["b_pw2"] = map(columns, (conv_b_dw[0], conv_ln_g[0], conv_ln_b[0], conv_b_pw2[0]))
    w_in = np.zeros((D, 10 * P), np.float32)
    w_in[:, 0:9 * P] = w_in_2[0][:, 0:9 * P]
    w_in[:, 9 * P + NOPE:9 * P + QK] = w_in_2[0][:, 9 * P:]
    a["w_in"] = units(w_in)
    a["w_out"], a["memq"], a["mem_o"] = units(w_out_2[0]), units(w_mem_q_2[0]), units(w_mem_o_2[0])
    a["memk"], a["memv"] = units(w_mem_kv_2[0][:, :D]), units(w_mem_kv_2[0][:, D:])
    n = np.arange(LAT)
    turn = np.outer(n, n) % LAT * (2 * np.pi / LAT)
    dft = np.stack([np.cos(turn), -np.sin(turn)], axis=1) / np.sqrt(LAT)
    a["dft"] = dft.reshape(LAT // P, P, 2, LAT).transpose(1, 0, 2, 3).astype(np.float32)
    turn = np.outer(n[:64], n[:64]) % 64 * (2 * np.pi / 64)
    a["group_dft"] = np.stack([np.kron(np.eye(2), np.cos(turn)), np.kron(np.eye(2), np.sin(turn))], axis=1).astype(np.float32) / 8
    a["w_fourier"] = np.zeros((P, 4, P), np.float32)
    for grp in range(8):
        h = grp % 2 * 64
        a["w_fourier"][h:h + 64, grp // 2, h:h + 64] = w_fourier_2[0][grp]
    a["rot_rope"] = rotation(QK, NOPE, ROPE // 2)
    a["positions"] = np.tile(positions_2, (QK, 1))
    wq = w_q_up_2[0].reshape(Q_RANK // P, P, MLA_HEADS // 2, 2 * QK)
    wkv = w_kv_up_2[0].reshape(KV_RANK // P, P, MLA_HEADS // 2, 2, NOPE + V_DIM)
    wk = np.zeros(wkv.shape[:4] + (QK,), np.float32)
    wk[..., :NOPE] = wkv[..., :NOPE]
    a["mla"] = np.concatenate([w.transpose(2, 1, 0, *range(3, w.ndim)).reshape(MLA_HEADS // 2, P, -1)
                               for w in (wq, wk, wkv[..., NOPE:])], axis=2)
    a["router"] = np.zeros((P, KD, P), np.float32)
    a["router"][:, :, :EXPERTS] = w_router_2[0].reshape(KD, P, EXPERTS).transpose(1, 0, 2)
    a["iota"] = np.tile(np.arange(1, CAPACITY + 1, dtype=np.float32), (P, 1))
    a["sum2"] = np.tile(np.eye(CAPACITY, dtype=np.float32), (2, 2))
    w = np.stack([w_exp_gate_2[0], w_exp_up_2[0], w_exp_down_2[0]], axis=1)
    w = w.reshape(EXPERTS, 3, 2, HALF_K, P, 2, 512).transpose(0, 1, 5, 2, 4, 3, 6).reshape(EXPERTS, 3, 4, P, HALF_K * 512)
    order = [(0, 0)]
    for e in range(EXPERTS):
        order += [(e, 1), (e + 1, 0), (e, 2)] if e + 1 < EXPERTS else [(e, 1), (e, 2)]
    a["experts"] = np.concatenate([w[e, part] for e, part in order])
    for name, v, w in (("g_mix", g_mix_2, g_mix_2), ("g_mem", g_mem_q_2, g_mem_kv_2), ("g_ffn", g_ffn_2, g_ffn_2)):
        prm[name] = both(columns(v[0]), columns(w[0]))
    prm["g_q"], prm["g_kv"], prm["final_2"] = columns(g_q_lat_2[0]), columns(g_kv_lat_2[0]), columns(g_final_2)
    freq = np.float32(1) / np.float32(10000.0) ** (np.arange(0, ROPE, 2, dtype=np.float32) / np.float32(ROPE))
    prm["freq"] = np.concatenate([np.zeros(NOPE), freq, freq, np.zeros(P - QK)])[:, None]
    prm["slot"] = (np.arange(P) % CAPACITY + 1.0)[:, None]
    prm["cond"] = both(columns(c[0]), columns(c_ctx))
    table = np.zeros((P, N_PARAMS), np.float32)
    for name, v in prm.items():
        at, n = PARAMS[name]
        table[:, at:at + n] = v
    a["params"] = table
    return {k: np.ascontiguousarray(v) for k, v in a.items()}


def kernel(**inputs):
    import concourse.bacc as _bacc
    from concourse.bass_utils import run_bass_kernel_spmd as _run

    nc = _bacc.Bacc("TRN2", target_bir_lowering=False, num_devices=1)
    arrays = layouts(**{name: np.asarray(v) for name, v in inputs.items()})
    dram = {n: nc.dram_tensor(n, a.shape, mybir.dt.from_np(a.dtype), kind="ExternalInput").ap() for n, a in arrays.items()}
    for n, shape in SCRATCH.items():
        dram[n] = nc.dram_tensor(n, shape, F32, kind="Internal").ap()
    out = nc.dram_tensor("out", (P, KD, LAT), F32, kind="ExternalOutput").ap()
    build(nc, dram, out)
    r = _run(nc, [arrays], core_ids=[0]).results[0]["out"]
    return np.ascontiguousarray(r.transpose(2, 1, 0).reshape(1, LAT, D))
```
